# Optimizing a Trainium2 kernel written in Bass

```python
import math
import jax, jax.numpy as jnp
from jax import lax
import numpy as np

D_MODEL = 1024
BATCH = 1
SEQ = 512
DEPTH = 1
DEC_BATCH = 8
DEC_SEQ = 1
PAST_LEN = 4096
PAGE_SIZE = 128

FOX_HEADS = 8
FOX_HEAD_DIM = 64
FOX_WIDTH = FOX_HEADS * FOX_HEAD_DIM
Q_BLOCK = 128
FORGET_BIAS_INIT = 3.0
GDN_HEADS = 4
GDN_HEAD_DIM = 128
GDN_WIDTH = GDN_HEADS * GDN_HEAD_DIM
CONV_WIDTH = 4
CONV_CH = 3 * GDN_WIDTH
CHUNK = 64
D_FF = 2816
EPS = 1e-6
SPLIT_SIZES = (FOX_WIDTH, FOX_WIDTH, FOX_WIDTH, FOX_HEADS, CONV_CH, GDN_HEADS, GDN_HEADS, GDN_WIDTH, D_MODEL, D_MODEL)
P_IN = 3 * FOX_WIDTH + FOX_HEADS + CONV_CH + 2 * GDN_HEADS + GDN_WIDTH + 2 * D_MODEL

kernel_name = "fox_gdn_parallel_macaron_step"

def rmsnorm(x, g):
    xf = x.astype(jnp.float32)
    y = xf * lax.rsqrt(jnp.mean(xf * xf, axis=-1, keepdims=True) + EPS)
    return (y * g.astype(jnp.float32)).astype(x.dtype)

def l2norm(x):
    xf = x.astype(jnp.float32)
    return xf * lax.rsqrt(jnp.sum(xf * xf, axis=-1, keepdims=True) + EPS)

def swiglu_half(x, g_pre, w_gate, w_up, w_down, g_post):
    h = rmsnorm(x, g_pre)
    y = (jax.nn.silu(h @ w_gate) * (h @ w_up)) @ w_down
    return x + 0.5 * rmsnorm(y, g_post)

def causal_conv(u, buf, w):
    T = u.shape[1]
    full = jnp.concatenate([buf.astype(u.dtype), u], axis=1)
    out = full[:, 0:T] * w[0]
    for i in range(1, CONV_WIDTH):
        out = out + full[:, i:i + T] * w[i]
    return jax.nn.silu(out), full[:, T:]

def mixer_inputs(h, conv_buf, w_in, b_f, conv_w, dt_bias, a_log):
    B, T, _ = h.shape
    p = h @ w_in
    idx = np.cumsum(SPLIT_SIZES)[:-1].tolist()
    qa, ka, va, fa, qkv_g, a_g, b_g, z, gate_a, gate_b = jnp.split(p, idx, axis=-1)
    qa = qa.reshape(B, T, FOX_HEADS, FOX_HEAD_DIM)
    ka = ka.reshape(B, T, FOX_HEADS, FOX_HEAD_DIM)
    va = va.reshape(B, T, FOX_HEADS, FOX_HEAD_DIM)
    logf = jax.nn.log_sigmoid(fa.astype(jnp.float32) + b_f.astype(jnp.float32))
    conv_out, new_buf = causal_conv(qkv_g, conv_buf, conv_w)
    qg, kg, vg = jnp.split(conv_out, 3, axis=-1)
    qg = l2norm(qg.reshape(B, T, GDN_HEADS, GDN_HEAD_DIM))
    kg = l2norm(kg.reshape(B, T, GDN_HEADS, GDN_HEAD_DIM))
    vg = vg.reshape(B, T, GDN_HEADS, GDN_HEAD_DIM).astype(jnp.float32)
    g = -jnp.exp(a_log.astype(jnp.float32)) * jax.nn.softplus(a_g.astype(jnp.float32) + dt_bias.astype(jnp.float32))
    beta = jax.nn.sigmoid(b_g.astype(jnp.float32))
    return qa, ka, va, logf, qg, kg, vg, g, beta, z, gate_a, gate_b, new_buf

def fox_block(q, cq, pos_q, k, v, ck, pos_k):
    s = jnp.einsum('bqhd,bkhd->bhqk', q, k).astype(jnp.float32) * (FOX_HEAD_DIM ** -0.5)
    s = s + jnp.swapaxes(cq, 1, 2)[..., :, None] - jnp.swapaxes(ck, 1, 2)[..., None, :]
    s = jnp.where(pos_k[None, :] <= pos_q[:, None], s, -jnp.inf)
    p = jax.nn.softmax(s, axis=-1)
    return jnp.einsum('bhqk,bkhd->bqhd', p.astype(v.dtype), v)

def fox_prompt(q, k, v, logf):
    B, S = q.shape[:2]
    c = jnp.cumsum(logf, axis=1)
    nb = S // Q_BLOCK
    qb = jnp.swapaxes(q.reshape(B, nb, Q_BLOCK, FOX_HEADS, FOX_HEAD_DIM), 0, 1)
    cb = jnp.swapaxes(c.reshape(B, nb, Q_BLOCK, FOX_HEADS), 0, 1)
    pos = jnp.arange(S)

    def one_block(args):
        i, q_i, c_i = args
        return fox_block(q_i, c_i, i * Q_BLOCK + jnp.arange(Q_BLOCK), k, v, c, pos)

    o = lax.map(one_block, (jnp.arange(nb), qb, cb))
    return jnp.swapaxes(o, 0, 1).reshape(B, S, FOX_HEADS, FOX_HEAD_DIM)

def fox_sample(q, k, v, logf, cache_k, cache_v, cache_logf, page_table):
    DB, T = q.shape[:2]
    past_k = cache_k[page_table].reshape(DB, -1, FOX_HEADS, FOX_HEAD_DIM)
    past_v = cache_v[page_table].reshape(DB, -1, FOX_HEADS, FOX_HEAD_DIM)
    past_lf = cache_logf[page_table].reshape(DB, -1, FOX_HEADS).astype(jnp.float32)
    P = past_k.shape[1]
    k_all = jnp.concatenate([past_k.astype(k.dtype), k], axis=1)
    v_all = jnp.concatenate([past_v.astype(v.dtype), v], axis=1)
    c = jnp.cumsum(jnp.concatenate([past_lf, logf], axis=1), axis=1)
    return fox_block(q, c[:, P:], P + jnp.arange(T), k_all, v_all, c, jnp.arange(P + T))

def gdn_chunked(q, k, v, g, beta, S0):
    B, T, H, dk = q.shape
    dv = v.shape[-1]
    n = T // CHUNK

    def to_chunks(a):
        a = jnp.moveaxis(a.astype(jnp.float32), 2, 1)
        return a.reshape((B, H, n, CHUNK) + a.shape[3:])

    qc = to_chunks(q) * (dk ** -0.5)
    kc, vc, bc = to_chunks(k), to_chunks(v), to_chunks(beta)
    gc = jnp.cumsum(to_chunks(g), axis=-1)
    tri = jnp.tril(jnp.ones((CHUNK, CHUNK), bool))
    diff = gc[..., :, None] - gc[..., None, :]
    decay = jnp.where(tri, jnp.exp(jnp.where(tri, diff, 0.0)), 0.0)
    kb = kc * bc[..., None]
    lower = jnp.einsum('bhncd,bhnsd->bhncs', kb, kc) * decay
    rhs = jnp.concatenate([vc * bc[..., None], kb * jnp.exp(gc)[..., None]], axis=-1)
    sol = lax.linalg.triangular_solve(lower, rhs, left_side=True, lower=True, unit_diagonal=True)
    u, w = sol[..., :dv], sol[..., dv:]
    attn = jnp.einsum('bhncd,bhnsd->bhncs', qc, kc) * decay

    def step(S, xs):
        q_i, k_i, u_i, w_i, g_i, a_i = xs
        v_new = u_i - jnp.einsum('bhcd,bhde->bhce', w_i, S)
        o = jnp.einsum('bhcd,bhde->bhce', q_i * jnp.exp(g_i)[..., None], S) + jnp.einsum('bhcs,bhse->bhce', a_i, v_new)
        g_last = g_i[..., -1]
        S = S * jnp.exp(g_last)[..., None, None] + jnp.einsum('bhcd,bhce->bhde', k_i * jnp.exp(g_last[..., None] - g_i)[..., None], v_new)
        return S, o

    xs = tuple(jnp.moveaxis(a, 2, 0) for a in (qc, kc, u, w, gc, attn))
    S, o = lax.scan(step, S0.astype(jnp.float32), xs)
    return jnp.transpose(o, (1, 0, 3, 2, 4)).reshape(B, T, H, dv), S

def gdn_recurrent(q, k, v, g, beta, S0):
    xs = tuple(jnp.moveaxis(a.astype(jnp.float32), 1, 0) for a in (q * (GDN_HEAD_DIM ** -0.5), k, v, g, beta))

    def step(S, xs_t):
        q_t, k_t, v_t, g_t, b_t = xs_t
        S = S * jnp.exp(g_t)[..., None, None]
        delta = (v_t - jnp.einsum('bhd,bhde->bhe', k_t, S)) * b_t[..., None]
        S = S + jnp.einsum('bhd,bhe->bhde', k_t, delta)
        return S, jnp.einsum('bhd,bhde->bhe', q_t, S)

    S, o = lax.scan(step, S0.astype(jnp.float32), xs)
    return jnp.moveaxis(o, 0, 1), S

def token_mixing(x, fox_cache, page_table, conv_buf, S0, mix):
    (g_pre, w_in, b_f, conv_w, dt_bias, a_log, g_gdn, w_branch_fox, w_branch_gdn, w_out, g_post) = mix
    B, T, _ = x.shape
    h = rmsnorm(x, g_pre)
    qa, ka, va, logf, qg, kg, vg, g, beta, z, gate_a, gate_b, new_buf = mixer_inputs(h, conv_buf, w_in, b_f, conv_w, dt_bias, a_log)
    if fox_cache is None:
        o_a = fox_prompt(qa, ka, va, logf)
        o_g, S = gdn_chunked(qg, kg, vg, g, beta, S0)
    else:
        cache_k, cache_v, cache_logf = fox_cache
        o_a = fox_sample(qa, ka, va, logf, cache_k, cache_v, cache_logf, page_table)
        o_g, S = gdn_recurrent(qg, kg, vg, g, beta, S0)
    o_g = rmsnorm(o_g.astype(x.dtype), g_gdn) * jax.nn.silu(z.reshape(B, T, GDN_HEADS, GDN_HEAD_DIM))
    y_a = o_a.reshape(B, T, FOX_WIDTH) @ w_branch_fox
    y_g = o_g.reshape(B, T, GDN_WIDTH) @ w_branch_gdn
    y = (jax.nn.sigmoid(gate_a) * y_a + jax.nn.sigmoid(gate_b) * y_g) @ w_out
    x = x + rmsnorm(y, g_post)
    return x, (ka, va, logf.astype(x.dtype), S.astype(S0.dtype), new_buf)

def setup_inputs(seed: int = 0) -> dict:
    key = jax.random.key(seed)
    keys = iter(jax.random.split(key, 40))
    f32 = jnp.float32
    n_pages = PAST_LEN // PAGE_SIZE
    n_phys = (DEC_BATCH * n_pages * 5) // 4

    def nrm(shape, scale=1.0):
        return scale * jax.random.normal(next(keys), shape, f32)

    def gain(n):
        return 1.0 + 0.02 * nrm((DEPTH, n))

    perm = jax.random.permutation(next(keys), n_phys)[: DEC_BATCH * n_pages]
    page_table = perm.reshape(DEC_BATCH, n_pages).astype(jnp.int32)
    dt = jnp.exp(jax.random.uniform(next(keys), (DEPTH, GDN_HEADS), f32, math.log(1e-3), math.log(1e-1)))
    dt_bias = dt + jnp.log(-jnp.expm1(-dt))
    a_log = jnp.log(jax.random.uniform(next(keys), (DEPTH, GDN_HEADS), f32, 1.0, 16.0))
    return {
        "x_prompt": nrm((BATCH, SEQ, D_MODEL)),
        "x_sample": nrm((DEC_BATCH, DEC_SEQ, D_MODEL)),
        "cache_k": nrm((DEPTH, n_phys, PAGE_SIZE, FOX_HEADS, FOX_HEAD_DIM)),
        "cache_v": nrm((DEPTH, n_phys, PAGE_SIZE, FOX_HEADS, FOX_HEAD_DIM)),
        "cache_logf": jax.nn.log_sigmoid(FORGET_BIAS_INIT + nrm((DEPTH, n_phys, PAGE_SIZE, FOX_HEADS))),
        "state_gdn": nrm((DEPTH, DEC_BATCH, GDN_HEADS, GDN_HEAD_DIM, GDN_HEAD_DIM), GDN_HEAD_DIM ** -0.5),
        "state_conv": nrm((DEPTH, DEC_BATCH, CONV_WIDTH - 1, CONV_CH)),
        "page_table": page_table,
        "ffn1_norm_pre": gain(D_MODEL),
        "ffn1_w_gate": nrm((DEPTH, D_MODEL, D_FF), D_MODEL ** -0.5),
        "ffn1_w_up": nrm((DEPTH, D_MODEL, D_FF), D_MODEL ** -0.5),
        "ffn1_w_down": nrm((DEPTH, D_FF, D_MODEL), D_FF ** -0.5),
        "ffn1_norm_post": gain(D_MODEL),
        "mix_norm_pre": gain(D_MODEL),
        "w_in": nrm((DEPTH, D_MODEL, P_IN), D_MODEL ** -0.5),
        "fox_forget_bias": FORGET_BIAS_INIT + nrm((DEPTH, FOX_HEADS), 0.1),
        "gdn_conv_w": nrm((DEPTH, CONV_WIDTH, CONV_CH), CONV_WIDTH ** -0.5),
        "gdn_dt_bias": dt_bias,
        "gdn_a_log": a_log,
        "gdn_out_norm": gain(GDN_HEAD_DIM),
        "w_branch_fox": nrm((DEPTH, FOX_WIDTH, D_MODEL), FOX_WIDTH ** -0.5),
        "w_branch_gdn": nrm((DEPTH, GDN_WIDTH, D_MODEL), GDN_WIDTH ** -0.5),
        "w_out": nrm((DEPTH, D_MODEL, D_MODEL), D_MODEL ** -0.5),
        "mix_norm_post": gain(D_MODEL),
        "ffn2_norm_pre": gain(D_MODEL),
        "ffn2_w_gate": nrm((DEPTH, D_MODEL, D_FF), D_MODEL ** -0.5),
        "ffn2_w_up": nrm((DEPTH, D_MODEL, D_FF), D_MODEL ** -0.5),
        "ffn2_w_down": nrm((DEPTH, D_FF, D_MODEL), D_FF ** -0.5),
        "ffn2_norm_post": gain(D_MODEL),
    }

def stack_field(states, i):
    return jnp.stack([s[i] for s in states], axis=0)

def reference(x_prompt, x_sample, cache_k, cache_v, cache_logf, state_gdn, state_conv, page_table,
              ffn1_norm_pre, ffn1_w_gate, ffn1_w_up, ffn1_w_down, ffn1_norm_post,
              mix_norm_pre, w_in, fox_forget_bias, gdn_conv_w, gdn_dt_bias, gdn_a_log, gdn_out_norm,
              w_branch_fox, w_branch_gdn, w_out, mix_norm_post,
              ffn2_norm_pre, ffn2_w_gate, ffn2_w_up, ffn2_w_down, ffn2_norm_post):
    xp, xs = x_prompt, x_sample
    st_p, st_s = [], []
    for l in range(DEPTH):
        ffn1 = (ffn1_norm_pre[l], ffn1_w_gate[l], ffn1_w_up[l], ffn1_w_down[l], ffn1_norm_post[l])
        ffn2 = (ffn2_norm_pre[l], ffn2_w_gate[l], ffn2_w_up[l], ffn2_w_down[l], ffn2_norm_post[l])
        mix = (mix_norm_pre[l], w_in[l], fox_forget_bias[l], gdn_conv_w[l], gdn_dt_bias[l], gdn_a_log[l],
               gdn_out_norm[l], w_branch_fox[l], w_branch_gdn[l], w_out[l], mix_norm_post[l])
        xp = swiglu_half(xp, *ffn1)
        buf0 = jnp.zeros((xp.shape[0], CONV_WIDTH - 1, CONV_CH), xp.dtype)
        s0 = jnp.zeros((xp.shape[0], GDN_HEADS, GDN_HEAD_DIM, GDN_HEAD_DIM), xp.dtype)
        xp, sp = token_mixing(xp, None, None, buf0, s0, mix)
        xp = swiglu_half(xp, *ffn2)
        xs = swiglu_half(xs, *ffn1)
        xs, ss = token_mixing(xs, (cache_k[l], cache_v[l], cache_logf[l]), page_table, state_conv[l], state_gdn[l], mix)
        xs = swiglu_half(xs, *ffn2)
        st_p.append(sp)
        st_s.append(ss)
    k_p, v_p, lf_p, S_p, buf_p = (stack_field(st_p, 0), stack_field(st_p, 1), stack_field(st_p, 2), stack_field(st_p, 3), stack_field(st_p, 4))
    k_s, v_s, lf_s, S_s, buf_s = (stack_field(st_s, 0), stack_field(st_s, 1), stack_field(st_s, 2), stack_field(st_s, 3), stack_field(st_s, 4))
    return (xp, xs, k_p, v_p, lf_p, S_p, buf_p, k_s, v_s, lf_s, S_s, buf_s)


_drawn_inputs = setup_inputs


def setup_inputs(seed=0):
    import zlib

    import numpy as np

    out = dict(_drawn_inputs(seed))
    spreads = {}
    factors = {'ffn1_norm_pre': 2.988,
     'ffn1_norm_post': 4.166,
     'gdn_out_norm': 12.738,
     'mix_norm_post': 11.257,
     'ffn2_norm_pre': 18.727,
     'ffn2_norm_post': 110.299,
     'cache_logf': 10.227}
    for name, (base, spread) in spreads.items():
        noise = np.random.default_rng([zlib.crc32(name.encode()), seed]).standard_normal(out[name].shape)
        drawn = base * np.exp(spread * noise) if base else spread * noise
        out[name] = __import__('jax').numpy.asarray(drawn.astype(out[name].dtype))
    for name, factor in factors.items():
        out[name] = (out[name] * factor).astype(out[name].dtype)
    return out
```

```python
from contextlib import ExitStack

import numpy as np

import concourse.bass as bass
from concourse import mybir

F32 = mybir.dt.float32
F32R = mybir.dt.float32r
I32 = mybir.dt.int32
ALU = mybir.AluOpType
ACT = mybir.ActivationFunctionType
AX = mybir.AxisListType

P = 128
D = 1024
KD = D // P
SEQ = 512
NS = 8
T = SEQ + NS
HT = T // 2
FF = 2816
KF = FF // P
NKD = KF // 2
PAGES = 32
PHYS = 320
HEADS = 8
DH = 64
GH = 4
C = 64
NCH = SEQ // C
EPS = 1e-6
NEG = -1e30
KV_RING = 3
LEVELS = 6

V_PRE1, V_POST1, V_PREM, V_POSTM, V_PRE2, V_POST2, V_GDN, V_CONV, V_BIAS, V_ALOG, V_SIGN = (
    0, 8, 16, 24, 32, 40, 48, 49, 97, 98, 99)
NVEC = 100
Q0, K0, V0, CV0, Z0, NPROJ = 0, 4, 8, 12, 24, 28


def ds(i, n=1):
    return bass.ds(i, n)


def program(nc, a):
    ctx = ExitStack()
    with ctx:
        start_of = {}

        def sb(name, shape, dt=F32, scope=ctx):
            start_of[name] = -(-nc.sbuf_base // 32) * 32
            return scope.enter_context(nc.sbuf_tensor(name, shape, dt))

        def over(name, shape, dt, tensor, skip=0):
            return nc.alloc_sbuf_tensor_at(name, shape, dt, offset=start_of[tensor] + 4 * skip)

        def sem(name):
            return ctx.enter_context(nc.semaphore(name))

        x = sb("x", [P, KD, T])
        ident = sb("ident", [P, P])
        ones = sb("ones", [P, P])
        vecs = sb("vecs", [P, NVEC])
        w_raw = sb("w_raw", [P, 2, NKD, P])
        w_high = sb("w_high", [P, 2, NKD, P], F32R)
        w_low = sb("w_low", [P, 2, NKD, P], F32R)
        psum = ctx.enter_context(nc.psum_tensor("psum", [P, 8, 512], F32))

        def pair(g):
            return psum[:, 2 * g:2 * g + 2, 0:HT]

        def halves(t):
            return t.rearrange("p (h t) -> p h t", h=2)

        loaded = [sem("block_loaded0"), sem("block_loaded1")]
        high_done = sem("block_high_done")
        low_done = sem("block_low_done")
        block_used = sem("block_used")
        s_in = sem("inputs_loaded")
        s_out = sem("outputs_stored")
        count = {"block": 0, "out": 0, "in": 0}

        def load_block(eng, dram, i, n, u, nk):
            if not isinstance(n, int) or n >= 2:
                eng.wait_ge(low_done, n - 1)
            eng.dma_start(w_raw[:, u, 0:nk, :].rearrange("p k m -> p (k m)"),
                          dram[ds(i), :, :].rearrange("a p k -> p (a k)")).then_inc(loaded[u], 16)

        def load_stream(eng, dram, blocks, n0, nk):
            for u in range(2):
                load_block(eng, dram, u, n0 + u, u, nk)
            with eng.Fori(1, blocks // 2) as i:
                for u in range(2):
                    load_block(eng, dram, i * 2 + u, i * 2 + (n0 + u), u, nk)

        def split_high(act, n, u, nk, guard=True):
            act.wait_ge(loaded[u], (n - u) * 8 + 16)
            if guard:
                act.wait_ge(block_used, n - 1)
            act.activation(w_high[:, u, 0:nk, :], w_raw[:, u, 0:nk, :], ACT.Copy).then_inc(high_done, 1)

        def split_low(dve, n, u, nk):
            dve.wait_ge(high_done, n + 1)
            dve.tensor_tensor(w_low[:, u, 0:nk, :], w_raw[:, u, 0:nk, :],
                              w_high[:, u, 0:nk, :].bitcast(F32), ALU.subtract).then_inc(low_done, 1)

        def block_products(pe, n, u, ks, banks, high, low, k0, start, stop, done=None):
            pe.wait_ge(low_done, n + 1)
            last = ks[-1]
            for h in range(2):
                tok = slice(h * HT, (h + 1) * HT)
                out = psum[:, 2 * banks + h, 0:HT]
                for j, k in enumerate(ks):
                    s = start and j == 0
                    e = stop and k == last
                    pe.matmul(out, w_high[:, u, k, :], high[:, k0 + j, tok], start=s, stop=False)
                    pe.matmul(out, w_high[:, u, k, :], low[:, k0 + j, tok], start=False, stop=False)
                    mm = pe.matmul(out, w_low[:, u, k, :], high[:, k0 + j, tok], start=False, stop=e)
            mm.then_inc(done if done is not None else block_used, 1)

        norm_sq = sem("norm_squares")
        norm_sum = sem("norm_sum")
        norm_root = sem("norm_root")
        norm_rec = sem("norm_factor")
        sq = sb("sq", [P, 2, T])
        root = sb("root", [P, T])
        factor = sb("factor", [P, T])
        norms = [0]

        def norm_act(act, src, n):
            for k in range(KD):
                if n or k >= 2:
                    act.wait_ge(norm_sum, n * KD + k - 1)
                act.activation(sq[:, k % 2, :], src[:, k, :], ACT.Square).then_inc(norm_sq, 1)
            act.wait_ge(norm_sum, (n + 1) * KD)
            act.activation(halves(root[:, :]), psum[:, 6:8, 0:HT], ACT.Sqrt, bias=eps_col[:, 0:1],
                           scale=1.0 / D).then_inc(norm_root, 1)

        def norm_pe(pe, n):
            for k in range(KD):
                pe.wait_ge(norm_sq, n * KD + k + 1)
                for h in range(2):
                    mm = pe.matmul(psum[:, 6 + h, 0:HT], ones[:, :], sq[:, k % 2, h * HT:(h + 1) * HT],
                                   start=(k == 0), stop=(k == KD - 1))
                mm.then_inc(norm_sum, 1)

        def norm_dve(dve, n):
            dve.wait_ge(norm_root, n + 1)
            dve.reciprocal(factor[:, :], root[:, :]).then_inc(norm_rec, 1)

        eps_col = sb("eps_col", [P, 1])
        s_eps = sem("eps_set")

        h_f = sb("h_f", [P, 2, T])
        h_ready = sem("h_ready")
        h_high_done = sem("h_high_done")
        h_low_done = sem("h_low_done")
        hcount = [0]

        def scaled_dve(dve, vcol, h_high, h_low, n, m0):
            dve.wait_ge(norm_rec, n + 1)
            for k in range(KD):
                if k >= 2:
                    dve.wait_ge(h_low_done, m0 + k - 1)
                dve.scalar_tensor_tensor(out=h_f[:, k % 2, :], in0=x[:, k, :], scalar=vecs[:, vcol + k:vcol + k + 1],
                                         in1=factor[:, :], op0=ALU.mult, op1=ALU.mult).then_inc(h_ready, 1)
                if k >= 1:
                    low_of(dve, h_high, h_low, m0, k - 1)
            low_of(dve, h_high, h_low, m0, KD - 1)

        def low_of(dve, h_high, h_low, m0, k):
            dve.wait_ge(h_high_done, m0 + k + 1)
            dve.tensor_tensor(h_low[:, k, :], h_f[:, k % 2, :], h_high[:, k, :].bitcast(F32),
                              ALU.subtract).then_inc(h_low_done, 1)

        def scaled_act(act, h_high, m0):
            for k in range(KD):
                act.wait_ge(h_ready, m0 + k + 1)
                act.activation(h_high[:, k, :], h_f[:, k % 2, :], ACT.Copy).then_inc(h_high_done, 1)

        res_tmp = h_f
        res_scaled = sem("residual_scaled")
        x_new = sem("x_updated")

        def residual_dve(dve, y, vcol, weight, n, r0):
            dve.wait_ge(norm_rec, n + 1)
            for k in range(KD):
                if k >= 2:
                    dve.wait_ge(x_new, r0 + k - 1)
                dve.scalar_tensor_tensor(out=res_tmp[:, k % 2, :], in0=y[:, k, :], scalar=vecs[:, vcol + k:vcol + k + 1],
                                         in1=factor[:, :], op0=ALU.mult, op1=ALU.mult).then_inc(res_scaled, 1)
                dve.wait_ge(res_scaled, r0 + k + 1)
                dve.scalar_tensor_tensor(out=x[:, k, :], in0=res_tmp[:, k % 2, :], scalar=weight, in1=x[:, k, :],
                                         op0=ALU.mult, op1=ALU.add).then_inc(x_new, 1)

        gate_silu = sem("gate_silu_done")
        hid_f = sem("hidden_done")
        hid_high = sem("hidden_high_done")
        hid_low = sem("hidden_low_done")
        y_copied = sem("y_copied")
        group_done = sem("product_group_done")

        def ffn(which, w_gu, w_dn, v_pre, v_post, store):
            n0 = count["block"]
            nb = n0 + 2 * KF
            norm_n = norms[0]
            m0 = hcount[0]
            f0 = which * KF
            y0 = which * KD
            r0 = norms[0] // 2 * KD
            with ExitStack() as scope:
                h_high = sb(f"h_high{which}", [P, KD, T], F32R, scope)
                h_low = sb(f"h_low{which}", [P, KD, T], F32R, scope)
                a_high = sb(f"a_high{which}", [P, KF, T], F32R, scope)
                a_low = sb(f"a_low{which}", [P, KF, T], F32R, scope)
                sg = sb(f"silu{which}", [P, 2, T], F32, scope)
                af = sb(f"hidden{which}", [P, 2, T], F32, scope)
                y = over(f"y{which}", [P, KD, T], F32, f"h_high{which}")
                g0 = {0: 0, 1: 2 * KF + KD + count["groups"] if which else 0}[which]
                block = scope.enter_context(nc.Block())

                @block.sync
                def _(sp):
                    if which == 0:
                        sp.dma_start(x[:, :, :], a["x"]).then_inc(s_in, 16)
                        sp.dma_start(ident[:, :], a["ident"]).then_inc(s_in, 16)
                        sp.dma_start(ones[:, :], a["ones"]).then_inc(s_in, 16)
                        sp.dma_start(vecs[:, :], a["vecs"]).then_inc(s_in, 16)
                    load_stream(sp, w_gu, 2 * KF, n0, KD)
                    load_stream(sp, w_dn, 2 * KD, nb, NKD)
                    if store:
                        for k in range(KD):
                            sp.wait_ge(x_new, r0 + k + 1)
                            sp.dma_start(a["o_y"][:, k, :], x[:, k, :]).then_inc(s_out, 16)
                        count["out"] += KD
                        sp.wait_ge(s_out, 16 * count["out"])

                @block.gpsimd
                def _(pool):
                    if which == 0:
                        pool.memset(eps_col[:, :], EPS).then_inc(s_eps, 1)

                @block.scalar
                def _(act):
                    act.wait_ge(s_in, 64)
                    act.wait_ge(s_eps, 1)
                    norm_act(act, x, norm_n)
                    scaled_act(act, h_high, m0)

                    def silu(m, u):
                        act.wait_ge(block_used, m * 2 + (n0 + 1))
                        if not isinstance(m, int) or m >= 2:
                            act.wait_ge(hid_f, m + (f0 - 1))
                        act.activation(halves(sg[:, u, :]), pair(0), ACT.Silu).then_inc(gate_silu, 1)

                    def high(m, u):
                        act.wait_ge(hid_f, m + (f0 + 1))
                        act.activation(a_high[:, ds(m) if not isinstance(m, int) else slice(m, m + 1), :],
                                       af[:, u:u + 1, :], ACT.Copy).then_inc(hid_high, 1)

                    split_high(act, n0, 0, KD, guard=n0 > 0)
                    split_high(act, n0 + 1, 1, KD, guard=n0 > 0)

                    def body(m, tail=False):
                        for u in range(2):
                            nk = NKD if tail and u == 1 else KD
                            split_high(act, m * 2 + (n0 + 2 * u + 2), 0, nk)
                            silu(m + u, u)
                            split_high(act, m * 2 + (n0 + 2 * u + 3), 1, nk)
                            high(m + u, u)
                    body(0)
                    with act.Fori(1, KF // 2 - 1) as i:
                        body(i * 2)
                    body(KF - 2, tail=True)

                    def down(m, tail=False):
                        for u in range(2):
                            if not (tail and u == 1):
                                split_high(act, m * 2 + (nb + 2 * u + 2), 0, NKD)
                                split_high(act, m * 2 + (nb + 2 * u + 3), 1, NKD)
                            act.wait_ge(block_used, m * 2 + (nb + 2 * u + 2))
                            if isinstance(m, int):
                                dst = y[:, m + u, :]
                                dst = halves(dst)
                            else:
                                dst = y[:, ds(m + u), :].rearrange("p a (h t) -> p (a h) t", h=2)
                            act.activation(dst, pair(u), ACT.Copy).then_inc(y_copied, 1)
                    with act.Fori(0, KD // 2 - 1) as i:
                        down(i * 2)
                    down(KD - 2, tail=True)
                    act.wait_ge(y_copied, y0 + KD)
                    norm_act(act, y, norm_n + 1)

                @block.vector
                def _(dve):
                    norm_dve(dve, norm_n)
                    scaled_dve(dve, v_pre, h_high, h_low, norm_n, m0)
                    split_low(dve, n0, 0, KD)
                    split_low(dve, n0 + 1, 1, KD)

                    def body(m, tail=False):
                        for u in range(2):
                            nk = NKD if tail and u == 1 else KD
                            split_low(dve, m * 2 + (n0 + 2 * u + 2), 0, nk)
                            split_low(dve, m * 2 + (n0 + 2 * u + 3), 1, nk)
                            dve.wait_ge(block_used, m * 2 + (n0 + 2 * u + 2))
                            dve.wait_ge(gate_silu, m + (f0 + u + 1))
                            if not isinstance(m, int) or m >= 2:
                                dve.wait_ge(hid_low, m + (f0 + u - 1))
                            dve.tensor_tensor(halves(af[:, u, :]), halves(sg[:, u, :]), pair(1),
                                              ALU.mult).then_inc(hid_f, 1)
                            dve.wait_ge(hid_high, m + (f0 + u + 1))
                            mm = m + u
                            at = slice(mm, mm + 1) if isinstance(mm, int) else ds(mm)
                            dve.tensor_tensor(a_low[:, at, :], af[:, u:u + 1, :], a_high[:, at, :].bitcast(F32),
                                              ALU.subtract).then_inc(hid_low, 1)
                    body(0)
                    with dve.Fori(1, KF // 2 - 1) as i:
                        body(i * 2)
                    body(KF - 2, tail=True)

                    def down(m, tail=False):
                        for u in range(2):
                            if not (tail and u == 1):
                                split_low(dve, m * 2 + (nb + 2 * u + 2), 0, NKD)
                                split_low(dve, m * 2 + (nb + 2 * u + 3), 1, NKD)
                    with dve.Fori(0, KD // 2 - 1) as i:
                        down(i * 2)
                    down(KD - 2, tail=True)
                    norm_dve(dve, norm_n + 1)
                    residual_dve(dve, y, v_post, 0.5, norm_n + 1, r0)
                    dve.wait_ge(x_new, r0 + KD)

                @block.tensor
                def _(pe):
                    pe.wait_ge(s_in, 64)
                    norm_pe(pe, norm_n)
                    pe.wait_ge(h_low_done, m0 + KD)

                    def body(m):
                        if not isinstance(m, int) or m >= 1:
                            pe.wait_ge(gate_silu, m + f0)
                        block_products(pe, m * 2 + n0, 0, range(KD), 0, h_high, h_low, 0, True, True)
                        if not isinstance(m, int) or m >= 1:
                            pe.wait_ge(hid_f, m + f0)
                        block_products(pe, m * 2 + (n0 + 1), 1, range(KD), 1, h_high, h_low, 0, True, True)
                    body(0)
                    with pe.Fori(1, KF) as m:
                        body(m)
                    pe.wait_ge(hid_low, f0 + KF)

                    def down(m, first=False):
                        for u in range(2):
                            if not first:
                                pe.wait_ge(y_copied, m + (y0 + u - 1))
                            block_products(pe, m * 2 + (nb + 2 * u), 0, range(NKD), u, a_high, a_low, 0, True, False)
                            block_products(pe, m * 2 + (nb + 2 * u + 1), 1, range(NKD), u, a_high, a_low, NKD, False, True)
                    down(0, first=True)
                    with pe.Fori(1, KD // 2) as i:
                        down(i * 2)
                    norm_pe(pe, norm_n + 1)
            count["block"] = nb + 2 * KD
            norms[0] += 2
            hcount[0] += KD

        def mixer():
            mix = ctx.enter_context(ExitStack())
            proj = sb("proj", [P, Z0 + 1, T], F32, mix)
            rows = sb("rows", [96, T], F32, mix)
            cum = sb("cum", [96, SEQ], F32, mix)
            start_of["branch"] = -(-nc.sbuf_base // 32) * 32
            h_high = sb("mix_h_high", [P, KD, T], F32R, mix)
            h_low = sb("mix_h_low", [P, KD, T], F32R, mix)
            fox_o = (over("fox_high", [P, 4, T], F32R, "branch"), over("fox_low", [P, 4, T], F32R, "branch", 4 * T))
            gdn_o = (over("gdn_high", [P, 4, T], F32R, "branch", 8 * T), over("gdn_low", [P, 4, T], F32R, "branch", 12 * T))
            attention(proj, rows, cum, h_high, h_low, fox_o)
            gdn(proj, rows, cum, gdn_o)
            merge(fox_o, gdn_o)
            mix.close()

        def attention(proj, rows, cum, h_high, h_low, fox_o):
            n0 = count["block"]
            norm_n, m0 = norms[0], hcount[0]
            NB, FIRST = NPROJ + 16, 12
            R, J = 2, 4
            NG = PAGES // 4
            NQ = SEQ // P
            tiles = [(h, i) for h in range(HEADS) for i in range(NQ)]
            N = len(tiles)
            VT = 17
            lin_out = sem("block_out_taken")
            spilled = [sem("spilled0"), sem("spilled1")]
            small_in = sem("small_loaded")
            small_pe = sem("small_products")
            small_dve = sem("small_vector_steps")
            small_act = sem("small_scalar_steps")
            stored = sem("proj_stored")
            conv_out = sem("conv_state_stored")
            pt_loaded = sem("page_table_loaded")
            gsel_loaded = sem("group_sel_loaded")
            ptb_loaded = sem("page_table_spread")
            mask_loaded = sem("head_mask_loaded")
            idx_done = sem("page_rows_ready")
            lf_loaded = sem("logf_gathered")
            kv_loaded = [sem(f"kv_loaded{u}") for u in range(4)]
            kv_used = sem("kv_used")
            qbd_done = sem("query_blocks_ready")
            sc_dve = sem("scores_done")
            pre_pe = sem("sample_small_products")
            sdve = sem("sample_vector_steps")
            nbias = sem("sample_max_ready")
            p_exp = sem("sample_exp_done")
            pt_pe = sem("prob_transposed")
            pt_act = sem("prob_copied")
            om_done = sem("sample_out_masked")
            so_pe = sem("sample_out_turned")
            so_copy = sem("sample_out_copied")
            fin = sem("fox_constants_loaded")
            vt_pe = sem("fox_values_turned")
            vt_copy = sem("fox_values_copied")
            fs_pe = sem("fox_scores")
            f_neg = sem("fox_max_ready")
            f_exp = sem("fox_exp_done")
            f_dve = sem("fox_probs_ready")
            ft_pe = sem("fox_probs_turned")
            ft_copy = sem("fox_probs_copied")
            fo_pe = sem("fox_out")
            fo_high = sem("fox_out_high")
            fo_low = sem("fox_out_low")
            conv_in = sem("conv_state_loaded")
            cs = sem("conv_steps_done")
            spill = h_f
            fox_high, fox_low = fox_o
            with ExitStack() as scope:
                sc = sb("scores", [P, PAGES * P + 1], F32, scope)
                ring = sb("kv_ring", [P, 4, J, 512], F32, scope)
                qbd = sb("query_blocks", [P, 4, J, 32], F32, scope)
                pt1 = sb("pages", [1, NS * PAGES], I32, scope)
                ptb = sb("pages_bc", [P, R, PAGES], I32, scope)
                hrow = sb("head_row", [P, 1], I32, scope)
                idx = sb("logf_rows", [P, R, PAGES], I32, scope)
                gsel = sb("group_sel", [P, 4], F32, scope)
                st = sb("sample_stats", [P, R, 24], F32, scope)
                so = sb("sample_o", [P, 4, NS], F32, scope)
                stat = sb("fox_stats", [P, N, 3], F32, scope)
                coef = sb("coef", [96, 1], F32, scope)
                w16 = over("w_small", [P, KD, 96], F32, "kv_ring")
                w16_high = over("w_small_high", [P, KD, 96], F32R, "kv_ring", KD * 96)
                w16_low = over("w_small_low", [P, KD, 96], F32R, "kv_ring", 2 * KD * 96)
                starts = over("chunk_start", [96, SEQ], F32, "kv_ring", 3 * KD * 96)
                wz = over("small_z", [96, T], F32, "sq")
                wb = over("small_beta", [96, T], F32, "sq", T)
                wl = over("small_log", [96, T], F32, "root")
                wsum = over("small_sum", [96, T], F32, "factor")
                hmask = over("head_mask", [P, 512], F32, "sq")
                om = over("sample_out", [P, 512], F32, "factor")
                vb = over("value_bc", [P, 4, J, 32], F32, "root")
                prb = over("fox_probs", [P, 2, SEQ], F32, "branch", 8 * T)
                prt = over("fox_probs_t", [P, 2, SEQ], F32, "branch", 8 * T + 2 * SEQ)
                sel = over("fox_sel", [8, 8, P], F32, "branch", 8 * T + 4 * SEQ)
                vtok = over("fox_v", [P, NQ, 512], F32, "w_raw")
                causal = over("causal", [P, P], F32, "w_raw", NQ * 512)
                buf = over("conv_buf", [P, 12, 3, NS], F32, "w_raw", NQ * 512 + P)
                tap = over("conv_tap", [P, 12, NS], F32, "w_raw", NQ * 512 + P + 288)
                cnew = over("conv_new", [P, 12, NS], F32, "w_raw", NQ * 512 + P + 384)
                MX, RS, SN, NM, PN, RI = 0, 8, 16, 17, 18, 19
                block = scope.enter_context(nc.Block())

                @block.sync
                def _(sp):
                    sp.dma_start(w16[:, :, :], a["w_small"]).then_inc(small_in, 16)
                    sp.dma_start(starts[:, :], a["chunk_start"][0:96, :]).then_inc(small_in, 16)
                    load_stream(sp, a["w_proj"], FIRST + 2, n0, KD)
                    sp.dma_start(pt1[:, :], a["page_order"]).then_inc(pt_loaded, 16)
                    sp.dma_start(gsel[:, :], a["group_sel"]).then_inc(gsel_loaded, 16)
                    sp.wait_ge(pt_loaded, 16)
                    sp.wait_ge(small_dve, 8)

                    def pages(g, r):
                        _, p = nc.values_load_multi_w_load_instructions(
                            pt1[0:1, ds(g * 16 + 4 * PAGES * r, 16)], engines=[mybir.EngineType.SP],
                            min_val=0, max_val=PHYS - 1)
                        return p

                    def load_step(u, p, cache, used):
                        if used is not None:
                            sp.wait_ge(kv_used, used)
                        for j in range(J):
                            sp.dma_start(ring[:, u, j, :], cache[ds(p[4 * u + j]), :, :]
                                         .rearrange("a p k -> p (a k)")).then_inc(kv_loaded[u], 16)
                    p = pages(0, 0)
                    for u in range(4):
                        load_step(u, p, a["cache_k"], None)

                    def group(g, r, cache, g0, block_n):
                        p = pages(g, r)
                        for half in range(2):
                            if block_n is not None:
                                load_block(sp, a["w_proj"], block_n + half, block_n + (n0 + half), half, KD)
                            for u in (2 * half, 2 * half + 1):
                                load_step(u, p, cache, g * 4 + (4 * g0 + u - 3))
                    with sp.Fori(1, NG) as g:
                        group(g, 0, a["cache_k"], 0, g * 2 + FIRST)
                    with sp.Fori(0, NG) as g:
                        group(g, 0, a["cache_v"], NG, g * 2 + (FIRST + 2 * NG))
                    sp.wait_ge(lin_out, Z0)
                    sp.dma_start(a["o_proj"], proj[:, K0:Z0, :]).then_inc(stored, 16)
                    sp.dma_start(a["o_conv_s"][:, :, 2, :], proj[:, CV0:Z0, SEQ:T]).then_inc(stored, 16)
                    sp.dma_start(a["o_logf"], rows[0:HEADS, :]).then_inc(stored, 16)
                    group(0, 1, a["cache_k"], 2 * NG, None)
                    sp.wait_ge(block_used, n0 + NB)
                    sp.dma_start(sel[:, :, :].rearrange("p h k -> p (h k)"), a["sel"][0:8, :]).then_inc(fin, 16)
                    sp.dma_start(causal[:, :], a["causal"]).then_inc(fin, 16)
                    sp.dma_start(buf[:, :, :, :], a["conv_in"]).then_inc(conv_in, 16)
                    sp.wait_ge(conv_in, 16)
                    sp.dma_start(a["o_conv_s"][:, :, 0:2, :], buf[:, :, 1:3, :]).then_inc(conv_out, 16)
                    with sp.Fori(1, NG) as g:
                        group(g, 1, a["cache_k"], 2 * NG, None)
                    with sp.Fori(0, NG) as g:
                        group(g, 1, a["cache_v"], 3 * NG, None)
                    sp.wait_ge(stored, 48)
                    sp.wait_ge(conv_out, 16)
                    for u in range(2):
                        sp.wait_ge(spilled[u], 16 * (NB - Z0) // 2)

                @block.gpsimd
                def _(pool):
                    pool.memset(qbd[:, :, :, :], 0.0).then_inc(qbd_done, 1)
                    pool.dma_start(hrow[:, :], a["head_row"]).then_inc(ptb_loaded, 16)
                    for r in range(R):
                        for j in range(J):
                            pool.dma_start(ptb[32 * j:32 * j + 32, r, :],
                                           a["page_table"][J * r + j:J * r + j + 1, :].broadcast_to([32, PAGES])
                                           ).then_inc(ptb_loaded, 16)

                    def gather(r, t):
                        if r:
                            pool.wait_ge(kv_used, PAGES + min(t + 2, PAGES))
                        pool.indirect_dma_start(sc[:, t * P + 1:(t + 1) * P + 1], None, a["cache_logf"],
                                                bass.IndirectOffsetOnAxis(ap=idx[:, r, t:t + 1], axis=0)
                                                ).then_inc(lf_loaded, 16)

                    def keep(n):
                        pool.wait_ge(lin_out, n + 1)
                        pool.dma_start(a["spill"][n - Z0, :, :], spill[:, n % 2, :]).then_inc(spilled[n % 2], 16)
                    pool.wait_ge(idx_done, 1)
                    for t in range(PAGES):
                        gather(0, t)
                    for n in range(Z0, NPROJ):
                        keep(n)
                    pool.wait_ge(idx_done, 2)
                    for g in range(NG):
                        keep(NPROJ + 2 * g)
                        keep(NPROJ + 2 * g + 1)
                        for t in range(max(4 * g - 3, 0), 4 * g + 1):
                            gather(1, t)
                    for t in range(4 * NG - 3, PAGES):
                        gather(1, t)
                    pool.wait_ge(small_dve, 8)
                    pool.dma_start(hmask[:, :], a["head_mask"]).then_inc(mask_loaded, 16)

                @block.scalar
                def _(act):
                    norm_act(act, x, norm_n)
                    scaled_act(act, h_high, m0)
                    act.wait_ge(small_in, 32)
                    act.activation(w16_high[:, :, :], w16[:, :, :], ACT.Copy).then_inc(small_act, 1)
                    split_high(act, n0, 0, KD)
                    split_high(act, n0 + 1, 1, KD)

                    def copy(n, u):
                        act.wait_ge(block_used, n + (n0 + 1))
                        dst = proj[:, ds(n), :].rearrange("p a (h t) -> p (a h) t", h=2)
                        act.activation(dst, pair(u), ACT.Copy).then_inc(lin_out, 1)

                    def copies(first, last):
                        with act.Fori(first // 2, last // 2) as i:
                            for u in range(2):
                                split_high(act, i * 2 + (n0 + 2 + u), u, KD)
                                copy(i * 2 + u, u)
                    copies(0, FIRST)
                    act.wait_ge(small_dve, 3)
                    act.activation(wl[:, :], wl[:, :], ACT.Exp).then_inc(small_act, 1)
                    act.activation(coef[:, :], vecs[0:96, V_ALOG:V_ALOG + 1], ACT.Exp).then_inc(small_act, 1)
                    act.activation(wb[64:96, :], wz[64:96, :], ACT.Exp, scale=-1.0).then_inc(small_act, 1)
                    act.wait_ge(small_act, 2)
                    act.activation(wl[:, :], wl[:, :], ACT.Ln, bias=1.0).then_inc(small_act, 1)
                    copies(FIRST, Z0)

                    def spill_out(n, func):
                        u = n % 2
                        act.wait_ge(block_used, n0 + n + 1)
                        if n >= Z0 + 2:
                            act.wait_ge(spilled[u], (n - Z0) // 2 * 16)
                        act.activation(halves(spill[:, u, :]), pair(u), func).then_inc(lin_out, 1)

                    def prob_exp(r, g):
                        if g == 0:
                            act.wait_ge(nbias, (NG + 2) * (r + 1))
                        act.activation(sc[:, g * 512:(g + 1) * 512], sc[:, g * 512:(g + 1) * 512], ACT.Exp,
                                       bias=st[:, r, NM:NM + 1], accum_out=st[:, r, RS + g:RS + g + 1]).then_inc(p_exp, 1)

                    def new_exp(r):
                        act.activation(st[:, r, PN:PN + 1], st[:, r, SN:SN + 1], ACT.Exp,
                                       bias=st[:, r, NM:NM + 1]).then_inc(p_exp, 1)

                    def prob_copy(r, g):
                        act.wait_ge(pt_pe, NG * r + g + 1)
                        act.activation(sc[:, g * 512:(g + 1) * 512], psum[:, 4 + g % 2, :], ACT.Copy).then_inc(pt_act, 1)
                    for n in range(Z0, NPROJ):
                        split_high(act, n0 + 2 + n, n % 2, KD)
                        spill_out(n, ACT.Silu)
                    for g in range(NG):
                        prob_exp(0, g)
                    new_exp(0)
                    for g in range(NG):
                        n = NPROJ + 2 * g
                        for u in range(2):
                            if n + u + 2 < NB:
                                split_high(act, n0 + 2 + n + u, u, KD)
                            spill_out(n + u, ACT.Sigmoid)
                            if u == 0:
                                prob_copy(0, g)

                    def exp(t):
                        S = (tiles[t][1] + 1) * P
                        act.wait_ge(f_neg, 2 * t + 2)
                        if t >= 2:
                            act.wait_ge(ft_pe, t - 1)
                        act.activation(prb[:, t % 2, 0:S], psum[:, t % 2, 0:S], ACT.Exp, bias=stat[:, t, 0:1],
                                       scale=DH ** -0.5, accum_out=stat[:, t, 1:2]).then_inc(f_exp, 1)

                    def turned(t):
                        S = (tiles[t][1] + 1) * P
                        act.wait_ge(ft_pe, t + 1)
                        if t >= 2:
                            act.wait_ge(fo_pe, t - 1)
                        act.activation(prt[:, t % 2, 0:S], psum[:, 2, 0:S], ACT.Copy).then_inc(ft_copy, 1)

                    def out(c):
                        act.wait_ge(fo_pe, 8 * c + 8)
                        act.activation(fox_high[:, c, 0:SEQ], psum[:, 3, :], ACT.Copy).then_inc(fo_high, 1)
                    for t in range(N + 2):
                        if t < N:
                            exp(t)
                        if 1 <= t <= N:
                            turned(t - 1)
                        if t % 8 == 1 and t > 8:
                            out(t // 8 - 1)
                        g = (t - VT) // 2
                        if t == VT - 1:
                            prob_exp(1, 0)
                            new_exp(1)
                        if t >= VT and (t - VT) % 2 == 0 and g < NG:
                            prob_copy(1, g)
                            if g + 1 < NG:
                                prob_exp(1, g + 1)
                    act.wait_ge(so_copy, R)
                    act.activation(fox_high[:, :, SEQ:T], so[:, :, :], ACT.Copy).then_inc(so_copy, 1)

                @block.vector
                def _(dve):
                    dve.wait_ge(ptb_loaded, 16 * 9)
                    for r in range(R):
                        dve.scalar_tensor_tensor(out=idx[:, r, :], in0=ptb[:, r, :], scalar=float(HEADS),
                                                 in1=hrow[:, :].broadcast_to([P, PAGES]), op0=ALU.mult,
                                                 op1=ALU.add).then_inc(idx_done, 1)
                    norm_dve(dve, norm_n)
                    scaled_dve(dve, V_PREM, h_high, h_low, norm_n, m0)
                    dve.wait_ge(small_act, 1)
                    dve.tensor_tensor(w16_low[:, :, :], w16[:, :, :], w16_high[:, :, :].bitcast(F32),
                                      ALU.subtract).then_inc(small_dve, 1)
                    split_low(dve, n0, 0, KD)
                    split_low(dve, n0 + 1, 1, KD)
                    dve.wait_ge(small_pe, 1)
                    dve.wait_ge(h_low_done, m0 + KD)
                    dve.tensor_scalar(halves(wz[:, :]), psum[0:96, 4:6, 0:HT], vecs[0:96, V_BIAS:V_BIAS + 1],
                                      vecs[0:96, V_SIGN:V_SIGN + 1], ALU.add, ALU.mult).then_inc(small_dve, 1)
                    dve.wait_ge(small_dve, 2)
                    dve.scalar_tensor_tensor(out=wl[:, :], in0=wz[:, :], scalar=-1.0, in1=wz[:, :],
                                             op0=ALU.mult, op1=ALU.min).then_inc(small_dve, 1)
                    with dve.Fori(0, FIRST // 2) as i:
                        for u in range(2):
                            split_low(dve, i * 2 + (n0 + 2 + u), u, KD)
                    dve.wait_ge(small_act, 5)
                    dve.scalar_tensor_tensor(out=wsum[:, :], in0=wz[:, :], scalar=0.0, in1=wl[:, :],
                                             op0=ALU.max, op1=ALU.add).then_inc(small_dve, 1)
                    dve.tensor_scalar(wb[64:96, :], wb[64:96, :], 1.0, None, ALU.add).then_inc(small_dve, 1)
                    dve.wait_ge(small_dve, 4)
                    dve.tensor_scalar(rows[0:64, :], wsum[0:64, :], coef[0:64, 0:1], -1.0, ALU.mult,
                                      ALU.mult).then_inc(small_dve, 1)
                    dve.wait_ge(small_dve, 5)
                    dve.reciprocal(rows[64:96, :], wb[64:96, :]).then_inc(small_dve, 1)
                    dve.wait_ge(small_dve, 7)
                    dve.tensor_tensor_scan(cum[:, :], starts[:, :], rows[:, 0:SEQ], 0.0, ALU.mult,
                                           ALU.add).then_inc(small_dve, 1)

                    def queries(r):
                        dve.wait_ge(qbd_done, 8 * r + 1)
                        if r:
                            dve.wait_ge(kv_used, PAGES)
                        for c in range(4):
                            for u in range(2):
                                dve.tensor_copy(qbd[64 * u:64 * u + 64, c, :, 2 * c + u],
                                                proj[64 * u:64 * u + 64, Q0 + c, SEQ + J * r:SEQ + J * r + J]
                                                ).then_inc(qbd_done, 1)

                    def forgets(r):
                        v = 8 * r
                        dve.wait_ge(pre_pe, 2 * r + 1)
                        dve.tensor_copy(st[:, r, SN:SN + 1], psum[:, 7, 0:1]).then_inc(sdve, 1)
                        if r:
                            dve.wait_ge(kv_used, 2 * PAGES)
                        dve.tensor_copy(sc[:, 0:1], psum[:, 7, 1:2]).then_inc(sdve, 1)
                        dve.wait_ge(lf_loaded, 16 * PAGES * (r + 1))
                        dve.wait_ge(sdve, v + 2)
                        dve.tensor_tensor_scan(sc[:, 0:PAGES * P], ones[:, 0:1].broadcast_to([P, PAGES * P]),
                                               sc[:, 0:PAGES * P], 0.0, ALU.mult, ALU.add).then_inc(sdve, 1)
                        dve.wait_ge(sdve, v + 3)

                    def take_scores(r, g, u):
                        dve.wait_ge(kv_used, g * 4 + (2 * PAGES * r + 4))
                        dve.scalar_tensor_tensor(out=sc[:, ds(g * 512, 512)], in0=psum[:, 4 + u, :],
                                                 scalar=DH ** -0.5, in1=sc[:, ds(g * 512, 512)],
                                                 op0=ALU.mult, op1=ALU.add).then_inc(sc_dve, 1)
                        dve.wait_ge(sc_dve, g + (NG * r + 1))
                        dve.tensor_reduce(st[:, r, ds(g + MX)], sc[:, ds(g * 512, 512)], AX.X,
                                          ALU.max).then_inc(nbias, 1)

                    def peak_scores(r):
                        nb = (NG + 2) * r + NG
                        dve.wait_ge(nbias, nb)
                        dve.tensor_reduce(st[:, r, NM:NM + 1], st[:, r, MX:MX + NG], AX.X, ALU.max).then_inc(nbias, 1)
                        dve.tensor_scalar(st[:, r, SN:SN + 1], st[:, r, SN:SN + 1], DH ** -0.5, None,
                                          ALU.mult).then_inc(sdve, 1)
                        dve.wait_ge(nbias, nb + 1)
                        dve.wait_ge(sdve, 8 * r + 4)
                        dve.tensor_scalar(st[:, r, NM:NM + 1], st[:, r, NM:NM + 1], st[:, r, SN:SN + 1], -1.0,
                                          ALU.max, ALU.mult).then_inc(nbias, 1)
                        if r:
                            dve.wait_ge(pre_pe, 2 * r)
                        for c in range(4):
                            ins = dve.tensor_copy(vb[:, c, :, :], proj[:, V0 + c, SEQ + J * r:SEQ + J * r + J]
                                                  .rearrange("p (j o) -> p j o", o=1).broadcast_to([P, J, 32]))
                        ins.then_inc(sdve, 1)

                    def probs_sum(r):
                        dve.wait_ge(p_exp, (NG + 1) * (r + 1))
                        dve.tensor_reduce(st[:, r, RI:RI + 1], st[:, r, RS:RS + NG], AX.X, ALU.add).then_inc(sdve, 1)
                        dve.wait_ge(sdve, 8 * r + 6)
                        dve.tensor_tensor(st[:, r, RI:RI + 1], st[:, r, RI:RI + 1], st[:, r, PN:PN + 1],
                                          ALU.add).then_inc(sdve, 1)
                        dve.wait_ge(sdve, 8 * r + 7)
                        dve.reciprocal(st[:, r, RI:RI + 1], st[:, r, RI:RI + 1]).then_inc(sdve, 1)
                        dve.wait_ge(sdve, 8 * r + 8)

                    def masked(r):
                        dve.wait_ge(mask_loaded, 16)
                        dve.wait_ge(pre_pe, 2 * r + 2)
                        if r:
                            dve.wait_ge(so_pe, r)
                        dve.tensor_scalar(om[:, :], psum[:, 7, :], st[:, r, PN:PN + 1], None,
                                          ALU.mult).then_inc(om_done, 1)
                        dve.wait_ge(om_done, 3 * r + 1)
                        dve.tensor_tensor(om[:, :], om[:, :], psum[:, 6, :], ALU.add).then_inc(om_done, 1)
                        dve.wait_ge(om_done, 3 * r + 2)
                        dve.scalar_tensor_tensor(out=om[:, :], in0=om[:, :], scalar=st[:, r, RI:RI + 1], in1=hmask[:, :],
                                                 op0=ALU.mult, op1=ALU.mult).then_inc(om_done, 1)

                    def sample_out(r):
                        dve.wait_ge(so_pe, r + 1)
                        dve.tensor_copy(so[:, :, J * r:J * r + J], psum[:, 7, 0:16].rearrange("p (c j) -> p c j", c=4)
                                        ).then_inc(so_copy, 1)
                    queries(0)
                    split_low(dve, n0 + FIRST + 2, 0, KD)
                    forgets(0)
                    split_low(dve, n0 + FIRST + 3, 1, KD)
                    for g in range(2):
                        if g:
                            for u in range(2):
                                split_low(dve, n0 + FIRST + 2 + 2 * g + u, u, KD)
                        take_scores(0, g, g)
                    with dve.Fori(1, NG // 2) as i:
                        for b in range(2):
                            for u in range(2):
                                split_low(dve, i * 4 + (n0 + FIRST + 2 + 2 * b + u), u, KD)
                            take_scores(0, i * 2 + b, b)
                    peak_scores(0)
                    queries(1)
                    with dve.Fori((FIRST + 2 * NG) // 2, NB // 2 - 1) as i:
                        for u in range(2):
                            split_low(dve, i * 2 + (n0 + 2 + u), u, KD)
                    probs_sum(0)
                    masked(0)

                    for b in range(NQ):
                        dve.wait_ge(vt_pe, b + 1)
                        dve.tensor_copy(vtok[:, b, :], psum[:, b, :]).then_inc(vt_copy, 1)
                    sample_out(0)

                    def peak(t):
                        S = (tiles[t][1] + 1) * P
                        dve.wait_ge(fs_pe, t + 1)
                        dve.tensor_reduce(stat[:, t, 0:1], psum[:, t % 2, 0:S], AX.X, ALU.max).then_inc(f_neg, 1)
                        dve.wait_ge(f_neg, 2 * t + 1)
                        dve.tensor_scalar(stat[:, t, 0:1], stat[:, t, 0:1], -DH ** -0.5, None,
                                          ALU.mult).then_inc(f_neg, 1)

                    def norm(t):
                        S = (tiles[t][1] + 1) * P
                        dve.wait_ge(f_exp, t + 1)
                        dve.reciprocal(stat[:, t, 2:3], stat[:, t, 1:2]).then_inc(f_dve, 1)
                        dve.wait_ge(f_dve, 2 * t + 1)
                        dve.tensor_scalar(prb[:, t % 2, 0:S], prb[:, t % 2, 0:S], stat[:, t, 2:3], None,
                                          ALU.mult).then_inc(f_dve, 1)

                    def low(c):
                        dve.wait_ge(fo_high, c + 1)
                        dve.tensor_tensor(fox_low[:, c, 0:SEQ], psum[:, 3, :], fox_high[:, c, 0:SEQ].bitcast(F32),
                                          ALU.subtract).then_inc(fo_low, 1)

                    def conv_new():
                        wv = vecs[:, V_CONV:V_CONV + 48].rearrange("p (n i) -> p n i", i=4)
                        dve.wait_ge(conv_in, 16)
                        dve.tensor_tensor(cnew[:, :, :], proj[:, CV0:Z0, SEQ:T], wv[:, :, 3:4].broadcast_to([P, 12, NS]),
                                          ALU.mult).then_inc(cs, 1)
                        for i in range(3):
                            dve.wait_ge(cs, 2 * i + 1)
                            dve.tensor_tensor(tap[:, :, :], buf[:, :, i, :], wv[:, :, i:i + 1].broadcast_to([P, 12, NS]),
                                              ALU.mult).then_inc(cs, 1)
                            dve.wait_ge(cs, 2 * i + 2)
                            dve.tensor_tensor(cnew[:, :, :], cnew[:, :, :], tap[:, :, :], ALU.add).then_inc(cs, 1)
                        dve.wait_ge(stored, 48)

                    def conv_step(k):
                        n, d = 11 - k // 4, k % 4
                        src, dst = proj[:, CV0 + n, :], proj[:, CV0 + 1 + n, :]
                        w = vecs[:, V_CONV + 4 * n + 3 - d:V_CONV + 4 * n + 4 - d]
                        dve.wait_ge(cs, 7 + k)
                        if d == 0:
                            dve.tensor_scalar(dst[:, 0:SEQ], src[:, 0:SEQ], w, None, ALU.mult).then_inc(cs, 1)
                        else:
                            dve.scalar_tensor_tensor(out=dst[:, d:SEQ], in0=src[:, 0:SEQ - d], scalar=w,
                                                     in1=dst[:, d:SEQ], op0=ALU.mult, op1=ALU.add).then_inc(cs, 1)
                    for t in range(N + 2):
                        if t < N:
                            peak(t)
                        if 1 <= t <= N:
                            norm(t - 1)
                        if t % 8 == 1 and t > 8:
                            low(t // 8 - 1)
                        if t == 1:
                            forgets(1)
                        if t % 2 == 1 and t < 2 * NG:
                            take_scores(1, t // 2, t // 2 % 2)
                        if t == 2 * NG - 1:
                            peak_scores(1)
                        if t == 4:
                            conv_new()
                        for k in range(2 * (t - 5), 2 * (t - 4)):
                            if 0 <= k < 48:
                                conv_step(k)
                    dve.wait_ge(cs, 7 + 48)
                    dve.tensor_copy(proj[:, CV0 + 1:Z0 + 1, SEQ:T], cnew[:, :, :]).then_inc(cs, 1)
                    probs_sum(1)
                    masked(1)
                    sample_out(1)
                    dve.wait_ge(so_copy, R + 1)
                    dve.tensor_tensor(fox_low[:, :, SEQ:T], so[:, :, :], fox_high[:, :, SEQ:T].bitcast(F32),
                                      ALU.subtract).then_inc(so_copy, 1)

                @block.tensor
                def _(pe):
                    norm_pe(pe, norm_n)
                    pe.wait_ge(h_low_done, m0 + KD)
                    pe.wait_ge(small_dve, 1)
                    for h in range(2):
                        tok = slice(h * HT, (h + 1) * HT)
                        for k in range(KD):
                            out = psum[0:96, 4 + h, 0:HT]
                            pe.matmul(out, w16_high[:, k, :], h_high[:, k, tok], start=(k == 0), stop=False)
                            pe.matmul(out, w16_high[:, k, :], h_low[:, k, tok], start=False, stop=False)
                            mm = pe.matmul(out, w16_low[:, k, :], h_high[:, k, tok], start=False, stop=(k == KD - 1))
                    mm.then_inc(small_pe, 1)

                    def products(n, u):
                        if not isinstance(n, int) or n >= 2:
                            pe.wait_ge(lin_out, n - 1)
                        block_products(pe, n + n0, u, range(KD), u, h_high, h_low, 0, True, True)
                    products(0, 0)
                    products(1, 1)
                    with pe.Fori(1, FIRST // 2) as i:
                        for u in range(2):
                            products(i * 2 + u, u)

                    def new_token(r):
                        pe.wait_ge(qbd_done, 8 * r + 9)
                        if r:
                            pe.wait_ge(so_copy, r)
                        else:
                            pe.wait_ge(small_dve, 8)
                        for c in range(4):
                            for j in range(J):
                                pe.matmul(psum[32 * j:32 * j + 32, 7, 0:1], qbd[:, c, j, :],
                                          proj[:, K0 + c, SEQ + J * r + j:SEQ + J * r + j + 1], start=(c == 0),
                                          stop=(c == 3))
                        for j in range(J):
                            mm = pe.matmul(psum[32 * j:32 * j + 32, 7, 1:2], ident[0:8, 0:32],
                                           rows[0:8, SEQ + J * r + j:SEQ + J * r + j + 1], start=True, stop=True)
                        mm.then_inc(pre_pe, 1)

                    def key_step(r, g, u, first):
                        if u == 0 and not first:
                            pe.wait_ge(sc_dve, g + (NG * r - 1))
                        pe.wait_ge(kv_loaded[u], g * 64 + (128 * PAGES // 4 * r + 64))
                        b = key_bank[0]
                        for c in range(4):
                            for j in range(J):
                                mm = pe.matmul(psum[32 * j:32 * j + 32, b, u * P:(u + 1) * P], qbd[:, c, j, :],
                                               ring[:, u, j, c * P:(c + 1) * P], start=(c == 0), stop=(c == 3))
                        mm.then_inc(kv_used, 1)
                    key_bank = [4]

                    def turn(r, g):
                        pe.wait_ge(p_exp, (NG + 1) * r + g + 1 + (r if g else 0))
                        if g >= 2:
                            pe.wait_ge(pt_act, NG * r + g - 1)
                        for u in range(4):
                            mm = pe.transpose(psum[:, 4 + g % 2, u * P:(u + 1) * P],
                                              sc[:, g * 512 + u * P:g * 512 + (u + 1) * P], ident[:, :])
                        mm.then_inc(pt_pe, 1)

                    def value_step(r, t):
                        s = (2 * r + 1) * PAGES + t
                        if t % 4 == 0:
                            pe.wait_ge(pt_act, NG * r + t // 4 + 1)
                        pe.wait_ge(kv_loaded[t % 4], 64 * (s // 4 + 1))
                        for j in range(J):
                            mm = pe.matmul(psum[32 * j:32 * j + 32, 6, :], sc[:, t * P + 32 * j:t * P + 32 * j + 32],
                                           ring[:, t % 4, j, :], start=(t == 0), stop=(t == PAGES - 1))
                        mm.then_inc(kv_used, 1)

                    def new_values(r):
                        pe.wait_ge(sdve, 8 * r + 5)
                        if r:
                            pe.wait_ge(so_copy, r)
                        for c in range(4):
                            mm = pe.matmul(psum[:, 7, c * P:(c + 1) * P],
                                           vb[:, c, :, :].rearrange("p j o -> p (j o)"), ident[:, :],
                                           start=True, stop=True)
                        mm.then_inc(pre_pe, 1)

                    def out_columns(r):
                        pe.wait_ge(om_done, 3 * (r + 1))
                        for c in range(4):
                            mm = pe.matmul(psum[:, 7, 4 * c:4 * c + 4], om[:, c * P:(c + 1) * P], gsel[:, :],
                                           start=True, stop=True)
                        mm.then_inc(so_pe, 1)

                    def key_slots(i, first):
                        for b in range(2):
                            for half in range(2):
                                products(i * 4 + (FIRST + 2 * b + half), half)
                                if first and b == 0 and half == 0:
                                    new_token(0)
                                key_bank[0] = 4 + b
                                key_step(0, i * 2 + b, 2 * half, first)
                                key_step(0, i * 2 + b, 2 * half + 1, first)
                    key_slots(0, True)
                    with pe.Fori(1, NG // 2) as i:
                        key_slots(i, False)
                    pe.wait_ge(gsel_loaded, 16)
                    for g in range(NG):
                        products(NPROJ + 2 * g, 0)
                        turn(0, g)
                        if g:
                            value_step(0, 4 * g - 2)
                            value_step(0, 4 * g - 1)
                        products(NPROJ + 2 * g + 1, 1)
                        value_step(0, 4 * g)
                        value_step(0, 4 * g + 1)
                    value_step(0, PAGES - 2)
                    value_step(0, PAGES - 1)
                    new_values(0)
                    pe.wait_ge(lin_out, NB)
                    for b in range(NQ):
                        for c in range(4):
                            mm = pe.transpose(psum[:, b, c * P:(c + 1) * P],
                                              proj[:, V0 + c, b * P:(b + 1) * P], ident[:, :])
                        mm.then_inc(vt_pe, 1)
                    out_columns(0)
                    pe.wait_ge(fin, 32)
                    pe.wait_ge(vt_copy, NQ)

                    def scores(t):
                        h, i = tiles[t]
                        c, lo = h // 2, 64 * (h % 2)
                        S = (i + 1) * P
                        if t >= 2:
                            pe.wait_ge(f_exp, t - 1)
                        bank = psum[:, t % 2, :]
                        pe.matmul(bank[:, 0:S], proj[lo:lo + 64, Q0 + c, i * P:(i + 1) * P],
                                  proj[lo:lo + 64, K0 + c, 0:S], start=True, stop=False)
                        pe.matmul(bank[:, 0:S], sel[:, h, :], cum[0:8, 0:S], start=False, stop=False)
                        pe.matmul(bank[:, S - P:S], ident[:, :], causal[:, :], start=False,
                                  stop=True).then_inc(fs_pe, 1)

                    def probs_turned(t):
                        h, i = tiles[t]
                        pe.wait_ge(f_dve, 2 * t + 2)
                        if t >= 1:
                            pe.wait_ge(ft_copy, t)
                        for j in range(i + 1):
                            mm = pe.transpose(psum[:, 2, j * P:(j + 1) * P], prb[:, t % 2, j * P:(j + 1) * P],
                                              ident[:, :])
                        mm.then_inc(ft_pe, 1)

                    def values(t):
                        h, i = tiles[t]
                        lo = 64 * (h % 2)
                        pe.wait_ge(ft_copy, t + 1)
                        if t % 8 == 0 and t:
                            pe.wait_ge(fo_low, t // 8)
                        for j in range(i + 1):
                            mm = pe.matmul(psum[lo:lo + 64, 3, i * P:(i + 1) * P],
                                           vtok[:, j, h * DH:(h + 1) * DH], prt[:, t % 2, j * P:(j + 1) * P],
                                           start=(j == 0), stop=(j == i))
                        mm.then_inc(fo_pe, 1)

                    def stream(t, half):
                        if t < 2 * NG:
                            key_bank[0] = 4 + t // 2 % 2
                            key_step(1, t // 2, 2 * (t % 2) + half, False)
                        elif t >= VT:
                            g, odd = divmod(t - VT, 2)
                            if not odd and half == 0 and g < NG:
                                turn(1, g)
                            s = 2 * (t - VT) - 2 + half
                            if 0 <= s < PAGES:
                                value_step(1, s)
                    for t in range(N + 2):
                        if t < N:
                            scores(t)
                        if t == 1:
                            new_token(1)
                        stream(t, 0)
                        if 1 <= t <= N:
                            probs_turned(t - 1)
                        stream(t, 1)
                        if t >= 2:
                            values(t - 2)
                    new_values(1)
                    out_columns(1)
            count["block"] += NB
            norms[0] += 1
            hcount[0] += KD

        def gdn(proj, rows, cum, gdn_o):
            NP = SEQ // P
            with ExitStack() as outer:
                cv = proj[:, CV0 + 1:Z0 + 1, :]
                gdn_high, gdn_low = gdn_o
                o = sb("gdn_o", [P, GH, T], F32, outer)
                selc = sb("gdn_sel", [68, GH, P], F32, outer)
                gin = sem("gdn_constants_loaded")

                silu_done = sem("conv_silu_done")
                l_sq = sem("length_squares")
                l_sum = sem("length_sums")
                l_root = sem("length_roots")
                l_dve = sem("length_steps")
                with ExitStack() as scope:
                    block = scope.enter_context(nc.Block())

                    @block.sync
                    def _(sp):
                        sp.dma_start(selc[:, :, :].rearrange("p h k -> p (h k)"), a["sel"][0:68, 0:GH * P]).then_inc(gin, 16)
                        sp.wait_ge(gin, 16)

                    @block.vector
                    def _(dve):
                        for n in range(8):
                            dve.wait_ge(l_root, n + 1)
                            if n:
                                dve.wait_ge(l_dve, 2 * n)
                            dve.reciprocal(factor[:, :], root[:, :]).then_inc(l_dve, 1)
                            dve.wait_ge(l_dve, 2 * n + 1)
                            dve.scalar_tensor_tensor(out=cv[:, n, :], in0=cv[:, n, :], scalar=P ** -0.5 if n < 4 else 1.0,
                                                     in1=factor[:, :], op0=ALU.mult, op1=ALU.mult).then_inc(l_dve, 1)

                    def length(act, n):
                        act.wait_ge(l_sum, n + 1)
                        if n >= 1:
                            act.wait_ge(l_dve, 2 * n - 1)
                        act.activation(halves(root[:, :]), pair(n % 2), ACT.Sqrt, bias=eps_col[:, 0:1]).then_inc(l_root, 1)

                    @block.scalar
                    def _(act):
                        for n in range(12):
                            act.activation(cv[:, n, :], cv[:, n, :], ACT.Silu).then_inc(silu_done, 1)
                        for n in range(8):
                            act.wait_ge(silu_done, n + 1)
                            if n >= 2:
                                act.wait_ge(l_sum, n - 1)
                            act.activation(sq[:, n % 2, :], cv[:, n, :], ACT.Square).then_inc(l_sq, 1)
                            if n >= 1:
                                length(act, n - 1)
                        length(act, 7)

                    @block.tensor
                    def _(pe):
                        for n in range(8):
                            pe.wait_ge(l_sq, n + 1)
                            if n >= 2:
                                pe.wait_ge(l_root, n - 1)
                            for h in range(2):
                                mm = pe.matmul(psum[:, 2 * (n % 2) + h, 0:HT], ones[:, :],
                                               sq[:, n % 2, h * HT:(h + 1) * HT], start=True, stop=True)
                            mm.then_inc(l_sum, 1)

                NI = GH * NS
                s_state = sem("state_loaded")
                g_dve = sem("step_vector")
                g_pe = sem("step_products")
                g_act = sem("step_scalar")
                s_stored = sem("state_stored")
                with ExitStack() as scope:
                    s0 = sb("state", [P, NI, P], F32, scope)
                    kz = sb("key_rows", [NI, NI, P], F32, scope)
                    kq = sb("key_query", [P, NI, 2], F32, scope)
                    sm = sb("step_small", [P, 8, NI], F32, scope)
                    rw = sb("step_rows", [NI, 2, P], F32, scope)
                    EGS, BBS, KK, KC, DL, T1, T2 = range(7)
                    block = scope.enter_context(nc.Block())

                    def by_head(t):
                        return t.rearrange("p (h b) -> p h b", h=GH)

                    @block.sync
                    def _(sp):
                        sp.dma_start(s0[:, :, :], a["state_in"]).then_inc(s_state, 16)
                        for g in range(8):
                            sp.wait_ge(g_dve, 15 + g)
                            sp.dma_start(a["o_state_s"][:, 4 * g:4 * g + 4, :], s0[:, 4 * g:4 * g + 4, :]).then_inc(s_stored, 16)
                        sp.wait_ge(s_stored, 16 * 8)

                    @block.scalar
                    def _(act):
                        act.wait_ge(g_pe, 1)
                        act.activation(sm[:, EGS, :], psum[:, 0, 0:NI], ACT.Exp).then_inc(g_act, 1)

                    @block.vector
                    def _(dve):
                        new = slice(SEQ, T)
                        dve.tensor_copy(kq[:, :, 0:1].rearrange("p (h b) o -> p h (b o)", h=GH), cv[:, 4:8, new]).then_inc(g_dve, 1)
                        dve.tensor_copy(kq[:, :, 1:2].rearrange("p (h b) o -> p h (b o)", h=GH), cv[:, 0:4, new]).then_inc(g_dve, 1)
                        dve.tensor_copy(by_head(sm[:, KC, :]), cv[:, 4:8, new]).then_inc(g_dve, 1)
                        dve.tensor_tensor(by_head(sm[:, KK, :]), cv[:, 4:8, new], cv[:, 0:4, new], ALU.mult).then_inc(g_dve, 1)
                        dve.wait_ge(g_pe, 2)
                        dve.wait_ge(g_act, 1)
                        ks = psum[:, 2, 0:2 * NI].rearrange("p (i o) -> p i o", o=2)
                        dve.tensor_tensor(sm[:, T1, :], ks[:, :, 0], sm[:, EGS, :], ALU.mult).then_inc(g_dve, 1)
                        dve.tensor_tensor(sm[:, T2, :], ks[:, :, 1], sm[:, EGS, :], ALU.mult).then_inc(g_dve, 1)
                        dve.wait_ge(g_dve, 5)
                        dve.tensor_tensor(by_head(sm[:, T1, :]), cv[:, 8:12, new], by_head(sm[:, T1, :]),
                                          ALU.subtract).then_inc(g_dve, 1)
                        dve.wait_ge(g_dve, 7)
                        dve.tensor_tensor(sm[:, DL, :], sm[:, T1, :], psum[:, 1, 0:NI], ALU.mult).then_inc(g_dve, 1)
                        dve.wait_ge(g_dve, 8)
                        dve.tensor_tensor(sm[:, T1, :], sm[:, DL, :], psum[:, 4, 0:NI], ALU.mult).then_inc(g_dve, 1)
                        dve.wait_ge(g_dve, 9)
                        dve.tensor_tensor(o[:, :, new], by_head(sm[:, T1, :]), by_head(sm[:, T2, :]), ALU.add).then_inc(g_dve, 1)
                        dve.wait_ge(g_pe, 3)
                        dve.tensor_copy(rw[:, 0, :], psum[0:NI, 3, 0:P]).then_inc(g_dve, 1)
                        dve.tensor_copy(rw[:, 1, :], psum[0:NI, 3, P:2 * P]).then_inc(g_dve, 1)
                        dve.wait_ge(g_dve, 12)
                        dve.tensor_tensor(kz[:, :, :], rw[:, 1:2, :].broadcast_to([NI, NI, P]),
                                          ident[0:NI, 0:NI].rearrange("p (i o) -> p i o", o=1).broadcast_to([NI, NI, P]),
                                          ALU.mult).then_inc(g_dve, 1)
                        dve.tensor_tensor(s0[:, :, :], s0[:, :, :], sm[:, EGS, :].rearrange("p (i o) -> p i o", o=1)
                                          .broadcast_to([P, NI, P]), ALU.mult).then_inc(g_dve, 1)
                        dve.wait_ge(g_dve, 14)
                        for g in range(8):
                            dve.wait_ge(g_pe, 4 + g)
                            dve.tensor_tensor(s0[:, 4 * g:4 * g + 4, :], s0[:, 4 * g:4 * g + 4, :],
                                              psum[:, 4 + g % 2, :].rearrange("p (i k) -> p i k", i=4),
                                              ALU.add).then_inc(g_dve, 1)

                    @block.tensor
                    def _(pe):
                        for h in range(GH):
                            pe.matmul(psum[:, 0, NS * h:NS * h + NS], selc[32:36, h, :], rows[32:36, SEQ:T],
                                      start=True, stop=True)
                            pe.matmul(psum[:, 1, NS * h:NS * h + NS], selc[64:68, h, :], rows[64:68, SEQ:T],
                                      start=True, stop=True)
                        pe.wait_ge(g_dve, 4)
                        pe.matmul(psum[:, 4, 0:NI], ones[:, :], sm[:, KK, :], start=True,
                                  stop=True).then_inc(g_pe, 1)
                        pe.wait_ge(s_state, 16)
                        for i in range(NI):
                            mm = pe.matmul(psum[:, 2, 2 * i:2 * i + 2], s0[:, i, :], kq[:, i, :], start=True, stop=True)
                        mm.then_inc(g_pe, 1)
                        pe.wait_ge(g_dve, 8)
                        pe.transpose(psum[0:NI, 3, 0:P], sm[:, DL, :], ident[:, :])
                        pe.transpose(psum[0:NI, 3, P:2 * P], sm[:, KC, :], ident[:, :]).then_inc(g_pe, 1)
                        pe.wait_ge(g_dve, 13)
                        for i in range(NI):
                            g = i // 4
                            if i % 4 == 0 and g >= 2:
                                pe.wait_ge(g_dve, 13 + g)
                            mm = pe.matmul(psum[:, 4 + g % 2, (i % 4) * P:(i % 4 + 1) * P], kz[:, i, :], rw[:, 0, :],
                                           start=True, stop=True)
                            if i % 4 == 3:
                                mm.then_inc(g_pe, 1)

                at = over("attn_t", [P, GH, SEQ], F32, "proj")
                e_t = over("inverse_t", [P, GH, SEQ], F32, "proj", GH * SEQ)
                dm = over("inverse", [P, GH, SEQ], F32, "proj", 2 * GH * SEQ)
                eg = over("exp_g", [P, SEQ], F32, "root")
                el = over("exp_left", [P, SEQ], F32, "factor")
                lo_ = over("level_part", [P, 2, SEQ], F32, "h_f")
                p_in = sem("chunk_masks_loaded")
                p_bc = sem("prep_products")
                p_act = sem("prep_scalar")
                p_dve = sem("prep_vector")
                p_raw = sem("prep_pairs")
                p_last = sem("prep_last")
                p_neg = sem("prep_negated")
                p_turn = sem("prep_turned")
                p_tok = sem("prep_token_major")
                l_mask = sem("level_masked")
                l_pe = sem("level_products")
                l_act = sem("level_copied")
                l_upd = sem("level_updated")
                w_pe = sem("solved_products")
                w_act = sem("solved_copied")
                c_pe = sem("scan_products")
                c_dve = sem("scan_steps")
                c_out = sem("scan_out")
                c_copy = sem("scan_out_copied")
                g_store = sem("prompt_state_stored")
                with ExitStack() as scope:
                    vbt = sb("v_tok", [P, GH, SEQ], F32, scope)
                    kbt = sb("k_tok", [P, GH, SEQ], F32, scope)
                    kht = sb("k_left_tok", [P, GH, SEQ], F32, scope)
                    lt = sb("lower_t", [P, GH, SEQ], F32, scope)
                    tmp = sb("gdn_tmp", [P, 4, SEQ], F32, scope)
                    S = sb("gdn_state", [P, GH, P], F32, scope)
                    egl = sb("exp_g_last", [P, GH, NCH], F32, scope)
                    gl = sb("g_last", [P, NCH], F32, scope)
                    neg_cum = sb("neg_cum", [36, SEQ], F32, scope)
                    mask = sb("chunk_mask", [P, P], F32, scope)
                    lev = over("levels", [P, LEVELS, P], F32, "sq")
                    KB, KBE, KH, DT = range(4)
                    block = scope.enter_context(nc.Block())

                    def pr(t, p):
                        return t[:, p * P:(p + 1) * P]

                    def pairs(t):
                        return t.rearrange("p (n k) -> p n k", n=NP)

                    def over_pairs(t):
                        return t.rearrange("p (o k) -> p o k", o=1).broadcast_to([P, NP, P])

                    @block.sync
                    def _(sp):
                        sp.dma_start(mask[:, :], a["chunk_mask"]).then_inc(p_in, 16)
                        sp.dma_start(lev[:, :, :].rearrange("p l k -> p (l k)"), a["levels"]).then_inc(p_in, 16)
                        sp.wait_ge(c_dve, 2 * NCH + 1)
                        sp.dma_start(a["o_state"], S[:, :, :]).then_inc(g_store, 16)
                        sp.wait_ge(g_store, 16)

                    @block.tensor
                    def _(pe):
                        pe.wait_ge(p_in, 32)
                        pe.wait_ge(p_neg, 1)
                        for h in range(GH):
                            if h:
                                pe.wait_ge(p_dve, 9 * h)
                            g_h, b_h = selc[32:36, h, :], selc[64:68, h, :]
                            pe.matmul(psum[:, 0, :], g_h, cum[32:36, :], start=True, stop=True)
                            pe.matmul(psum[:, 1, :], b_h, rows[64:68, 0:SEQ], start=True, stop=True)
                            pe.matmul(psum[:, 2, :], g_h, cum[32:36, :], start=True, stop=False)
                            for p in range(NP):
                                pe.matmul(pr(psum[:, 2, :], p), neg_cum[32:36, p * P:(p + 1) * P], g_h,
                                          start=False, stop=False)
                                mm = pe.matmul(pr(psum[:, 2, :], p), ident[:, :], mask[:, :], start=False,
                                               stop=(p == NP - 1))
                            mm.then_inc(p_bc, 1)
                            pe.wait_ge(p_dve, 9 * h + 3)
                            k = cv[:, 4 + h, 0:SEQ]
                            for p in range(NP):
                                pe.matmul(pr(psum[:, 3, :], p), pr(k, p), pr(tmp[:, KB, :], p), start=True, stop=True)
                            for p in range(NP):
                                mm = pe.matmul(pr(psum[:, 4, :], p), pr(k, p), pr(cv[:, h, 0:SEQ], p), start=True, stop=True)
                            mm.then_inc(p_raw, 1)
                            pe.wait_ge(p_dve, 9 * h + 6)
                            if h:
                                pe.wait_ge(p_tok, 3 * h)
                            for n, src in enumerate((cv[:, 8 + h, 0:SEQ], tmp[:, KBE, :], tmp[:, KH, :])):
                                for p in range(NP):
                                    mm = pe.transpose(pr(psum[:, 5 + n, :], p), pr(src, p), ident[:, :])
                            mm.then_inc(p_turn, 1)
                        for h in range(GH):
                            pe.wait_ge(l_upd, h + 1)
                            for p in range(NP):
                                mm = pe.transpose(pr(psum[:, h, :], p), pr(e_t[:, h, :], p), ident[:, :])
                            mm.then_inc(l_pe, 1)
                        for lv in range(1, LEVELS):
                            n = (lv - 1) * GH
                            for h in range(GH):
                                pe.wait_ge(l_mask, n + h + 1)
                                pe.wait_ge(l_act, GH + n)
                                if lv > 1:
                                    pe.wait_ge(l_upd, GH + 2 * (n - GH) + 2 * h + 2)
                                for p in range(NP):
                                    mm = pe.matmul(pr(psum[:, h, :], p), pr(lo_[:, h % 2, :], p), pr(dm[:, h, :], p),
                                                   start=True, stop=True)
                                mm.then_inc(l_pe, 1)
                            for h in range(GH):
                                pe.wait_ge(l_act, GH + n + h + 1)
                                if h >= 2:
                                    pe.wait_ge(l_upd, GH + 2 * n + 2 * (h - 2) + 2)
                                b = 4 + 2 * (h % 2)
                                for p in range(NP):
                                    pe.matmul(pr(psum[:, b, :], p), pr(e_t[:, h, :], p), pr(tmp[:, h, :], p),
                                              start=True, stop=True)
                                for p in range(NP):
                                    mm = pe.matmul(pr(psum[:, b + 1, :], p), pr(tmp[:, h, :], p), pr(e_t[:, h, :], p),
                                                   start=True, stop=True)
                                mm.then_inc(w_pe, 1)
                        nu = GH * (LEVELS - 1)
                        for h in range(GH):
                            pe.wait_ge(l_upd, GH + 2 * (nu - GH) + 2 * h + 2)
                            if h >= 2:
                                pe.wait_ge(w_act, 2 * (h - 2) + 2)
                            b = 2 * (h % 2)
                            for p in range(NP):
                                pe.matmul(pr(psum[:, b, :], p), pr(e_t[:, h, :], p), pr(vbt[:, h, :], p), start=True, stop=True)
                            for p in range(NP):
                                mm = pe.matmul(pr(psum[:, b + 1, :], p), pr(kbt[:, h, :], p), pr(e_t[:, h, :], p),
                                               start=True, stop=True)
                            mm.then_inc(w_pe, 1)
                        pe.wait_ge(w_act, 2 * GH)
                        for n in range(NCH):
                            p, r = n // 2, C * (n % 2)
                            tok = slice(n * C, (n + 1) * C)
                            pe.wait_ge(c_dve, 2 * n + 1)
                            for h in range(GH):
                                mm = pe.matmul(psum[r:r + C, 4, h * P:(h + 1) * P], dm[:, h, tok], S[:, h, :],
                                               start=True, stop=True)
                            mm.then_inc(c_pe, 1)
                            if n % 2 == 0 and p >= 2:
                                pe.wait_ge(c_copy, p - 1)
                            for h in range(GH):
                                pe.matmul(psum[:, 6 + p % 2, h * P + r:h * P + r + C], S[:, h, :], cv[:, h, tok],
                                          start=(n % 2 == 0 and h == 0), stop=False, skip_group_check=True)
                            pe.wait_ge(c_dve, 2 * n + 2)
                            for h in range(GH):
                                mm = pe.matmul(psum[:, 5, h * P:(h + 1) * P], kht[r:r + C, h, p * P:(p + 1) * P],
                                               vbt[r:r + C, h, p * P:(p + 1) * P], start=True, stop=True)
                            mm.then_inc(c_pe, 1)
                            if n % 2:
                                for h in range(GH):
                                    mm = pe.matmul(psum[:, 6 + p % 2, h * P:(h + 1) * P], vbt[:, h, p * P:(p + 1) * P],
                                                   at[:, h, p * P:(p + 1) * P], start=False, stop=(h == GH - 1),
                                                   skip_group_check=True)
                                mm.then_inc(c_out, 1)

                    @block.gpsimd
                    def _(pool):
                        pool.wait_ge(p_in, 32)
                        for lv in range(1, LEVELS):
                            n = (lv - 1) * GH
                            for h in range(GH):
                                if n + h >= 2:
                                    m = n + h - 2
                                    pool.wait_ge(l_pe, GH + m + 1)
                                    pool.wait_ge(l_mask, m + 1)
                                else:
                                    pool.wait_ge(l_upd, GH)
                                pool.tensor_tensor(pairs(lo_[:, h % 2, :]), pairs(lt[:, h, :]), over_pairs(lev[:, lv, :]),
                                                   ALU.mult).then_inc(l_mask, 1)

                    @block.scalar
                    def _(act):
                        for h in range(GH):
                            act.wait_ge(p_bc, h + 1)
                            if h:
                                act.wait_ge(p_dve, 9 * h)
                            act.activation(eg[:, :], psum[:, 0, :], ACT.Exp).then_inc(p_act, 1)
                            act.activation(tmp[:, DT, :], psum[:, 2, :], ACT.Exp).then_inc(p_act, 1)
                            act.wait_ge(p_dve, 9 * h + 1)
                            act.activation(el[:, :], el[:, :], ACT.Exp).then_inc(p_act, 1)
                            act.wait_ge(p_turn, h + 1)
                            for n, t in enumerate((vbt, kbt, kht)):
                                act.activation(t[:, h, :], psum[:, 5 + n, :], ACT.Copy).then_inc(p_tok, 1)
                        for h in range(GH):
                            act.wait_ge(l_pe, h + 1)
                            act.activation(dm[:, h, :], psum[:, h, :], ACT.Copy).then_inc(l_act, 1)
                        for lv in range(1, LEVELS):
                            n = (lv - 1) * GH
                            for h in range(GH):
                                act.wait_ge(l_pe, GH + n + h + 1)
                                if lv > 1:
                                    act.wait_ge(w_pe, n - GH + h + 1)
                                act.activation(tmp[:, h, :], psum[:, h, :], ACT.Copy).then_inc(l_act, 1)
                        for h in range(GH):
                            act.wait_ge(w_pe, GH * (LEVELS - 1) + h + 1)
                            b = 2 * (h % 2)
                            act.activation(vbt[:, h, :], psum[:, b, :], ACT.Copy).then_inc(w_act, 1)
                            act.activation(dm[:, h, :], psum[:, b + 1, :], ACT.Copy).then_inc(w_act, 1)
                        for p in range(NP):
                            act.wait_ge(c_out, p + 1)
                            act.activation(o[:, :, p * P:(p + 1) * P], psum[:, 6 + p % 2, :].rearrange("p (h k) -> p h k", h=GH),
                                           ACT.Copy).then_inc(c_copy, 1)

                    @block.vector
                    def _(dve):
                        dve.tensor_scalar(neg_cum[32:36, :], cum[32:36, :], -1.0, None, ALU.mult).then_inc(p_neg, 1)
                        for h in range(GH):
                            k, q, v = cv[:, 4 + h, 0:SEQ], cv[:, h, 0:SEQ], cv[:, 8 + h, 0:SEQ]
                            dve.wait_ge(p_bc, h + 1)
                            if h:
                                dve.wait_ge(p_turn, h)
                                dve.wait_ge(p_dve, 9 * h)
                            gb = psum[:, 0, :].rearrange("p (n c) -> p n c", c=C)
                            dve.wait_ge(p_act, 3 * h + 1)
                            dve.tensor_copy(egl[:, h, :], eg[:, :].rearrange("p (n c) -> p n c", c=C)[:, :, C - 1]
                                            ).then_inc(p_last, 1)
                            dve.tensor_copy(gl[:, :], gb[:, :, C - 1]).then_inc(p_last, 1)
                            dve.wait_ge(p_last, 2 * h + 2)
                            dve.tensor_tensor(el[:, :].rearrange("p (n c) -> p n c", c=C),
                                              gl[:, :].rearrange("p (n o) -> p n o", o=1).broadcast_to([P, NCH, C]), gb,
                                              ALU.subtract).then_inc(p_dve, 1)
                            dve.tensor_tensor(v, v, psum[:, 1, :], ALU.mult).then_inc(p_dve, 1)
                            dve.tensor_tensor(tmp[:, KB, :], k, psum[:, 1, :], ALU.mult).then_inc(p_dve, 1)
                            dve.wait_ge(p_dve, 9 * h + 3)
                            dve.tensor_tensor(tmp[:, KBE, :], tmp[:, KB, :], eg[:, :], ALU.mult).then_inc(p_dve, 1)
                            dve.wait_ge(p_act, 3 * h + 3)
                            dve.tensor_tensor(tmp[:, KH, :], k, el[:, :], ALU.mult).then_inc(p_dve, 1)
                            dve.wait_ge(p_raw, h + 1)
                            dve.tensor_tensor(q, q, eg[:, :], ALU.mult).then_inc(p_dve, 1)
                            dve.tensor_tensor(lt[:, h, :], psum[:, 3, :], tmp[:, DT, :], ALU.mult).then_inc(p_dve, 1)
                            dve.tensor_tensor(at[:, h, :], psum[:, 4, :], tmp[:, DT, :], ALU.mult).then_inc(p_dve, 1)
                            dve.wait_ge(p_dve, 9 * h + 7)
                            dve.tensor_tensor(pairs(e_t[:, h, :]), pairs(lt[:, h, :]), over_pairs(lev[:, 0, :]),
                                              ALU.mult).then_inc(p_dve, 1)
                            dve.wait_ge(p_dve, 9 * h + 9)
                            dve.tensor_tensor(pairs(e_t[:, h, :]), over_pairs(ident[:, :]), pairs(e_t[:, h, :]),
                                              ALU.subtract).then_inc(l_upd, 1)
                        for lv in range(1, LEVELS):
                            n = (lv - 1) * GH
                            for h in range(GH):
                                dve.wait_ge(w_pe, n + h + 1)
                                b = 4 + 2 * (h % 2)
                                dve.tensor_tensor(dm[:, h, :], dm[:, h, :], psum[:, b, :], ALU.subtract).then_inc(l_upd, 1)
                                dve.tensor_tensor(e_t[:, h, :], e_t[:, h, :], psum[:, b + 1, :],
                                                  ALU.subtract).then_inc(l_upd, 1)
                        dve.memset(S[:, :, :], 0.0).then_inc(c_dve, 1)
                        dve.wait_ge(w_act, 2 * GH)
                        for n in range(NCH):
                            p, r = n // 2, C * (n % 2)
                            dve.wait_ge(c_pe, 2 * n + 1)
                            new = vbt[r:r + C, :, p * P:(p + 1) * P]
                            dve.tensor_tensor(new, new, psum[r:r + C, 4, :].rearrange("p (h k) -> p h k", h=GH),
                                              ALU.subtract).then_inc(c_dve, 1)
                            dve.wait_ge(c_pe, 2 * n + 2)
                            for h in range(GH):
                                ins = dve.scalar_tensor_tensor(out=S[:, h, :], in0=S[:, h, :], scalar=egl[:, h, n:n + 1],
                                                               in1=psum[:, 5, h * P:(h + 1) * P], op0=ALU.mult, op1=ALU.add)
                            ins.then_inc(c_dve, 1)

                z_in = sem("z_loaded")
                z_dve = sem("gated_steps")
                z_sq = sem("gated_squares")
                z_sum = sem("gated_sums")
                z_root = sem("gated_roots")
                z_high = sem("gated_high")
                with ExitStack() as scope:
                    zt = sb("silu_z", [P, GH, T], F32, scope)
                    block = scope.enter_context(nc.Block())

                    @block.sync
                    def _(sp):
                        sp.dma_start(zt[:, :, :], a["spill"][0:GH, :, :].rearrange("h p t -> p h t")).then_inc(z_in, 16)

                    @block.scalar
                    def _(act):
                        for h in range(GH):
                            if h >= 2:
                                act.wait_ge(z_sum, h - 1)
                            act.activation(sq[:, h % 2, :], o[:, h, :], ACT.Square).then_inc(z_sq, 1)
                        for h in range(GH):
                            act.wait_ge(z_sum, h + 1)
                            if h:
                                act.wait_ge(z_dve, 3 * (h - 1) + 1)
                            act.activation(halves(root[:, :]), pair(h % 2), ACT.Sqrt, bias=eps_col[:, 0:1],
                                           scale=1.0 / P).then_inc(z_root, 1)
                        for h in range(GH):
                            act.wait_ge(z_dve, 3 * h + 3)
                            act.activation(gdn_high[:, h, :], o[:, h, :], ACT.Copy).then_inc(z_high, 1)

                    @block.tensor
                    def _(pe):
                        for h in range(GH):
                            pe.wait_ge(z_sq, h + 1)
                            if h >= 2:
                                pe.wait_ge(z_root, h - 1)
                            for u in range(2):
                                mm = pe.matmul(psum[:, 2 * (h % 2) + u, 0:HT], ones[:, :], sq[:, h % 2, u * HT:(u + 1) * HT],
                                               start=True, stop=True)
                            mm.then_inc(z_sum, 1)

                    @block.vector
                    def _(dve):
                        dve.wait_ge(z_in, 16)
                        for h in range(GH):
                            dve.wait_ge(z_root, h + 1)
                            if h:
                                dve.wait_ge(z_dve, 3 * (h - 1) + 2)
                            dve.reciprocal(factor[:, :], root[:, :]).then_inc(z_dve, 1)
                            dve.wait_ge(z_dve, 3 * h + 1)
                            dve.scalar_tensor_tensor(out=o[:, h, :], in0=o[:, h, :], scalar=vecs[:, V_GDN:V_GDN + 1],
                                                     in1=factor[:, :], op0=ALU.mult, op1=ALU.mult).then_inc(z_dve, 1)
                            dve.wait_ge(z_dve, 3 * h + 2)
                            dve.tensor_tensor(o[:, h, :], o[:, h, :], zt[:, h, :], ALU.mult).then_inc(z_dve, 1)
                        for h in range(GH):
                            dve.wait_ge(z_high, h + 1)
                            dve.tensor_tensor(gdn_low[:, h, :], o[:, h, :], gdn_high[:, h, :].bitcast(F32),
                                              ALU.subtract).then_inc(z_dve, 1)

        def merge(fox_o, gdn_o):
            n0 = count["block"]
            nb = n0 + KD
            norm_n = norms[0]
            r0 = KD
            g_in = [sem("gates_loaded0"), sem("gates_loaded1")]
            fox_used = sem("fox_products")
            m_dve = sem("merge_steps")
            m_high = sem("merged_high")
            m_low = sem("merged_low")
            y_out = sem("mixed_copied")
            with ExitStack() as scope:
                gt = sb("gates", [P, 2, 2, T], F32, scope)
                mf = sb("merged", [P, 2, 2, T], F32, scope)
                mg_high = sb("merged_high", [P, KD, T], F32R, scope)
                mg_low = over("merged_low", [P, KD, T], F32R, "proj")
                y = over("mixed", [P, KD, T], F32, "proj", KD * T)
                block = scope.enter_context(nc.Block())

                @block.sync
                def _(sp):
                    for m in range(KD):
                        load_block(sp, a["w_merge"], m, n0 + m, m % 2, KD)
                        if m >= 2:
                            sp.wait_ge(m_dve, 3 * (m - 1))
                        for n in range(2):
                            sp.dma_start(gt[:, m % 2, n, :], a["spill"][4 + 8 * n + m, :, :]).then_inc(g_in[m % 2], 16)
                    load_stream(sp, a["w_out"], KD, nb, KD)

                @block.scalar
                def _(act):
                    split_high(act, n0, 0, KD)
                    split_high(act, n0 + 1, 1, KD)
                    for m in range(KD):
                        split_high(act, n0 + 2 + m, m % 2, KD)
                        act.wait_ge(m_dve, 3 * m + 3)
                        act.activation(mg_high[:, m, :], mf[:, m % 2, 0, :], ACT.Copy).then_inc(m_high, 1)
                    for m in range(KD):
                        if m < KD - 2:
                            split_high(act, nb + 2 + m, m % 2, KD)
                        act.wait_ge(block_used, nb + m + 1)
                        act.activation(halves(y[:, m, :]), pair(m % 2), ACT.Copy).then_inc(y_out, 1)
                    act.wait_ge(y_out, KD)
                    norm_act(act, y, norm_n)

                @block.vector
                def _(dve):
                    split_low(dve, n0, 0, KD)
                    split_low(dve, n0 + 1, 1, KD)
                    for m in range(KD):
                        split_low(dve, n0 + 2 + m, m % 2, KD)
                        dve.wait_ge(g_in[m % 2], 32 * (m // 2 + 1))
                        dve.wait_ge(fox_used, m + 1)
                        if m >= 2:
                            dve.wait_ge(m_low, m - 1)
                        dve.tensor_tensor(halves(mf[:, m % 2, 0, :]), halves(gt[:, m % 2, 0, :]), pair(0),
                                          ALU.mult).then_inc(m_dve, 1)
                        dve.wait_ge(block_used, n0 + m + 1)
                        dve.tensor_tensor(halves(mf[:, m % 2, 1, :]), halves(gt[:, m % 2, 1, :]), pair(1),
                                          ALU.mult).then_inc(m_dve, 1)
                        dve.wait_ge(m_dve, 3 * m + 2)
                        dve.tensor_tensor(mf[:, m % 2, 0, :], mf[:, m % 2, 0, :], mf[:, m % 2, 1, :],
                                          ALU.add).then_inc(m_dve, 1)
                        dve.wait_ge(m_high, m + 1)
                        dve.tensor_tensor(mg_low[:, m, :], mf[:, m % 2, 0, :], mg_high[:, m, :].bitcast(F32),
                                          ALU.subtract).then_inc(m_low, 1)
                    for m in range(KD - 2):
                        split_low(dve, nb + 2 + m, m % 2, KD)
                    norm_dve(dve, norm_n)
                    residual_dve(dve, y, V_POSTM, 1.0, norm_n, r0)

                @block.tensor
                def _(pe):
                    for m in range(KD):
                        if m:
                            pe.wait_ge(m_dve, 3 * (m - 1) + 2)
                        block_products(pe, n0 + m, m % 2, range(0, 4), 0, *fox_o, 0, True, True, fox_used)
                        block_products(pe, n0 + m, m % 2, range(4, 8), 1, *gdn_o, 0, True, True)
                    pe.wait_ge(m_low, KD)
                    for m in range(KD):
                        if m >= 2:
                            pe.wait_ge(y_out, m - 1)
                        block_products(pe, nb + m, m % 2, range(KD), m % 2, mg_high, mg_low, 0, True, True)
                    norm_pe(pe, norm_n)
            count["block"] = nb + KD
            norms[0] += 1

        count["groups"] = 0
        ffn(0, a["w_gu1"], a["w_dn1"], V_PRE1, V_POST1, False)
        mixer()
        ffn(1, a["w_gu2"], a["w_dn2"], V_PRE2, V_POST2, True)


_INS = ["x_prompt", "x_sample", "cache_k", "cache_v", "cache_logf", "state_gdn", "state_conv", "page_table",
        "ffn1_norm_pre", "ffn1_w_gate", "ffn1_w_up", "ffn1_w_down", "ffn1_norm_post", "mix_norm_pre", "w_in",
        "fox_forget_bias", "gdn_conv_w", "gdn_dt_bias", "gdn_a_log", "gdn_out_norm", "w_branch_fox",
        "w_branch_gdn", "w_out", "mix_norm_post", "ffn2_norm_pre", "ffn2_w_gate", "ffn2_w_up", "ffn2_w_down",
        "ffn2_norm_post"]


def blocks_of(w, nk):
    k, m = w.shape
    w = w.reshape(k // (P * nk), nk, P, m // P, P).transpose(3, 0, 2, 1, 4)
    return np.ascontiguousarray(w.reshape(-1, P, nk * P))


def alternate(*ws):
    return np.ascontiguousarray(np.stack(ws, 1).reshape(-1, *ws[0].shape[1:]))


def chunks(v):
    return np.asarray(v).reshape(-1, P).T


def layout(i):
    f = np.float32
    out = {}
    xs = np.concatenate([i["x_prompt"][0], i["x_sample"][:, 0]], 0)
    out["x"] = xs.T.reshape(KD, P, T).transpose(1, 0, 2)
    for n in (1, 2):
        out[f"w_gu{n}"] = alternate(blocks_of(i[f"ffn{n}_w_gate"][0], KD), blocks_of(i[f"ffn{n}_w_up"][0], KD))
        out[f"w_dn{n}"] = blocks_of(i[f"ffn{n}_w_down"][0], NKD)
    w = i["w_in"][0]
    at = np.cumsum([512, 512, 512, 8, 1536, 4, 4, 512, 1024, 1024])
    qkv, fa, cv, al, be, z, ga, gb = (w[:, 0:at[2]], w[:, at[2]:at[3]], w[:, at[3]:at[4]], w[:, at[4]:at[5]],
                                      w[:, at[5]:at[6]], w[:, at[6]:at[7]], w[:, at[7]:at[8]], w[:, at[8]:at[9]])
    out["w_proj"] = blocks_of(np.concatenate([qkv, cv, z, ga, gb], 1), KD)
    small = np.zeros((D, 96), f)
    small[:, 0:8], small[:, 32:36], small[:, 64:68] = fa, al, be
    out["w_small"] = small.reshape(KD, P, 96).transpose(1, 0, 2)
    branch = np.concatenate([i["w_branch_fox"][0], i["w_branch_gdn"][0]], 0)
    out["w_merge"] = blocks_of(branch, KD)
    out["w_out"] = blocks_of(i["w_out"][0], KD)
    v = np.zeros((P, NVEC), f)
    for c, name in ((V_PRE1, "ffn1_norm_pre"), (V_POST1, "ffn1_norm_post"), (V_PREM, "mix_norm_pre"),
                    (V_POSTM, "mix_norm_post"), (V_PRE2, "ffn2_norm_pre"), (V_POST2, "ffn2_norm_post")):
        v[:, c:c + KD] = chunks(i[name][0])
    v[:, V_GDN] = i["gdn_out_norm"][0]
    v[:, V_CONV:V_CONV + 48] = i["gdn_conv_w"][0].reshape(4, 12, P).transpose(2, 1, 0).reshape(P, 48)
    v[0:8, V_BIAS] = i["fox_forget_bias"][0]
    v[32:36, V_BIAS] = i["gdn_dt_bias"][0]
    v[32:36, V_ALOG] = i["gdn_a_log"][0]
    v[:, V_SIGN] = 1.0
    v[0:8, V_SIGN] = -1.0
    out["vecs"] = v
    out["cache_k"] = i["cache_k"][0][:, ::-1].reshape(PHYS, P, 4, P).transpose(0, 3, 2, 1).reshape(PHYS, P, 512)
    out["cache_v"] = i["cache_v"][0][:, ::-1].reshape(PHYS, P, 512)
    out["cache_logf"] = i["cache_logf"][0][:, ::-1].transpose(0, 2, 1).reshape(PHYS * HEADS, P)
    out["page_table"] = i["page_table"][:, ::-1]
    out["page_order"] = out["page_table"].reshape(2, 4, PAGES).transpose(0, 2, 1).reshape(1, NS * PAGES)
    out["conv_in"] = i["state_conv"][0].transpose(2, 1, 0).reshape(12, P, 3, NS).transpose(1, 0, 2, 3)
    out["state_in"] = i["state_gdn"][0].transpose(2, 1, 0, 3).reshape(P, GH * NS, P)
    out["ident"] = np.eye(P, dtype=f)
    out["ones"] = np.ones((P, P), f)
    r, c = np.arange(P)[:, None], np.arange(P)[None, :]
    sel = np.zeros((P, 8, P), f)
    for h in range(8):
        sel[h, h] = -DH ** 0.5
    for h in range(4):
        sel[32 + h, h] = sel[64 + h, h] = 1.0
    out["sel"] = sel.reshape(P, 1024)
    out["causal"] = np.where(c <= r, 0.0, NEG).astype(f)
    out["chunk_mask"] = np.where((r <= c) & (r // C == c // C), 0.0, NEG).astype(f)
    lev = [((r // (2 * s) == c // (2 * s)) & (r // s % 2 == 0) & (c // s % 2 == 1)).astype(f)
           for s in (1 << n for n in range(LEVELS))]
    out["levels"] = np.stack(lev, 1).reshape(P, LEVELS * P)
    out["chunk_start"] = np.where(np.arange(P)[:, None] < 32, 1.0, np.arange(SEQ) % C != 0).astype(f)
    out["head_mask"] = ((np.arange(P)[:, None] % 32) == (np.arange(512)[None, :] // DH)).astype(f)
    out["group_sel"] = (np.arange(P)[:, None] // 32 == np.arange(4)[None, :]).astype(f)
    out["head_row"] = (np.arange(P)[:, None] % 8).astype(np.int32)
    return {k: np.ascontiguousarray(v) for k, v in out.items()}


_OUTS = [("o_y", (P, KD, T)), ("o_proj", (P, 20, T)), ("o_logf", (HEADS, T)),
         ("o_state", (P, GH, P)), ("o_state_s", (P, GH * NS, P)), ("o_conv_s", (P, 12, 3, NS))]


def kernel(**inputs):
    import concourse.bacc as _bacc
    from concourse.bass_utils import run_bass_kernel_spmd as _run

    arrays = layout({k: np.asarray(v) for k, v in inputs.items()})
    nc = _bacc.Bacc("TRN2", target_bir_lowering=False, num_devices=1)
    aps = {n: nc.dram_tensor("in_" + n, v.shape, mybir.dt.from_np(v.dtype), kind="ExternalInput").ap() for n, v in arrays.items()}
    for n, shape in _OUTS:
        aps[n] = nc.dram_tensor(n, shape, F32, kind="ExternalOutput").ap()
    aps["spill"] = nc.dram_tensor("spill", (20, P, T), F32, kind="Internal").ap()
    program(nc, aps)
    r = _run(nc, [{"in_" + n: v for n, v in arrays.items()}], core_ids=[0]).results[0]
    y = np.ascontiguousarray(r["o_y"].transpose(2, 1, 0).reshape(T, D))
    pr = r["o_proj"].transpose(2, 1, 0).reshape(T, 20 * P)
    k, v, u = pr[:, 0:512], pr[:, 512:1024], pr[:, 1024:]
    lf = r["o_logf"].T
    conv_s = r["o_conv_s"].transpose(3, 2, 1, 0).reshape(NS, 3, 12 * P)
    c = np.ascontiguousarray
    return (c(y[None, :SEQ]), c(y[SEQ:, None]),
            c(k[:SEQ].reshape(1, 1, SEQ, HEADS, DH)), c(v[:SEQ].reshape(1, 1, SEQ, HEADS, DH)), c(lf[:SEQ][None, None]),
            c(r["o_state"].transpose(1, 0, 2)[None, None]), c(u[SEQ - 3:SEQ][None, None]),
            c(k[SEQ:].reshape(1, NS, 1, HEADS, DH)), c(v[SEQ:].reshape(1, NS, 1, HEADS, DH)), c(lf[SEQ:][None, :, None]),
            c(r["o_state_s"].reshape(P, GH, NS, P).transpose(2, 1, 0, 3)[None]), c(conv_s[None]))
```

```python
from contextlib import ExitStack

import numpy as np

import concourse.bass as bass
from concourse import mybir

F32 = mybir.dt.float32
F32R = mybir.dt.float32r
I32 = mybir.dt.int32
ALU = mybir.AluOpType
ACT = mybir.ActivationFunctionType
AX = mybir.AxisListType

P = 128
D = 1024
KD = D // P
SEQ = 512
NS = 8
T = SEQ + NS
HT = T // 2
FF = 2816
KF = FF // P
NKD = KF // 2
PAGES = 32
PHYS = 320
HEADS = 8
DH = 64
GH = 4
C = 64
NCH = SEQ // C
EPS = 1e-6
NEG = -1e30
KV_RING = 3
LEVELS = 6

V_PRE1, V_POST1, V_PREM, V_POSTM, V_PRE2, V_POST2, V_GDN, V_CONV, V_BIAS, V_ALOG, V_SIGN = (
    0, 8, 16, 24, 32, 40, 48, 49, 97, 98, 99)
NVEC = 100
Q0, K0, V0, CV0, Z0, NPROJ = 0, 4, 8, 12, 24, 28


def ds(i, n=1):
    return bass.ds(i, n)


def program(nc, a):
    ctx = ExitStack()
    with ctx:
        start_of = {}

        def sb(name, shape, dt=F32, scope=ctx):
            start_of[name] = -(-nc.sbuf_base // 32) * 32
            return scope.enter_context(nc.sbuf_tensor(name, shape, dt))

        def over(name, shape, dt, tensor, skip=0):
            return nc.alloc_sbuf_tensor_at(name, shape, dt, offset=start_of[tensor] + 4 * skip)

        def sem(name):
            return ctx.enter_context(nc.semaphore(name))

        x = sb("x", [P, KD, T])
        ident = sb("ident", [P, P])
        ones = sb("ones", [P, P])
        vecs = sb("vecs", [P, NVEC])
        w_raw = sb("w_raw", [P, 2, NKD, P])
        w_high = sb("w_high", [P, 2, NKD, P], F32R)
        w_low = sb("w_low", [P, 2, NKD, P], F32R)
        psum = ctx.enter_context(nc.psum_tensor("psum", [P, 8, 512], F32))

        def pair(g):
            return psum[:, 2 * g:2 * g + 2, 0:HT]

        def halves(t):
            return t.rearrange("p (h t) -> p h t", h=2)

        loaded = [sem("block_loaded0"), sem("block_loaded1")]
        high_done = sem("block_high_done")
        low_done = sem("block_low_done")
        block_used = sem("block_used")
        s_in = sem("inputs_loaded")
        x_in = [sem(f"x_loaded{k}") for k in range(KD)]
        s_out = sem("outputs_stored")
        count = {"block": 0, "out": 0, "in": 0}

        def load_block(eng, dram, i, n, u, nk):
            if not isinstance(n, int) or n >= 2:
                eng.wait_ge(low_done, n - 1)
            eng.dma_start(w_raw[:, u, 0:nk, :].rearrange("p k m -> p (k m)"),
                          dram[ds(i), :, :].rearrange("a p k -> p (a k)")).then_inc(loaded[u], 16)

        def load_first(eng, dram, n0, nk):
            for u in range(2):
                load_block(eng, dram, u, n0 + u, u, nk)

        def load_stream(eng, dram, blocks, n0, nk, first=True):
            if first:
                load_first(eng, dram, n0, nk)
            with eng.Fori(1, blocks // 2) as i:
                for u in range(2):
                    load_block(eng, dram, i * 2 + u, i * 2 + (n0 + u), u, nk)

        def split_high(act, n, u, nk, guard=True):
            act.wait_ge(loaded[u], (n - u) * 8 + 16)
            if guard:
                act.wait_ge(block_used, n - 1)
            act.activation(w_high[:, u, 0:nk, :], w_raw[:, u, 0:nk, :], ACT.Copy).then_inc(high_done, 1)

        def split_low(dve, n, u, nk):
            dve.wait_ge(high_done, n + 1)
            dve.tensor_tensor(w_low[:, u, 0:nk, :], w_raw[:, u, 0:nk, :],
                              w_high[:, u, 0:nk, :].bitcast(F32), ALU.subtract).then_inc(low_done, 1)

        def block_products(pe, n, u, ks, banks, high, low, k0, start, stop, done=None,
                           by_chunk=None):
            pe.wait_ge(low_done, n + 1)
            last = ks[-1]
            for h in range(2):
                tok = slice(h * HT, (h + 1) * HT)
                out = psum[:, 2 * banks + h, 0:HT]
                for j, k in enumerate(ks):
                    s = start and j == 0
                    e = stop and k == last
                    if by_chunk is not None and h == 0:
                        pe.wait_ge(by_chunk[0], by_chunk[1] + k + 1)
                    pe.matmul(out, w_high[:, u, k, :], high[:, k0 + j, tok], start=s, stop=False)
                    pe.matmul(out, w_high[:, u, k, :], low[:, k0 + j, tok], start=False, stop=False)
                    mm = pe.matmul(out, w_low[:, u, k, :], high[:, k0 + j, tok], start=False, stop=e)
            mm.then_inc(done if done is not None else block_used, 1)

        norm_sq = sem("norm_squares")
        norm_sum = sem("norm_sum")
        norm_root = sem("norm_root")
        norm_rec = sem("norm_factor")
        sq = sb("sq", [P, 2, T])
        root = sb("root", [P, T])
        factor = sb("factor", [P, T])
        norms = [0]

        def square(act, src, k, n, u=None):
            u = k % 2 if u is None else u
            if n or not isinstance(k, int) or k >= 2:
                act.wait_ge(norm_sum, k + (n * KD - 1))
            dst = sq[:, u, :] if src.shape[1] != 2 else halves(sq[:, u, :])
            act.activation(dst, src, ACT.Square).then_inc(norm_sq, 1)

        def factor_act(act, n, width=D):
            act.wait_ge(norm_sum, (n + 1) * KD)
            act.activation(halves(root[:, :]), psum[:, 6:8, 0:HT], ACT.Ln, bias=eps_col[:, 0:1],
                           scale=1.0 / width).then_inc(norm_root, 1)
            act.wait_ge(norm_root, n + 1)
            act.activation(factor[:, :], root[:, :], ACT.Exp, scale=-0.5).then_inc(norm_rec, 1)

        def next_norm_act(act, n, r0, block_n):
            for k in range(KD):
                act.wait_ge(x_new, r0 + k + 1)
                square(act, x[:, k, :], k, n)
                if k in (2, 4):
                    split_high(act, block_n + k // 4, k // 4, KD)
            factor_act(act, n)

        def square_sum(pe, k, n, u, start=False, stop=False):
            pe.wait_ge(norm_sq, k + (n * KD + 1))
            for h in range(2):
                mm = pe.matmul(psum[:, 6 + h, 0:HT], ones[:, :], sq[:, u, h * HT:(h + 1) * HT],
                               start=start, stop=stop)
            mm.then_inc(norm_sum, 1)

        def norm_pe(pe, n):
            if n:
                pe.wait_ge(norm_root, n)
            for k in range(KD):
                square_sum(pe, k, n, k % 2, k == 0, k == KD - 1)

        eps_col = sb("eps_col", [P, 1])
        s_eps = sem("eps_set")

        h_f = sb("h_f", [P, 2, T])
        h_ready = sem("h_ready")
        h_high_done = sem("h_high_done")
        h_low_done = sem("h_low_done")
        hcount = [0]

        def scaled_dve(dve, vcol, h_high, h_low, n, m0):
            dve.wait_ge(norm_rec, n + 1)
            for k in range(KD):
                if k >= 2:
                    dve.wait_ge(h_low_done, m0 + k - 1)
                dve.scalar_tensor_tensor(out=h_f[:, k % 2, :], in0=x[:, k, :], scalar=vecs[:, vcol + k:vcol + k + 1],
                                         in1=factor[:, :], op0=ALU.mult, op1=ALU.mult).then_inc(h_ready, 1)
                if k >= 1:
                    low_of(dve, h_high, h_low, m0, k - 1)
            low_of(dve, h_high, h_low, m0, KD - 1)

        def low_of(dve, h_high, h_low, m0, k):
            dve.wait_ge(h_high_done, m0 + k + 1)
            dve.tensor_tensor(h_low[:, k, :], h_f[:, k % 2, :], h_high[:, k, :].bitcast(F32),
                              ALU.subtract).then_inc(h_low_done, 1)

        def scaled_act(act, h_high, m0):
            for k in range(KD):
                act.wait_ge(h_ready, m0 + k + 1)
                act.activation(h_high[:, k, :], h_f[:, k % 2, :], ACT.Copy).then_inc(h_high_done, 1)

        res_tmp = h_f
        res_scaled = sem("residual_scaled")
        x_new = sem("x_updated")

        def residual_dve(dve, y, vcol, weight, n, r0):
            dve.wait_ge(norm_rec, n + 1)
            for k in range(KD):
                if k >= 2:
                    dve.wait_ge(x_new, r0 + k - 1)
                dve.scalar_tensor_tensor(out=res_tmp[:, k % 2, :], in0=y[:, k, :], scalar=vecs[:, vcol + k:vcol + k + 1],
                                         in1=factor[:, :], op0=ALU.mult, op1=ALU.mult).then_inc(res_scaled, 1)
                dve.wait_ge(res_scaled, r0 + k + 1)
                dve.scalar_tensor_tensor(out=x[:, k, :], in0=res_tmp[:, k % 2, :], scalar=weight, in1=x[:, k, :],
                                         op0=ALU.mult, op1=ALU.add).then_inc(x_new, 1)

        gate_silu = sem("gate_silu_done")
        hid_f = sem("hidden_done")
        hid_high = sem("hidden_high_done")
        hid_low = sem("hidden_low_done")
        y_copied = sem("y_copied")

        def ffn(which, w_gu, w_dn, v_pre, v_post, store):
            n0 = count["block"]
            nb = n0 + 2 * KF
            norm_n = norms[0]
            m0 = hcount[0]
            f0 = which * KF
            y0 = which * KD
            r0 = norms[0] // 2 * KD
            with ExitStack() as scope:
                h_high = sb(f"h_high{which}", [P, KD, T], F32R, scope)
                h_low = sb(f"h_low{which}", [P, KD, T], F32R, scope)
                a_high = sb(f"a_high{which}", [P, KF, T], F32R, scope)
                a_low = sb(f"a_low{which}", [P, KF, T], F32R, scope)
                sg = sb(f"silu{which}", [P, 2, T], F32, scope)
                af = sb(f"hidden{which}", [P, 2, T], F32, scope)
                y = over(f"y{which}", [P, KD, T], F32, f"h_high{which}")
                block = scope.enter_context(nc.Block())

                @block.sync
                def _(sp):
                    if which == 0:
                        sp.dma_start(ones[:, :], a["ones"]).then_inc(s_in, 16)
                        for k in range(KD):
                            sp.dma_start(x[:, k, :], a["x"][:, k, :]).then_inc(x_in[k], 16)
                        sp.dma_start(ident[:, :], a["ident"]).then_inc(s_in, 16)
                        sp.dma_start(vecs[:, :], a["vecs"]).then_inc(s_in, 16)
                    load_stream(sp, w_gu, 2 * KF, n0, KD, first=which == 0)
                    load_stream(sp, w_dn, 2 * KD, nb, NKD)
                    if which == 0:
                        load_first(sp, a["w_proj"], nb + 2 * KD, KD)
                    if store:
                        for k in range(KD):
                            sp.wait_ge(x_new, r0 + k + 1)
                            sp.dma_start(a["o_y"][:, k, :], x[:, k, :]).then_inc(s_out, 16)
                        count["out"] += KD
                        sp.wait_ge(s_out, 16 * count["out"])

                @block.gpsimd
                def _(pool):
                    if which == 0:
                        pool.memset(eps_col[:, :], EPS).then_inc(s_eps, 1)

                @block.scalar
                def _(act):
                    if which == 0:
                        act.wait_ge(s_eps, 1)
                    if which == 0:
                        for k in range(KD):
                            act.wait_ge(x_in[k], 16)
                            square(act, x[:, k, :], k, norm_n)
                        factor_act(act, norm_n)
                    if which == 0:
                        split_high(act, n0, 0, KD, guard=False)
                        split_high(act, n0 + 1, 1, KD, guard=False)
                    scaled_act(act, h_high, m0)

                    def silu(m, u):
                        act.wait_ge(block_used, m * 2 + (n0 + 1))
                        if not isinstance(m, int) or m >= 2:
                            act.wait_ge(hid_f, m + (f0 - 1))
                        act.activation(halves(sg[:, u, :]), pair(0), ACT.Silu).then_inc(gate_silu, 1)

                    def high(m, u):
                        act.wait_ge(hid_f, m + (f0 + 1))
                        act.activation(a_high[:, ds(m) if not isinstance(m, int) else slice(m, m + 1), :],
                                       af[:, u:u + 1, :], ACT.Copy).then_inc(hid_high, 1)


                    def body(m, tail=False):
                        for u in range(2):
                            nk = NKD if tail and u == 1 else KD
                            split_high(act, m * 2 + (n0 + 2 * u + 2), 0, nk)
                            silu(m + u, u)
                            split_high(act, m * 2 + (n0 + 2 * u + 3), 1, nk)
                            high(m + u, u)
                    body(0)
                    with act.Fori(1, KF // 2 - 1) as i:
                        body(i * 2)
                    body(KF - 2, tail=True)

                    def down(m, tail=False):
                        for u in range(2):
                            if not (tail and u == 1):
                                split_high(act, m * 2 + (nb + 2 * u + 2), 0, NKD)
                                split_high(act, m * 2 + (nb + 2 * u + 3), 1, NKD)
                            act.wait_ge(block_used, m * 2 + (nb + 2 * u + 2))
                            if isinstance(m, int):
                                dst = y[:, m + u, :]
                                dst = halves(dst)
                            else:
                                dst = y[:, ds(m + u), :].rearrange("p a (h t) -> p (a h) t", h=2)
                            square(act, pair(u), m + u, norm_n + 1, u)
                            act.activation(dst, pair(u), ACT.Copy).then_inc(y_copied, 1)
                    with act.Fori(0, KD // 2 - 1) as i:
                        down(i * 2)
                    down(KD - 2, tail=True)
                    factor_act(act, norm_n + 1)
                    if which == 0:
                        next_norm_act(act, norm_n + 2, r0, nb + 2 * KD)

                @block.vector
                def _(dve):
                    if which == 0:
                        split_low(dve, n0, 0, KD)
                        split_low(dve, n0 + 1, 1, KD)
                    scaled_dve(dve, v_pre, h_high, h_low, norm_n, m0)

                    def body(m, tail=False):
                        for u in range(2):
                            nk = NKD if tail and u == 1 else KD
                            split_low(dve, m * 2 + (n0 + 2 * u + 2), 0, nk)
                            split_low(dve, m * 2 + (n0 + 2 * u + 3), 1, nk)
                            dve.wait_ge(block_used, m * 2 + (n0 + 2 * u + 2))
                            dve.wait_ge(gate_silu, m + (f0 + u + 1))
                            if not isinstance(m, int) or m >= 2:
                                dve.wait_ge(hid_low, m + (f0 + u - 1))
                            dve.tensor_tensor(halves(af[:, u, :]), halves(sg[:, u, :]), pair(1),
                                              ALU.mult).then_inc(hid_f, 1)
                            dve.wait_ge(hid_high, m + (f0 + u + 1))
                            mm = m + u
                            at = slice(mm, mm + 1) if isinstance(mm, int) else ds(mm)
                            dve.tensor_tensor(a_low[:, at, :], af[:, u:u + 1, :], a_high[:, at, :].bitcast(F32),
                                              ALU.subtract).then_inc(hid_low, 1)
                    body(0)
                    with dve.Fori(1, KF // 2 - 1) as i:
                        body(i * 2)
                    body(KF - 2, tail=True)

                    def down(m, tail=False):
                        for u in range(2):
                            if not (tail and u == 1):
                                split_low(dve, m * 2 + (nb + 2 * u + 2), 0, NKD)
                                split_low(dve, m * 2 + (nb + 2 * u + 3), 1, NKD)
                    with dve.Fori(0, KD // 2 - 1) as i:
                        down(i * 2)
                    down(KD - 2, tail=True)
                    dve.wait_ge(y_copied, y0 + KD)
                    residual_dve(dve, y, v_post, 0.5, norm_n + 1, r0)
                    if which == 0:
                        split_low(dve, nb + 2 * KD, 0, KD)
                        split_low(dve, nb + 2 * KD + 1, 1, KD)
                    dve.wait_ge(x_new, r0 + KD)

                @block.tensor
                def _(pe):
                    pe.wait_ge(s_in, 48)
                    if which == 0:
                        norm_pe(pe, norm_n)

                    def body(m):
                        if not isinstance(m, int) or m >= 1:
                            pe.wait_ge(gate_silu, m + f0)
                        block_products(pe, m * 2 + n0, 0, range(KD), 0, h_high, h_low, 0, True, True,
                                       by_chunk=(h_low_done, m0) if isinstance(m, int) else None)
                        if not isinstance(m, int) or m >= 1:
                            pe.wait_ge(hid_f, m + f0)
                        block_products(pe, m * 2 + (n0 + 1), 1, range(KD), 1, h_high, h_low, 0, True, True)
                    body(0)
                    with pe.Fori(1, KF) as m:
                        body(m)
                    pe.wait_ge(hid_low, f0 + KF)

                    def down(m, first=False):
                        for u in range(2):
                            if not first:
                                pe.wait_ge(y_copied, m + (y0 + u - 1))
                            block_products(pe, m * 2 + (nb + 2 * u), 0, range(NKD), u, a_high, a_low, 0, True, False)
                            block_products(pe, m * 2 + (nb + 2 * u + 1), 1, range(NKD), u, a_high, a_low, NKD, False, True)
                            if not (first and u == 0):
                                square_sum(pe, m + (u - 1), norm_n + 1, 1 - u, start=first)
                    down(0, first=True)
                    with pe.Fori(1, KD // 2) as i:
                        down(i * 2)
                    square_sum(pe, KD - 1, norm_n + 1, 1, stop=True)
                    if which == 0:
                        norm_pe(pe, norm_n + 2)
            count["block"] = nb + 2 * KD
            norms[0] += 2
            hcount[0] += KD

        def mixer():
            mix = ctx.enter_context(ExitStack())
            proj = sb("proj", [P, Z0 + 1, T], F32, mix)
            rows = sb("rows", [96, T], F32, mix)
            cum = sb("cum", [96, SEQ], F32, mix)
            start_of["branch"] = -(-nc.sbuf_base // 32) * 32
            h_high = sb("mix_h_high", [P, KD, T], F32R, mix)
            h_low = sb("mix_h_low", [P, KD, T], F32R, mix)
            fox_o = (over("fox_high", [P, 4, T], F32R, "branch"), over("fox_low", [P, 4, T], F32R, "branch", 4 * T))
            gdn_o = (over("gdn_high", [P, 4, T], F32R, "branch", 8 * T), over("gdn_low", [P, 4, T], F32R, "branch", 12 * T))
            attention(proj, rows, cum, h_high, h_low, fox_o)
            gdn(proj, rows, cum, gdn_o)
            merge(fox_o, gdn_o)
            mix.close()

        def attention(proj, rows, cum, h_high, h_low, fox_o):
            n0 = count["block"]
            norm_n, m0 = norms[0], hcount[0]
            NB, FIRST = NPROJ + 16, 8
            R, J = 2, 4
            NG = PAGES // 4
            NQ = SEQ // P
            tiles = [(h, i) for h in range(HEADS) for i in range(NQ)]
            N = len(tiles)
            VB = FIRST + 2 * NG
            VE = VB + 2 * NG
            G1 = 2
            slots = [(t, half) for t in range(N + 2) for half in range(2) if (t % 6, half) != (5, 1)]
            key_plan = {slots[n]: (G1 + n // 4, n % 4) for n in range(4 * (NG - G1))}
            taken = {slots[4 * n + 3][0]: G1 + n for n in range(NG - G1)}
            T1 = slots[4 * (NG - G1) - 1][0]
            after = [s for s in slots if s[0] > T1]
            turn_plan = {after[4 * g]: g for g in range(NG)}
            value_plan = {after[n + 1]: n for n in range(PAGES)}
            lin_out = sem("block_out_taken")
            spilled = [sem("spilled0"), sem("spilled1")]
            small_in = sem("small_loaded")
            small_pe = sem("small_products")
            small_dve = sem("small_vector_steps")
            small_act = sem("small_scalar_steps")
            stored = sem("proj_stored")
            conv_out = sem("conv_state_stored")
            pt_loaded = sem("page_table_loaded")
            gsel_loaded = sem("group_sel_loaded")
            ptb_loaded = sem("page_table_spread")
            mask_loaded = sem("head_mask_loaded")
            idx_done = sem("page_rows_ready")
            lf_loaded = sem("logf_gathered")
            kv_loaded = [sem(f"kv_loaded{u}") for u in range(4)]
            kv_used = sem("kv_used")
            qbd_done = sem("query_blocks_ready")
            sc_dve = sem("scores_done")
            pre_pe = sem("sample_small_products")
            sdve = sem("sample_vector_steps")
            nbias = sem("sample_max_ready")
            p_exp = sem("sample_exp_done")
            pt_pe = sem("prob_transposed")
            pt_act = sem("prob_copied")
            om_done = sem("sample_out_masked")
            so_pe = sem("sample_out_turned")
            so_copy = sem("sample_out_copied")
            fin = sem("fox_constants_loaded")
            vt_pe = sem("fox_values_turned")
            vt_copy = sem("fox_values_copied")
            fs_pe = sem("fox_scores")
            f_neg = sem("fox_max_ready")
            f_exp = sem("fox_exp_done")
            f_dve = sem("fox_probs_ready")
            ft_pe = sem("fox_probs_turned")
            ft_copy = sem("fox_probs_copied")
            fo_pe = sem("fox_out")
            fo_high = sem("fox_out_high")
            fo_low = sem("fox_out_low")
            conv_in = sem("conv_state_loaded")
            cs = sem("conv_steps_done")
            spill = h_f
            fox_high, fox_low = fox_o
            with ExitStack() as scope:
                sc = sb("scores", [P, PAGES * P + 1], F32, scope)
                ring = sb("kv_ring", [P, 4, J, 512], F32, scope)
                qbd = sb("query_blocks", [P, 4, J, 32], F32, scope)
                pt1 = sb("pages", [1, NS * PAGES], I32, scope)
                ptb = sb("pages_bc", [P, R, PAGES], I32, scope)
                hrow = sb("head_row", [P, 1], I32, scope)
                idx = sb("logf_rows", [P, R, PAGES], I32, scope)
                gsel = sb("group_sel", [P, 4], F32, scope)
                st = sb("sample_stats", [P, R, 24], F32, scope)
                so = sb("sample_o", [P, 4, NS], F32, scope)
                stat = sb("fox_stats", [P, N, 3], F32, scope)
                coef = sb("coef", [96, 1], F32, scope)
                w16 = over("w_small", [P, KD, 96], F32, "kv_ring")
                w16_high = over("w_small_high", [P, KD, 96], F32R, "kv_ring", KD * 96)
                w16_low = over("w_small_low", [P, KD, 96], F32R, "kv_ring", 2 * KD * 96)
                starts = over("chunk_start", [96, SEQ], F32, "kv_ring", 3 * KD * 96)
                wz = over("small_z", [96, T], F32, "sq")
                wb = over("small_beta", [96, T], F32, "sq", T)
                wl = over("small_log", [96, T], F32, "root")
                wsum = over("small_sum", [96, T], F32, "factor")
                hmask = over("head_mask", [P, 512], F32, "sq")
                om = over("sample_out", [P, 512], F32, "factor")
                vb = over("value_bc", [P, 4, J, 32], F32, "root")
                prb = over("fox_probs", [P, 2, SEQ], F32, "branch", 8 * T)
                prt = over("fox_probs_t", [P, 2, SEQ], F32, "branch", 8 * T + 2 * SEQ)
                sel = sb("fox_sel", [8, 8, P], F32, scope)
                vtok = over("fox_v", [P, NQ, 512], F32, "w_raw")
                causal = sb("causal", [P, P], F32, scope)
                buf = over("conv_buf", [P, 12, 3, NS], F32, "w_raw", NQ * 512 + P)
                tap = over("conv_tap", [P, 12, NS], F32, "w_raw", NQ * 512 + P + 288)
                cnew = over("conv_new", [P, 12, NS], F32, "w_raw", NQ * 512 + P + 384)
                MX, RS, SN, NM, PN, RI = 0, 8, 16, 17, 18, 19
                block = scope.enter_context(nc.Block())

                @block.sync
                def _(sp):
                    sp.dma_start(w16[:, :, :], a["w_small"]).then_inc(small_in, 16)
                    sp.dma_start(starts[:, :], a["chunk_start"][0:96, :]).then_inc(small_in, 16)
                    sp.dma_start(pt1[:, :], a["page_order"]).then_inc(pt_loaded, 16)
                    sp.dma_start(gsel[:, :], a["group_sel"]).then_inc(gsel_loaded, 16)
                    sp.dma_start(sel[:, :, :].rearrange("p h k -> p (h k)"), a["sel"][0:8, :]).then_inc(fin, 16)
                    sp.dma_start(causal[:, :], a["causal"]).then_inc(fin, 16)
                    load_stream(sp, a["w_proj"], FIRST + 2, n0, KD, first=False)
                    sp.wait_ge(pt_loaded, 16)
                    sp.wait_ge(small_dve, 8)

                    def pages(g, r):
                        _, p = nc.values_load_multi_w_load_instructions(
                            pt1[0:1, ds(g * 16 + 4 * PAGES * r, 16)], engines=[mybir.EngineType.SP],
                            min_val=0, max_val=PHYS - 1,
                            skip_runtime_bounds_check_because="a page table holds pages of the cache")
                        return p

                    def load_step(u, p, cache, used):
                        if used is not None:
                            sp.wait_ge(kv_used, used)
                        for j in range(J):
                            sp.dma_start(ring[:, u, j, :], cache[ds(p[4 * u + j]), :, :]
                                         .rearrange("a p k -> p (a k)")).then_inc(kv_loaded[u], 16)
                    p = pages(0, 0)
                    for u in range(4):
                        load_step(u, p, a["cache_k"], None)
                        if u % 2:
                            n = FIRST + 2 + u // 2
                            load_block(sp, a["w_proj"], n, n0 + n, u // 2, KD)

                    def group(g, r, cache, g0, block_n):
                        p = pages(g, r)
                        for half in range(2):
                            if block_n is not None:
                                load_block(sp, a["w_proj"], block_n + half, block_n + (n0 + half), half, KD)
                            for u in (2 * half, 2 * half + 1):
                                load_step(u, p, cache, g * 4 + (4 * g0 + u - 3))
                    with sp.Fori(1, NG) as g:
                        group(g, 0, a["cache_k"], 0, g * 2 + (FIRST + 2))
                    with sp.Fori(0, NG) as g:
                        group(g, 0, a["cache_v"], NG, g * 2 + (VB + 2))
                    group(0, 1, a["cache_k"], 2 * NG, NB - 2)
                    group(1, 1, a["cache_k"], 2 * NG, None)
                    sp.wait_ge(lin_out, Z0)
                    sp.dma_start(a["o_proj"][:, CV0 - K0:, :], proj[:, CV0:Z0, :]).then_inc(stored, 16)
                    sp.dma_start(a["o_conv_s"][:, :, 2, :], proj[:, CV0:Z0, SEQ:T]).then_inc(stored, 16)
                    sp.dma_start(a["o_logf"], rows[0:HEADS, :]).then_inc(stored, 16)
                    sp.wait_ge(block_used, n0 + NB)
                    sp.dma_start(buf[:, :, :, :], a["conv_in"]).then_inc(conv_in, 16)
                    sp.wait_ge(conv_in, 16)
                    sp.dma_start(a["o_conv_s"][:, :, 0:2, :], buf[:, :, 1:3, :]).then_inc(conv_out, 16)
                    with sp.Fori(G1, NG) as g:
                        group(g, 1, a["cache_k"], 2 * NG, None)
                    with sp.Fori(0, NG) as g:
                        group(g, 1, a["cache_v"], 3 * NG, None)
                    sp.wait_ge(stored, 48)
                    sp.wait_ge(conv_out, 16)
                    for u in range(2):
                        sp.wait_ge(spilled[u], 16 * (NB - Z0) // 2)

                @block.gpsimd
                def _(pool):
                    pool.memset(qbd[:, :, :, :], 0.0).then_inc(qbd_done, 1)
                    pool.dma_start(hrow[:, :], a["head_row"]).then_inc(ptb_loaded, 16)
                    for r in range(R):
                        for j in range(J):
                            pool.dma_start(ptb[32 * j:32 * j + 32, r, :],
                                           a["page_table"][J * r + j:J * r + j + 1, :].broadcast_to([32, PAGES])
                                           ).then_inc(ptb_loaded, 16)

                    def gather(r, t):
                        if r:
                            pool.wait_ge(kv_used, PAGES + min(t + 2, PAGES))
                        pool.indirect_dma_start(sc[:, t * P + 1:(t + 1) * P + 1], None, a["cache_logf"],
                                                bass.IndirectOffsetOnAxis(ap=idx[:, r, t:t + 1], axis=0)
                                                ).then_inc(lf_loaded, 16)

                    def keep(n):
                        pool.wait_ge(lin_out, n + 1)
                        pool.dma_start(a["spill"][n - Z0, :, :], spill[:, n % 2, :]).then_inc(spilled[n % 2], 16)
                    pool.wait_ge(idx_done, 1)
                    for t in range(PAGES):
                        gather(0, t)
                    pool.wait_ge(small_dve, 8)
                    pool.dma_start(hmask[:, :], a["head_mask"]).then_inc(mask_loaded, 16)
                    pool.wait_ge(idx_done, 2)
                    for g in range(NG):
                        keep(VB + 2 * g)
                        for t in range(max(4 * g - 3, 0), 4 * g - 1):
                            gather(1, t)
                        keep(VB + 2 * g + 1)
                        for t in range(max(4 * g - 1, 0), 4 * g + 1):
                            gather(1, t)
                    keep(VE)
                    for t in range(4 * NG - 3, PAGES):
                        gather(1, t)
                    for n in range(VE + 1, NB):
                        keep(n)

                @block.scalar
                def _(act):
                    scaled_act(act, h_high, m0)
                    act.wait_ge(small_in, 32)
                    act.activation(w16_high[:, :, :], w16[:, :, :], ACT.Copy).then_inc(small_act, 1)

                    def copy(n, u):
                        act.wait_ge(block_used, n + (n0 + 1))
                        dst = proj[:, ds(n), :].rearrange("p a (h t) -> p (a h) t", h=2)
                        act.activation(dst, pair(u), ACT.Copy).then_inc(lin_out, 1)

                    def copies(first, last):
                        with act.Fori(first // 2, last // 2) as i:
                            for u in range(2):
                                split_high(act, i * 2 + (n0 + 2 + u), u, KD)
                                copy(i * 2 + u, u)
                    copies(0, 4)
                    act.wait_ge(small_dve, 3)
                    act.activation(wl[:, :], wl[:, :], ACT.Exp).then_inc(small_act, 1)
                    act.activation(coef[:, :], vecs[0:96, V_ALOG:V_ALOG + 1], ACT.Exp).then_inc(small_act, 1)
                    act.activation(wb[64:96, :], wz[64:96, :], ACT.Exp, scale=-1.0).then_inc(small_act, 1)
                    act.wait_ge(small_act, 2)
                    act.activation(wl[:, :], wl[:, :], ACT.Ln, bias=1.0).then_inc(small_act, 1)
                    copies(4, Z0)

                    def spill_out(n):
                        func = ACT.Silu if n < NPROJ else ACT.Sigmoid
                        u = n % 2
                        act.wait_ge(block_used, n0 + n + 1)
                        if n >= Z0 + 2:
                            act.wait_ge(spilled[u], (n - Z0) // 2 * 16)
                        act.activation(halves(spill[:, u, :]), pair(u), func).then_inc(lin_out, 1)

                    def prob_exp(r, g):
                        if g == 0:
                            act.wait_ge(nbias, (NG + 2) * (r + 1))
                        act.activation(sc[:, g * 512:(g + 1) * 512], sc[:, g * 512:(g + 1) * 512], ACT.Exp,
                                       bias=st[:, r, NM:NM + 1], accum_out=st[:, r, RS + g:RS + g + 1]).then_inc(p_exp, 1)

                    def new_exp(r):
                        act.activation(st[:, r, PN:PN + 1], st[:, r, SN:SN + 1], ACT.Exp,
                                       bias=st[:, r, NM:NM + 1]).then_inc(p_exp, 1)

                    def prob_copy(r, g):
                        act.wait_ge(pt_pe, NG * r + g + 1)
                        act.activation(sc[:, g * 512:(g + 1) * 512], psum[:, 4 + g % 2, :], ACT.Copy).then_inc(pt_act, 1)
                    for n in range(Z0, VB):
                        split_high(act, n0 + 2 + n, n % 2, KD)
                        spill_out(n)
                    for g in range(NG):
                        prob_exp(0, g)
                    new_exp(0)
                    for g in range(NG):
                        n = VB + 2 * g
                        for u in range(2):
                            split_high(act, n0 + 2 + n + u, u, KD)
                            spill_out(n + u)
                            if u == 0:
                                prob_copy(0, g)
                    for n in range(VE, NB):
                        if n + 2 < NB:
                            split_high(act, n0 + 2 + n, n % 2, KD)
                        spill_out(n)

                    def exp(t):
                        S = (tiles[t][1] + 1) * P
                        act.wait_ge(f_neg, 2 * t + 2)
                        if t >= 2:
                            act.wait_ge(ft_pe, t - 1)
                        act.activation(prb[:, t % 2, 0:S], psum[:, t % 2, 0:S], ACT.Exp, bias=stat[:, t, 0:1],
                                       scale=DH ** -0.5, accum_out=stat[:, t, 1:2]).then_inc(f_exp, 1)

                    def turned(t):
                        S = (tiles[t][1] + 1) * P
                        act.wait_ge(ft_pe, t + 1)
                        if t >= 2:
                            act.wait_ge(fo_pe, t - 1)
                        act.activation(prt[:, t % 2, 0:S], psum[:, 2, 0:S], ACT.Copy).then_inc(ft_copy, 1)

                    def out(c):
                        act.wait_ge(fo_pe, 8 * c + 8)
                        act.activation(fox_high[:, c, 0:SEQ], psum[:, 3, :], ACT.Copy).then_inc(fo_high, 1)
                    for t in range(N + 2):
                        if t < N:
                            exp(t)
                        if 1 <= t <= N:
                            turned(t - 1)
                        if t % 8 == 1 and t > 8:
                            out(t // 8 - 1)
                        if t == T1:
                            prob_exp(1, 0)
                            new_exp(1)
                        for half in range(2):
                            if (t, half) in turn_plan:
                                g = turn_plan[t, half]
                                prob_copy(1, g)
                                if g + 1 < NG:
                                    prob_exp(1, g + 1)
                    act.wait_ge(so_copy, R)
                    act.activation(fox_high[:, :, SEQ:T], so[:, :, :], ACT.Copy).then_inc(so_copy, 1)

                @block.vector
                def _(dve):
                    scaled_dve(dve, V_PREM, h_high, h_low, norm_n, m0)
                    dve.wait_ge(small_act, 1)
                    dve.tensor_tensor(w16_low[:, :, :], w16[:, :, :], w16_high[:, :, :].bitcast(F32),
                                      ALU.subtract).then_inc(small_dve, 1)
                    split_low(dve, n0 + 2, 0, KD)
                    split_low(dve, n0 + 3, 1, KD)
                    dve.wait_ge(small_pe, 1)
                    dve.wait_ge(h_low_done, m0 + KD)
                    dve.tensor_scalar(halves(wz[:, :]), psum[0:96, 4:6, 0:HT], vecs[0:96, V_BIAS:V_BIAS + 1],
                                      vecs[0:96, V_SIGN:V_SIGN + 1], ALU.add, ALU.mult).then_inc(small_dve, 1)
                    dve.wait_ge(small_dve, 2)
                    dve.scalar_tensor_tensor(out=wl[:, :], in0=wz[:, :], scalar=-1.0, in1=wz[:, :],
                                             op0=ALU.mult, op1=ALU.min).then_inc(small_dve, 1)
                    dve.wait_ge(ptb_loaded, 16 * 9)
                    for r in range(R):
                        dve.scalar_tensor_tensor(out=idx[:, r, :], in0=ptb[:, r, :], scalar=float(HEADS),
                                                 in1=hrow[:, :].broadcast_to([P, PAGES]), op0=ALU.mult,
                                                 op1=ALU.add).then_inc(idx_done, 1)
                    split_low(dve, n0 + 4, 0, KD)
                    split_low(dve, n0 + 5, 1, KD)
                    dve.wait_ge(small_act, 5)
                    dve.scalar_tensor_tensor(out=wsum[:, :], in0=wz[:, :], scalar=0.0, in1=wl[:, :],
                                             op0=ALU.max, op1=ALU.add).then_inc(small_dve, 1)
                    dve.tensor_scalar(wb[64:96, :], wb[64:96, :], 1.0, None, ALU.add).then_inc(small_dve, 1)
                    dve.wait_ge(small_dve, 4)
                    dve.tensor_scalar(rows[0:64, :], wsum[0:64, :], coef[0:64, 0:1], -1.0, ALU.mult,
                                      ALU.mult).then_inc(small_dve, 1)
                    dve.wait_ge(small_dve, 5)
                    dve.reciprocal(rows[64:96, :], wb[64:96, :]).then_inc(small_dve, 1)
                    dve.wait_ge(small_dve, 7)
                    dve.tensor_tensor_scan(cum[:, :], starts[:, :], rows[:, 0:SEQ], 0.0, ALU.mult,
                                           ALU.add).then_inc(small_dve, 1)

                    def queries(r):
                        dve.wait_ge(qbd_done, 8 * r + 1)
                        if r:
                            dve.wait_ge(kv_used, PAGES)
                        for c in range(4):
                            for u in range(2):
                                dve.tensor_copy(qbd[64 * u:64 * u + 64, c, :, 2 * c + u],
                                                proj[64 * u:64 * u + 64, Q0 + c, SEQ + J * r:SEQ + J * r + J]
                                                ).then_inc(qbd_done, 1)

                    def forgets(r):
                        v = 8 * r
                        dve.wait_ge(pre_pe, 2 * r + 1)
                        dve.tensor_copy(st[:, r, SN:SN + 1], psum[:, 7, 0:1]).then_inc(sdve, 1)
                        if r:
                            dve.wait_ge(kv_used, 2 * PAGES)
                        dve.tensor_copy(sc[:, 0:1], psum[:, 7, 1:2]).then_inc(sdve, 1)
                        dve.wait_ge(lf_loaded, 16 * PAGES * (r + 1))
                        dve.wait_ge(sdve, v + 2)
                        dve.tensor_tensor_scan(sc[:, 0:PAGES * P], ones[:, 0:1].broadcast_to([P, PAGES * P]),
                                               sc[:, 0:PAGES * P], 0.0, ALU.mult, ALU.add).then_inc(sdve, 1)
                        dve.wait_ge(sdve, v + 3)

                    def take_scores(r, g, u):
                        dve.wait_ge(kv_used, g * 4 + (2 * PAGES * r + 4))
                        dve.scalar_tensor_tensor(out=sc[:, ds(g * 512, 512)], in0=psum[:, 4 + u, :],
                                                 scalar=DH ** -0.5, in1=sc[:, ds(g * 512, 512)],
                                                 op0=ALU.mult, op1=ALU.add).then_inc(sc_dve, 1)
                        dve.wait_ge(sc_dve, g + (NG * r + 1))
                        dve.tensor_reduce(st[:, r, ds(g + MX)], sc[:, ds(g * 512, 512)], AX.X,
                                          ALU.max).then_inc(nbias, 1)

                    def peak_scores(r):
                        nb = (NG + 2) * r + NG
                        dve.wait_ge(nbias, nb)
                        dve.tensor_reduce(st[:, r, NM:NM + 1], st[:, r, MX:MX + NG], AX.X, ALU.max).then_inc(nbias, 1)
                        dve.tensor_scalar(st[:, r, SN:SN + 1], st[:, r, SN:SN + 1], DH ** -0.5, None,
                                          ALU.mult).then_inc(sdve, 1)
                        dve.wait_ge(nbias, nb + 1)
                        dve.wait_ge(sdve, 8 * r + 4)
                        dve.tensor_scalar(st[:, r, NM:NM + 1], st[:, r, NM:NM + 1], st[:, r, SN:SN + 1], -1.0,
                                          ALU.max, ALU.mult).then_inc(nbias, 1)
                        if r:
                            dve.wait_ge(pre_pe, 2 * r)
                        for c in range(4):
                            ins = dve.tensor_copy(vb[:, c, :, :], proj[:, V0 + c, SEQ + J * r:SEQ + J * r + J]
                                                  .rearrange("p (j o) -> p j o", o=1).broadcast_to([P, J, 32]))
                        ins.then_inc(sdve, 1)

                    def probs_sum(r):
                        dve.wait_ge(p_exp, (NG + 1) * (r + 1))
                        dve.tensor_reduce(st[:, r, RI:RI + 1], st[:, r, RS:RS + NG], AX.X, ALU.add).then_inc(sdve, 1)
                        dve.wait_ge(sdve, 8 * r + 6)
                        dve.tensor_tensor(st[:, r, RI:RI + 1], st[:, r, RI:RI + 1], st[:, r, PN:PN + 1],
                                          ALU.add).then_inc(sdve, 1)
                        dve.wait_ge(sdve, 8 * r + 7)
                        dve.reciprocal(st[:, r, RI:RI + 1], st[:, r, RI:RI + 1]).then_inc(sdve, 1)
                        dve.wait_ge(sdve, 8 * r + 8)

                    def masked(r):
                        dve.wait_ge(mask_loaded, 16)
                        dve.wait_ge(pre_pe, 2 * r + 2)
                        if r:
                            dve.wait_ge(so_pe, r)
                        dve.tensor_scalar(om[:, :], psum[:, 7, :], st[:, r, PN:PN + 1], None,
                                          ALU.mult).then_inc(om_done, 1)
                        dve.wait_ge(om_done, 3 * r + 1)
                        dve.tensor_tensor(om[:, :], om[:, :], psum[:, 6, :], ALU.add).then_inc(om_done, 1)
                        dve.wait_ge(om_done, 3 * r + 2)
                        dve.scalar_tensor_tensor(out=om[:, :], in0=om[:, :], scalar=st[:, r, RI:RI + 1], in1=hmask[:, :],
                                                 op0=ALU.mult, op1=ALU.mult).then_inc(om_done, 1)

                    def sample_out(r):
                        dve.wait_ge(so_pe, r + 1)
                        dve.tensor_copy(so[:, :, J * r:J * r + J], psum[:, 7, 0:16].rearrange("p (c j) -> p c j", c=4)
                                        ).then_inc(so_copy, 1)
                    with dve.Fori(2, FIRST // 2) as i:
                        for u in range(2):
                            split_low(dve, i * 2 + (n0 + 2 + u), u, KD)
                    dve.wait_ge(lin_out, Q0 + 4)
                    queries(0)
                    split_low(dve, n0 + FIRST + 2, 0, KD)
                    forgets(0)
                    split_low(dve, n0 + FIRST + 3, 1, KD)
                    for g in range(2):
                        if g:
                            for u in range(2):
                                split_low(dve, n0 + FIRST + 2 + 2 * g + u, u, KD)
                        take_scores(0, g, g)
                    with dve.Fori(1, NG // 2) as i:
                        for b in range(2):
                            for u in range(2):
                                split_low(dve, i * 4 + (n0 + FIRST + 2 + 2 * b + u), u, KD)
                            take_scores(0, i * 2 + b, b)
                    peak_scores(0)
                    queries(1)
                    with dve.Fori(VB // 2, NB // 2 - 1) as i:
                        for u in range(2):
                            split_low(dve, i * 2 + (n0 + 2 + u), u, KD)
                    probs_sum(0)
                    masked(0)

                    for b in range(NQ):
                        dve.wait_ge(vt_pe, b + 1)
                        dve.tensor_copy(vtok[:, b, :], psum[:, b, :]).then_inc(vt_copy, 1)
                    sample_out(0)
                    forgets(1)
                    for g in range(G1):
                        take_scores(1, g, g % 2)

                    def peak(t):
                        S = (tiles[t][1] + 1) * P
                        dve.wait_ge(fs_pe, t + 1)
                        dve.tensor_reduce(stat[:, t, 0:1], psum[:, t % 2, 0:S], AX.X, ALU.max).then_inc(f_neg, 1)
                        dve.wait_ge(f_neg, 2 * t + 1)
                        dve.tensor_scalar(stat[:, t, 0:1], stat[:, t, 0:1], -DH ** -0.5, None,
                                          ALU.mult).then_inc(f_neg, 1)

                    def norm(t):
                        S = (tiles[t][1] + 1) * P
                        dve.wait_ge(f_exp, t + 1)
                        dve.reciprocal(stat[:, t, 2:3], stat[:, t, 1:2]).then_inc(f_dve, 1)
                        dve.wait_ge(f_dve, 2 * t + 1)
                        dve.tensor_scalar(prb[:, t % 2, 0:S], prb[:, t % 2, 0:S], stat[:, t, 2:3], None,
                                          ALU.mult).then_inc(f_dve, 1)

                    def low(c):
                        dve.wait_ge(fo_high, c + 1)
                        dve.tensor_tensor(fox_low[:, c, 0:SEQ], psum[:, 3, :], fox_high[:, c, 0:SEQ].bitcast(F32),
                                          ALU.subtract).then_inc(fo_low, 1)

                    def conv_new():
                        wv = vecs[:, V_CONV:V_CONV + 48].rearrange("p (n i) -> p n i", i=4)
                        dve.wait_ge(conv_in, 16)
                        dve.tensor_tensor(cnew[:, :, :], proj[:, CV0:Z0, SEQ:T], wv[:, :, 3:4].broadcast_to([P, 12, NS]),
                                          ALU.mult).then_inc(cs, 1)
                        for i in range(3):
                            dve.wait_ge(cs, 2 * i + 1)
                            dve.tensor_tensor(tap[:, :, :], buf[:, :, i, :], wv[:, :, i:i + 1].broadcast_to([P, 12, NS]),
                                              ALU.mult).then_inc(cs, 1)
                            dve.wait_ge(cs, 2 * i + 2)
                            dve.tensor_tensor(cnew[:, :, :], cnew[:, :, :], tap[:, :, :], ALU.add).then_inc(cs, 1)
                        dve.wait_ge(stored, 48)

                    def conv_step(k):
                        n, d = 11 - k // 4, k % 4
                        src, dst = proj[:, CV0 + n, :], proj[:, CV0 + 1 + n, :]
                        w = vecs[:, V_CONV + 4 * n + 3 - d:V_CONV + 4 * n + 4 - d]
                        dve.wait_ge(cs, 7 + k)
                        if d == 0:
                            dve.tensor_scalar(dst[:, 0:SEQ], src[:, 0:SEQ], w, None, ALU.mult).then_inc(cs, 1)
                        else:
                            dve.scalar_tensor_tensor(out=dst[:, d:SEQ], in0=src[:, 0:SEQ - d], scalar=w,
                                                     in1=dst[:, d:SEQ], op0=ALU.mult, op1=ALU.add).then_inc(cs, 1)
                    for t in range(N + 2):
                        if t < N:
                            peak(t)
                        if 1 <= t <= N:
                            norm(t - 1)
                        if t % 8 == 1 and t > 8:
                            low(t // 8 - 1)
                        if t in taken:
                            take_scores(1, taken[t], taken[t] % 2)
                        if t == T1:
                            peak_scores(1)
                        if t == 4:
                            conv_new()
                        for k in range(2 * (t - 5), 2 * (t - 4)):
                            if 0 <= k < 48:
                                conv_step(k)
                    dve.wait_ge(cs, 7 + 48)
                    dve.tensor_copy(proj[:, CV0 + 1:Z0 + 1, SEQ:T], cnew[:, :, :]).then_inc(cs, 1)
                    probs_sum(1)
                    masked(1)
                    sample_out(1)
                    dve.wait_ge(so_copy, R + 1)
                    dve.tensor_tensor(fox_low[:, :, SEQ:T], so[:, :, :], fox_high[:, :, SEQ:T].bitcast(F32),
                                      ALU.subtract).then_inc(so_copy, 1)

                @block.tensor
                def _(pe):

                    def products(n, u):
                        if not isinstance(n, int) or n >= 2:
                            pe.wait_ge(lin_out, n - 1)
                        block_products(pe, n + n0, u, range(KD), u, h_high, h_low, 0, True, True,
                                       by_chunk=(h_low_done, m0) if isinstance(n, int) and n == 0 else None)
                    products(0, 0)
                    products(1, 1)
                    pe.wait_ge(small_dve, 1)
                    for h in range(2):
                        tok = slice(h * HT, (h + 1) * HT)
                        for k in range(KD):
                            out = psum[0:96, 4 + h, 0:HT]
                            pe.matmul(out, w16_high[:, k, :], h_high[:, k, tok], start=(k == 0), stop=False)
                            pe.matmul(out, w16_high[:, k, :], h_low[:, k, tok], start=False, stop=False)
                            mm = pe.matmul(out, w16_low[:, k, :], h_high[:, k, tok], start=False, stop=(k == KD - 1))
                    mm.then_inc(small_pe, 1)
                    with pe.Fori(1, FIRST // 2) as i:
                        for u in range(2):
                            products(i * 2 + u, u)

                    def new_token(r):
                        pe.wait_ge(qbd_done, 8 * r + 9)
                        if r:
                            pe.wait_ge(so_copy, r)
                        else:
                            pe.wait_ge(small_dve, 8)
                            pe.wait_ge(lin_out, K0 + 4)
                        for c in range(4):
                            for j in range(J):
                                pe.matmul(psum[32 * j:32 * j + 32, 7, 0:1], qbd[:, c, j, :],
                                          proj[:, K0 + c, SEQ + J * r + j:SEQ + J * r + j + 1], start=(c == 0),
                                          stop=(c == 3))
                        for j in range(J):
                            mm = pe.matmul(psum[32 * j:32 * j + 32, 7, 1:2], ident[0:8, 0:32],
                                           rows[0:8, SEQ + J * r + j:SEQ + J * r + j + 1], start=True, stop=True)
                        mm.then_inc(pre_pe, 1)

                    def key_step(r, g, u, first):
                        if u == 0 and not first:
                            pe.wait_ge(sc_dve, g + (NG * r - 1))
                        pe.wait_ge(kv_loaded[u], g * 64 + (128 * PAGES // 4 * r + 64))
                        b = key_bank[0]
                        for c in range(4):
                            for j in range(J):
                                mm = pe.matmul(psum[32 * j:32 * j + 32, b, u * P:(u + 1) * P], qbd[:, c, j, :],
                                               ring[:, u, j, c * P:(c + 1) * P], start=(c == 0), stop=(c == 3))
                        mm.then_inc(kv_used, 1)
                    key_bank = [4]

                    def turn(r, g):
                        pe.wait_ge(p_exp, (NG + 1) * r + g + 1 + (r if g else 0))
                        if g >= 2:
                            pe.wait_ge(pt_act, NG * r + g - 1)
                        for u in range(4):
                            mm = pe.transpose(psum[:, 4 + g % 2, u * P:(u + 1) * P],
                                              sc[:, g * 512 + u * P:g * 512 + (u + 1) * P], ident[:, :])
                        mm.then_inc(pt_pe, 1)

                    def value_step(r, t):
                        s = (2 * r + 1) * PAGES + t
                        if t % 4 == 0:
                            pe.wait_ge(pt_act, NG * r + t // 4 + 1)
                        pe.wait_ge(kv_loaded[t % 4], 64 * (s // 4 + 1))
                        for j in range(J):
                            mm = pe.matmul(psum[32 * j:32 * j + 32, 6, :], sc[:, t * P + 32 * j:t * P + 32 * j + 32],
                                           ring[:, t % 4, j, :], start=(t == 0), stop=(t == PAGES - 1))
                        mm.then_inc(kv_used, 1)

                    def new_values(r):
                        pe.wait_ge(sdve, 8 * r + 5)
                        if r:
                            pe.wait_ge(so_copy, r)
                        for c in range(4):
                            mm = pe.matmul(psum[:, 7, c * P:(c + 1) * P],
                                           vb[:, c, :, :].rearrange("p j o -> p (j o)"), ident[:, :],
                                           start=True, stop=True)
                        mm.then_inc(pre_pe, 1)

                    def out_columns(r):
                        pe.wait_ge(om_done, 3 * (r + 1))
                        for c in range(4):
                            mm = pe.matmul(psum[:, 7, 4 * c:4 * c + 4], om[:, c * P:(c + 1) * P], gsel[:, :],
                                           start=True, stop=True)
                        mm.then_inc(so_pe, 1)

                    def key_slots(i, first):
                        for b in range(2):
                            for half in range(2):
                                products(i * 4 + (FIRST + 2 * b + half), half)
                                if first and b == 0 and half == 0:
                                    new_token(0)
                                key_bank[0] = 4 + b
                                key_step(0, i * 2 + b, 2 * half, first)
                                key_step(0, i * 2 + b, 2 * half + 1, first)
                    key_slots(0, True)
                    with pe.Fori(1, NG // 2) as i:
                        key_slots(i, False)
                    pe.wait_ge(gsel_loaded, 16)
                    for g in range(NG):
                        products(VB + 2 * g, 0)
                        turn(0, g)
                        if g:
                            value_step(0, 4 * g - 2)
                            value_step(0, 4 * g - 1)
                        products(VB + 2 * g + 1, 1)
                        value_step(0, 4 * g)
                        value_step(0, 4 * g + 1)
                    products(VE, 0)
                    value_step(0, PAGES - 2)
                    value_step(0, PAGES - 1)
                    new_values(0)
                    pe.wait_ge(qbd_done, 17)
                    steps = [(g, u) for g in range(G1) for u in range(4)]
                    for n in range(VE + 1, NB):
                        products(n, n % 2)
                        for g, u in steps[:3]:
                            key_bank[0] = 4 + g % 2
                            key_step(1, g, u, False)
                        steps = steps[3:]
                    pe.wait_ge(lin_out, NB)
                    for b in range(NQ):
                        for c in range(4):
                            mm = pe.transpose(psum[:, b, c * P:(c + 1) * P],
                                              proj[:, V0 + c, b * P:(b + 1) * P], ident[:, :])
                        mm.then_inc(vt_pe, 1)
                    out_columns(0)
                    new_token(1)
                    pe.wait_ge(fin, 32)
                    pe.wait_ge(vt_copy, NQ)

                    def scores(t):
                        h, i = tiles[t]
                        c, lo = h // 2, 64 * (h % 2)
                        S = (i + 1) * P
                        if t >= 2:
                            pe.wait_ge(f_exp, t - 1)
                        bank = psum[:, t % 2, :]
                        pe.matmul(bank[:, 0:S], proj[lo:lo + 64, Q0 + c, i * P:(i + 1) * P],
                                  proj[lo:lo + 64, K0 + c, 0:S], start=True, stop=False)
                        pe.matmul(bank[:, 0:S], sel[:, h, :], cum[0:8, 0:S], start=False, stop=False)
                        pe.matmul(bank[:, S - P:S], ident[:, :], causal[:, :], start=False,
                                  stop=True).then_inc(fs_pe, 1)

                    def probs_turned(t):
                        h, i = tiles[t]
                        pe.wait_ge(f_dve, 2 * t + 2)
                        if t >= 1:
                            pe.wait_ge(ft_copy, t)
                        for j in range(i + 1):
                            mm = pe.transpose(psum[:, 2, j * P:(j + 1) * P], prb[:, t % 2, j * P:(j + 1) * P],
                                              ident[:, :])
                        mm.then_inc(ft_pe, 1)

                    def values(t):
                        h, i = tiles[t]
                        lo = 64 * (h % 2)
                        pe.wait_ge(ft_copy, t + 1)
                        if t % 8 == 0 and t:
                            pe.wait_ge(fo_low, t // 8)
                        for j in range(i + 1):
                            mm = pe.matmul(psum[lo:lo + 64, 3, i * P:(i + 1) * P],
                                           vtok[:, j, h * DH:(h + 1) * DH], prt[:, t % 2, j * P:(j + 1) * P],
                                           start=(j == 0), stop=(j == i))
                        mm.then_inc(fo_pe, 1)

                    def stream(t, half):
                        if (t, half) in key_plan:
                            g, u = key_plan[t, half]
                            key_bank[0] = 4 + g % 2
                            key_step(1, g, u, False)
                        if (t, half) in value_plan:
                            value_step(1, value_plan[t, half])
                        if (t, half) in turn_plan:
                            turn(1, turn_plan[t, half])
                    for t in range(N + 2):
                        if t < N:
                            scores(t)
                        stream(t, 0)
                        if 1 <= t <= N:
                            probs_turned(t - 1)
                        stream(t, 1)
                        if t >= 2:
                            values(t - 2)
                    new_values(1)
                    out_columns(1)
            count["block"] += NB
            norms[0] += 1
            hcount[0] += KD

        def gdn(proj, rows, cum, gdn_o):
            NP = SEQ // P
            n_merge = count["block"]
            with ExitStack() as outer:
                cv = proj[:, CV0 + 1:Z0 + 1, :]
                gdn_high, gdn_low = gdn_o
                o = sb("gdn_o", [P, GH, T], F32, outer)
                selc = sb("gdn_sel", [68, GH, P], F32, outer)
                gin = sem("gdn_constants_loaded")
                kv_out = sem("kv_stored")

                silu_done = sem("conv_silu_done")
                l_sq = sem("length_squares")
                l_sum = sem("length_sums")
                l_root = sem("length_roots")
                l_dve = sem("length_steps")
                inv8 = over("lengths", [P, 8, T], F32, "branch", 8 * T)
                NI = GH * NS
                step_scope = ExitStack()
                s0 = sb("state", [P, NI, P], F32, step_scope)
                s_state = sem("state_loaded")
                zt = over("silu_z", [P, GH, T], F32, "w_low")
                z_in = sem("z_loaded")
                mask = over("chunk_mask", [P, P], F32, "w_high")
                mask_r = over("mask_part", [P, SEQ], F32R, "w_high", P)
                ident_r = over("ident_part", [P, P], F32R, "w_high", P + SEQ)
                sel_r = over("sel_part", [68, GH, P], F32R, "w_high", 2 * P + SEQ)
                gb_high = over("g_beta_high", [68, SEQ], F32R, "w_high", 2 * P + 2 * SEQ)
                gb_low = over("g_beta_low", [68, SEQ], F32R, "w_high", 2 * P + 3 * SEQ)
                lev = over("levels", [P, LEVELS, P], F32, "sq")
                mask_in = sem("chunk_mask_loaded")
                p_in = sem("level_masks_loaded")
                parts_high = sem("high_parts")
                parts_low = sem("low_parts")
                with ExitStack() as scope:
                    block = scope.enter_context(nc.Block())

                    @block.sync
                    def _(sp):
                        sp.dma_start(mask[:, :], a["chunk_mask"]).then_inc(mask_in, 16)
                        sp.dma_start(lev[:, :, :].rearrange("p l k -> p (l k)"), a["levels"]).then_inc(p_in, 16)
                        sp.dma_start(s0[:, :, :], a["state_in"]).then_inc(s_state, 16)
                        sp.dma_start(zt[:, :, :], a["spill"][0:GH, :, :].rearrange("h p t -> p h t")).then_inc(z_in, 16)
                        for m in range(2):
                            load_block(sp, a["w_merge"], m, n_merge + m, m, KD)
                        sp.dma_start(a["o_proj"][:, 0:CV0 - K0, :], proj[:, K0:CV0, :]).then_inc(kv_out, 16)
                        sp.wait_ge(kv_out, 16)
                        sp.dma_start(selc[:, :, :].rearrange("p h k -> p (h k)"), a["sel"][0:68, 0:GH * P]).then_inc(gin, 16)
                        sp.wait_ge(gin, 16)

                    @block.vector
                    def _(dve):
                        for n in range(8):
                            dve.wait_ge(silu_done, n + 1)
                            dve.tensor_tensor(inv8[:, n, :], cv[:, n, :], cv[:, n, :], ALU.mult).then_inc(l_sq, 1)
                        for n in range(8):
                            dve.wait_ge(l_root, 8 + n + 1)
                            dve.scalar_tensor_tensor(out=cv[:, n, :], in0=cv[:, n, :], scalar=P ** -0.5 if n < 4 else 1.0,
                                                     in1=inv8[:, n, :], op0=ALU.mult, op1=ALU.mult).then_inc(l_dve, 1)

                    @block.scalar
                    def _(act):
                        for n in range(12):
                            act.activation(cv[:, n, :], cv[:, n, :], ACT.Silu).then_inc(silu_done, 1)
                        for n in range(8):
                            act.wait_ge(l_sum, n + 1)
                            act.activation(halves(inv8[:, n, :]), pair(n % 4), ACT.Ln, bias=eps_col[:, 0:1]).then_inc(l_root, 1)
                        for n in range(8):
                            act.wait_ge(l_root, n + 1)
                            act.activation(inv8[:, n, :], inv8[:, n, :], ACT.Exp, scale=-0.5).then_inc(l_root, 1)

                    @block.tensor
                    def _(pe):
                        for n in range(8):
                            pe.wait_ge(l_sq, n + 1)
                            if n >= 4:
                                pe.wait_ge(l_root, n - 3)
                            for h in range(2):
                                mm = pe.matmul(psum[:, 2 * (n % 4) + h, 0:HT], ones[:, :],
                                               inv8[:, n, h * HT:(h + 1) * HT], start=True, stop=True)
                            mm.then_inc(l_sum, 1)

                g_dve = sem("step_vector")
                g_pe = sem("step_products")
                g_act = sem("step_scalar")
                g_new = sem("states_updated")
                s_stored = sem("state_stored")
                with ExitStack() as scope:
                    kz = sb("key_rows", [NI, NI, P], F32, scope)
                    kq = sb("key_query", [P, NI, 2], F32, scope)
                    sm = sb("step_small", [P, 8, NI], F32, scope)
                    rw = sb("step_rows", [NI, 2, P], F32, scope)
                    EGS, BBS, KK, KC, DL, T1, T2 = range(7)
                    block = scope.enter_context(nc.Block())

                    def by_head(t):
                        return t.rearrange("p (h b) -> p h b", h=GH)

                    @block.sync
                    def _(sp):
                        for g in range(8):
                            sp.wait_ge(g_new, g + 1)
                            sp.dma_start(a["o_state_s"][:, 4 * g:4 * g + 4, :], s0[:, 4 * g:4 * g + 4, :]).then_inc(s_stored, 16)
                    @block.scalar
                    def _(act):
                        act.wait_ge(g_pe, 1)
                        act.activation(sm[:, EGS, :], psum[:, 0, 0:NI], ACT.Exp).then_inc(g_act, 1)
                        act.activation(gb_high[32:36, :], cum[32:36, :], ACT.Copy)
                        act.activation(gb_high[64:68, :], rows[64:68, 0:SEQ], ACT.Copy).then_inc(parts_high, 1)
                        for r in (32, 64):
                            act.activation(sel_r[r:r + 4, :, :], selc[r:r + 4, :, :], ACT.Copy)
                        act.activation(ident_r[:, :], ident[:, :], ACT.Copy)
                        act.wait_ge(mask_in, 16)
                        act.activation(mask_r[:, :].rearrange("p (n k) -> p n k", k=P),
                                       mask[:, :].rearrange("p (o k) -> p o k", o=1).broadcast_to([P, NP, P]),
                                       ACT.Copy).then_inc(parts_high, 1)

                    @block.gpsimd
                    def _(pool):
                        pool.wait_ge(parts_high, 1)
                        pool.tensor_tensor(gb_low[32:36, :], cum[32:36, :], gb_high[32:36, :].bitcast(F32),
                                           ALU.subtract).then_inc(parts_low, 1)
                        pool.tensor_tensor(gb_low[64:68, :], rows[64:68, 0:SEQ], gb_high[64:68, :].bitcast(F32),
                                           ALU.subtract).then_inc(parts_low, 1)

                    @block.vector
                    def _(dve):
                        new = slice(SEQ, T)
                        dve.tensor_copy(by_head(sm[:, KC, :]), cv[:, 4:8, new]).then_inc(g_dve, 1)
                        dve.tensor_tensor(by_head(sm[:, KK, :]), cv[:, 4:8, new], cv[:, 0:4, new], ALU.mult).then_inc(g_dve, 1)
                        dve.tensor_copy(kq[:, :, 0:1].rearrange("p (h b) o -> p h (b o)", h=GH), cv[:, 4:8, new]).then_inc(g_dve, 1)
                        dve.tensor_copy(kq[:, :, 1:2].rearrange("p (h b) o -> p h (b o)", h=GH), cv[:, 0:4, new]).then_inc(g_dve, 1)
                        dve.wait_ge(g_pe, 1)
                        dve.tensor_copy(rw[:, 1, :], psum[0:NI, 3, 0:P]).then_inc(g_dve, 1)
                        dve.wait_ge(g_dve, 5)
                        dve.tensor_tensor(kz[:, :, :], rw[:, 1:2, :].broadcast_to([NI, NI, P]),
                                          ident[0:NI, 0:NI].rearrange("p (i o) -> p i o", o=1).broadcast_to([NI, NI, P]),
                                          ALU.mult).then_inc(g_dve, 1)
                        dve.wait_ge(g_pe, 2)
                        dve.wait_ge(g_act, 1)
                        ks = psum[:, 2, 0:2 * NI].rearrange("p (i o) -> p i o", o=2)
                        dve.tensor_tensor(sm[:, T1, :], ks[:, :, 0], sm[:, EGS, :], ALU.mult).then_inc(g_dve, 1)
                        dve.wait_ge(g_dve, 7)
                        dve.tensor_tensor(by_head(sm[:, T1, :]), cv[:, 8:12, new], by_head(sm[:, T1, :]),
                                          ALU.subtract).then_inc(g_dve, 1)
                        dve.wait_ge(g_dve, 8)
                        dve.tensor_tensor(sm[:, DL, :], sm[:, T1, :], psum[:, 1, 0:NI], ALU.mult).then_inc(g_dve, 1)
                        dve.wait_ge(g_pe, 3)
                        dve.tensor_copy(rw[:, 0, :], psum[0:NI, 5, 0:P]).then_inc(g_dve, 1)
                        dve.tensor_tensor(sm[:, T2, :], ks[:, :, 1], sm[:, EGS, :], ALU.mult).then_inc(g_dve, 1)
                        dve.wait_ge(g_dve, 9)
                        dve.tensor_tensor(sm[:, T1, :], sm[:, DL, :], psum[:, 4, 0:NI], ALU.mult).then_inc(g_dve, 1)
                        dve.wait_ge(g_dve, 12)
                        dve.tensor_tensor(o[:, :, new], by_head(sm[:, T1, :]), by_head(sm[:, T2, :]), ALU.add).then_inc(g_dve, 1)
                        for i in range(NI):
                            g = i // 4
                            if i % 4 == 0:
                                dve.wait_ge(g_pe, 4 + g)
                            ins = dve.scalar_tensor_tensor(out=s0[:, i, :], in0=s0[:, i, :], scalar=sm[:, EGS, i:i + 1],
                                                           in1=psum[:, 6 + g % 2, (i % 4) * P:(i % 4 + 1) * P],
                                                           op0=ALU.mult, op1=ALU.add)
                            if i % 4 == 3:
                                ins.then_inc(g_new, 1)

                    @block.tensor
                    def _(pe):
                        for h in range(GH):
                            pe.matmul(psum[:, 0, NS * h:NS * h + NS], selc[32:36, h, :], rows[32:36, SEQ:T],
                                      start=True, stop=True)
                            pe.matmul(psum[:, 1, NS * h:NS * h + NS], selc[64:68, h, :], rows[64:68, SEQ:T],
                                      start=True, stop=True)
                        pe.wait_ge(g_dve, 2)
                        pe.matmul(psum[:, 4, 0:NI], ones[:, :], sm[:, KK, :], start=True, stop=True)
                        pe.transpose(psum[0:NI, 3, 0:P], sm[:, KC, :], ident[:, :]).then_inc(g_pe, 1)
                        pe.wait_ge(s_state, 16)
                        pe.wait_ge(g_dve, 4)
                        for i in range(NI):
                            mm = pe.matmul(psum[:, 2, 2 * i:2 * i + 2], s0[:, i, :], kq[:, i, :], start=True, stop=True)
                        mm.then_inc(g_pe, 1)
                        pe.wait_ge(g_dve, 9)
                        pe.transpose(psum[0:NI, 5, 0:P], sm[:, DL, :], ident[:, :]).then_inc(g_pe, 1)
                        pe.wait_ge(g_dve, 10)
                        for i in range(NI):
                            g = i // 4
                            if i % 4 == 0 and g >= 2:
                                pe.wait_ge(g_new, g - 1)
                            mm = pe.matmul(psum[:, 6 + g % 2, (i % 4) * P:(i % 4 + 1) * P], kz[:, i, :], rw[:, 0, :],
                                           start=True, stop=True)
                            if i % 4 == 3:
                                mm.then_inc(g_pe, 1)
                step_scope.close()

                at = over("attn_t", [P, GH, SEQ], F32, "proj")
                e_t = over("inverse_t", [P, GH, SEQ], F32, "proj", GH * SEQ)
                dm = over("inverse", [P, GH, SEQ], F32, "proj", 2 * GH * SEQ)
                eg = over("exp_g", [P, SEQ], F32, "root")
                el = over("exp_left", [P, SEQ], F32, "factor")
                lo_ = over("level_part", [P, 2, SEQ], F32, "h_f")
                p_bc = sem("prep_products")
                p_act = sem("prep_scalar")
                p_dve = sem("prep_vector")
                p_raw = sem("prep_pairs")
                p_last = sem("prep_last")
                p_neg = sem("prep_negated")
                p_turn = sem("prep_turned")
                p_tok = sem("prep_token_major")
                l_mask = sem("level_masked")
                l_pe = sem("level_products")
                l_act = sem("level_copied")
                l_upd = sem("level_updated")
                w_pe = sem("solved_products")
                w_act = sem("solved_copied")
                c_pe = sem("scan_products")
                c_dve = sem("scan_steps")
                c_out = sem("scan_out")
                c_copy = sem("scan_out_copied")
                g_store = sem("prompt_state_stored")
                with ExitStack() as scope:
                    vbt = sb("v_tok", [P, GH, SEQ], F32, scope)
                    kbt = sb("k_tok", [P, GH, SEQ], F32, scope)
                    kht = sb("k_left_tok", [P, GH, SEQ], F32, scope)
                    lt = sb("lower_t", [P, GH, SEQ], F32, scope)
                    tmp = sb("gdn_tmp", [P, 4, SEQ], F32, scope)
                    S = sb("gdn_state", [P, GH, P], F32, scope)
                    egl = sb("exp_g_last", [P, GH, NCH], F32, scope)
                    gl = sb("g_last", [P, NCH], F32, scope)
                    neg_g = sb("neg_g", [P, NP, GH], F32, scope)
                    KB, KBE, KH, DT = range(4)
                    block = scope.enter_context(nc.Block())

                    def pr(t, p):
                        return t[:, p * P:(p + 1) * P]

                    def pairs(t):
                        return t.rearrange("p (n k) -> p n k", n=NP)

                    def over_pairs(t):
                        return t.rearrange("p (o k) -> p o k", o=1).broadcast_to([P, NP, P])

                    @block.sync
                    def _(sp):
                        sp.wait_ge(s_stored, 16 * 8)
                        sp.wait_ge(c_dve, 2 * NCH + 1)
                        sp.dma_start(a["o_state"], S[:, :, :]).then_inc(g_store, 16)
                        sp.wait_ge(g_store, 16)

                    @block.tensor
                    def _(pe):
                        for p in range(NP):
                            mm = pe.matmul(psum[:, 7, GH * p:GH * p + GH], cum[32:36, p * P:(p + 1) * P],
                                           ident[32:36, 32:36], start=True, stop=True)
                        mm.then_inc(p_neg, 1)

                        def spread(h):
                            if h:
                                pe.wait_ge(p_dve, 9 * (h - 1) + 3)
                                pe.wait_ge(p_act, 3 * (h - 1) + 2)
                            g_h, b_h = sel_r[32:36, h, :], sel_r[64:68, h, :]
                            pe.matmul(psum[:, 0, :], g_h, gb_high[32:36, :], start=True, stop=False)
                            pe.matmul(psum[:, 0, :], g_h, gb_low[32:36, :], start=False, stop=True)
                            pe.matmul(psum[:, 2, :], g_h, gb_high[32:36, :], start=True, stop=False)
                            pe.matmul(psum[:, 2, :], g_h, gb_low[32:36, :], start=False, stop=False)
                            pe.matmul(psum[:, 2, :], ident_r[:, :], mask_r[:, :], start=False, stop=True)
                            pe.matmul(psum[:, 1, :], b_h, gb_high[64:68, :], start=True, stop=False)
                            pe.matmul(psum[:, 1, :], b_h, gb_low[64:68, :], start=False, stop=True).then_inc(p_bc, 1)
                        spread(0)
                        for h in range(GH):
                            pe.wait_ge(p_dve, 9 * h + 3)
                            k = cv[:, 4 + h, 0:SEQ]
                            for p in range(NP):
                                pe.matmul(pr(psum[:, 3, :], p), pr(k, p), pr(tmp[:, KB, :], p), start=True, stop=True)
                            for p in range(NP):
                                mm = pe.matmul(pr(psum[:, 4, :], p), pr(k, p), pr(cv[:, h, 0:SEQ], p), start=True, stop=True)
                            mm.then_inc(p_raw, 1)
                            if h < GH - 1:
                                spread(h + 1)
                            pe.wait_ge(p_dve, 9 * h + 6)
                            if h:
                                pe.wait_ge(p_tok, 3 * h)
                            else:
                                pe.wait_ge(p_neg, 2)
                            for n, src in enumerate((cv[:, 8 + h, 0:SEQ], tmp[:, KBE, :], tmp[:, KH, :])):
                                for p in range(NP):
                                    mm = pe.transpose(pr(psum[:, 5 + n, :], p), pr(src, p), ident[:, :])
                            mm.then_inc(p_turn, 1)
                        for h in range(GH):
                            pe.wait_ge(l_upd, h + 1)
                            for p in range(NP):
                                mm = pe.transpose(pr(psum[:, h, :], p), pr(e_t[:, h, :], p), ident[:, :])
                            mm.then_inc(l_pe, 1)
                        for lv in range(1, LEVELS):
                            n = (lv - 1) * GH
                            for h in range(GH):
                                pe.wait_ge(l_mask, n + h + 1)
                                pe.wait_ge(l_act, GH + n)
                                if lv > 1:
                                    pe.wait_ge(l_upd, GH + 2 * (n - GH) + 2 * h + 2)
                                for p in range(NP):
                                    mm = pe.matmul(pr(psum[:, h, :], p), pr(lo_[:, h % 2, :], p), pr(dm[:, h, :], p),
                                                   start=True, stop=True)
                                mm.then_inc(l_pe, 1)
                            for h in range(GH):
                                pe.wait_ge(l_act, GH + n + h + 1)
                                if h >= 2:
                                    pe.wait_ge(l_upd, GH + 2 * n + 2 * (h - 2) + 2)
                                b = 4 + 2 * (h % 2)
                                for p in range(NP):
                                    pe.matmul(pr(psum[:, b, :], p), pr(e_t[:, h, :], p), pr(tmp[:, h, :], p),
                                              start=True, stop=True)
                                for p in range(NP):
                                    mm = pe.matmul(pr(psum[:, b + 1, :], p), pr(tmp[:, h, :], p), pr(e_t[:, h, :], p),
                                                   start=True, stop=True)
                                mm.then_inc(w_pe, 1)
                        nu = GH * (LEVELS - 1)
                        for h in range(GH):
                            pe.wait_ge(l_upd, GH + 2 * (nu - GH) + 2 * h + 2)
                            if h >= 2:
                                pe.wait_ge(w_act, 2 * (h - 2) + 2)
                            b = 2 * (h % 2)
                            for p in range(NP):
                                pe.matmul(pr(psum[:, b, :], p), pr(e_t[:, h, :], p), pr(vbt[:, h, :], p), start=True, stop=True)
                            for p in range(NP):
                                mm = pe.matmul(pr(psum[:, b + 1, :], p), pr(kbt[:, h, :], p), pr(e_t[:, h, :], p),
                                               start=True, stop=True)
                            mm.then_inc(w_pe, 1)
                        pe.wait_ge(w_act, 2 * GH)
                        for n in range(NCH):
                            p, r = n // 2, C * (n % 2)
                            tok = slice(n * C, (n + 1) * C)
                            pe.wait_ge(c_dve, 2 * n + 1)
                            for h in range(GH):
                                mm = pe.matmul(psum[r:r + C, 4, h * P:(h + 1) * P], dm[:, h, tok], S[:, h, :],
                                               start=True, stop=True)
                            mm.then_inc(c_pe, 1)
                            if n % 2 == 0 and p >= 2:
                                pe.wait_ge(c_copy, p - 1)
                            for h in range(GH):
                                pe.matmul(psum[:, 6 + p % 2, h * P + r:h * P + r + C], S[:, h, :], cv[:, h, tok],
                                          start=(n % 2 == 0 and h == 0), stop=False, skip_group_check=True)
                            pe.wait_ge(c_dve, 2 * n + 2)
                            for h in range(GH):
                                mm = pe.matmul(psum[:, 5, h * P:(h + 1) * P], kht[r:r + C, h, p * P:(p + 1) * P],
                                               vbt[r:r + C, h, p * P:(p + 1) * P], start=True, stop=True)
                            mm.then_inc(c_pe, 1)
                            if n % 2:
                                for h in range(GH):
                                    mm = pe.matmul(psum[:, 6 + p % 2, h * P:(h + 1) * P], vbt[:, h, p * P:(p + 1) * P],
                                                   at[:, h, p * P:(p + 1) * P], start=False, stop=(h == GH - 1),
                                                   skip_group_check=True)
                                mm.then_inc(c_out, 1)

                    @block.gpsimd
                    def _(pool):
                        pool.wait_ge(p_in, 16)
                        for lv in range(1, LEVELS):
                            n = (lv - 1) * GH
                            for h in range(GH):
                                if n + h >= 2:
                                    m = n + h - 2
                                    pool.wait_ge(l_pe, GH + m + 1)
                                    pool.wait_ge(l_mask, m + 1)
                                else:
                                    pool.wait_ge(l_upd, GH)
                                pool.tensor_tensor(pairs(lo_[:, h % 2, :]), pairs(lt[:, h, :]), over_pairs(lev[:, lv, :]),
                                                   ALU.mult).then_inc(l_mask, 1)

                    @block.scalar
                    def _(act):
                        def exps(h):
                            act.wait_ge(p_bc, h + 1)
                            if h:
                                act.wait_ge(p_dve, 9 * h)
                            act.activation(eg[:, :], psum[:, 0, :], ACT.Exp).then_inc(p_act, 1)
                            for p in range(NP):
                                ins = act.activation(pr(tmp[:, DT, :], p), pr(psum[:, 2, :], p), ACT.Exp,
                                                     bias=neg_g[:, p, h:h + 1])
                            ins.then_inc(p_act, 1)

                        def left(h):
                            act.wait_ge(p_dve, 9 * h + 1)
                            act.activation(el[:, :], el[:, :], ACT.Exp).then_inc(p_act, 1)
                        act.wait_ge(p_neg, 2)
                        exps(0)
                        left(0)
                        for h in range(GH):
                            if h < GH - 1:
                                exps(h + 1)
                            act.wait_ge(p_turn, h + 1)
                            if h == 0:
                                act.wait_ge(s_stored, 16 * 8)
                            for n, t in enumerate((vbt, kbt, kht)):
                                act.activation(t[:, h, :], psum[:, 5 + n, :], ACT.Copy).then_inc(p_tok, 1)
                            if h < GH - 1:
                                left(h + 1)
                        for h in range(GH):
                            act.wait_ge(l_pe, h + 1)
                            act.activation(dm[:, h, :], psum[:, h, :], ACT.Copy).then_inc(l_act, 1)
                        for lv in range(1, LEVELS):
                            n = (lv - 1) * GH
                            for h in range(GH):
                                act.wait_ge(l_pe, GH + n + h + 1)
                                if lv > 1:
                                    act.wait_ge(w_pe, n - GH + h + 1)
                                act.activation(tmp[:, h, :], psum[:, h, :], ACT.Copy).then_inc(l_act, 1)
                        for h in range(GH):
                            act.wait_ge(w_pe, GH * (LEVELS - 1) + h + 1)
                            b = 2 * (h % 2)
                            act.activation(vbt[:, h, :], psum[:, b, :], ACT.Copy).then_inc(w_act, 1)
                            act.activation(dm[:, h, :], psum[:, b + 1, :], ACT.Copy).then_inc(w_act, 1)
                        for p in range(NP):
                            act.wait_ge(c_out, p + 1)
                            act.activation(o[:, :, p * P:(p + 1) * P], psum[:, 6 + p % 2, :].rearrange("p (h k) -> p h k", h=GH),
                                           ACT.Copy).then_inc(c_copy, 1)

                    @block.vector
                    def _(dve):
                        dve.wait_ge(p_neg, 1)
                        dve.tensor_scalar(neg_g[:, :, :], psum[:, 7, 0:NP * GH].rearrange("p (n h) -> p n h", h=GH),
                                          -1.0, None, ALU.mult).then_inc(p_neg, 1)
                        for h in range(GH):
                            k, q, v = cv[:, 4 + h, 0:SEQ], cv[:, h, 0:SEQ], cv[:, 8 + h, 0:SEQ]
                            dve.wait_ge(p_bc, h + 1)
                            if h:
                                dve.wait_ge(p_turn, h)
                                dve.wait_ge(p_dve, 9 * h)
                            gb = psum[:, 0, :].rearrange("p (n c) -> p n c", c=C)
                            dve.wait_ge(p_act, 3 * h + 1)
                            dve.tensor_copy(egl[:, h, :], eg[:, :].rearrange("p (n c) -> p n c", c=C)[:, :, C - 1]
                                            ).then_inc(p_last, 1)
                            dve.tensor_copy(gl[:, :], gb[:, :, C - 1]).then_inc(p_last, 1)
                            dve.wait_ge(p_last, 2 * h + 2)
                            dve.tensor_tensor(el[:, :].rearrange("p (n c) -> p n c", c=C),
                                              gl[:, :].rearrange("p (n o) -> p n o", o=1).broadcast_to([P, NCH, C]), gb,
                                              ALU.subtract).then_inc(p_dve, 1)
                            dve.tensor_tensor(v, v, psum[:, 1, :], ALU.mult).then_inc(p_dve, 1)
                            dve.tensor_tensor(tmp[:, KB, :], k, psum[:, 1, :], ALU.mult).then_inc(p_dve, 1)
                            dve.wait_ge(p_dve, 9 * h + 3)
                            dve.tensor_tensor(tmp[:, KBE, :], tmp[:, KB, :], eg[:, :], ALU.mult).then_inc(p_dve, 1)
                            dve.wait_ge(p_act, 3 * h + 3)
                            dve.tensor_tensor(tmp[:, KH, :], k, el[:, :], ALU.mult).then_inc(p_dve, 1)
                            dve.wait_ge(p_raw, h + 1)
                            dve.tensor_tensor(q, q, eg[:, :], ALU.mult).then_inc(p_dve, 1)
                            dve.tensor_tensor(lt[:, h, :], psum[:, 3, :], tmp[:, DT, :], ALU.mult).then_inc(p_dve, 1)
                            dve.tensor_tensor(at[:, h, :], psum[:, 4, :], tmp[:, DT, :], ALU.mult).then_inc(p_dve, 1)
                            dve.wait_ge(p_in, 16)
                            dve.wait_ge(p_dve, 9 * h + 7)
                            dve.tensor_tensor(pairs(e_t[:, h, :]), pairs(lt[:, h, :]), over_pairs(lev[:, 0, :]),
                                              ALU.mult).then_inc(p_dve, 1)
                            dve.wait_ge(p_dve, 9 * h + 9)
                            dve.tensor_tensor(pairs(e_t[:, h, :]), over_pairs(ident[:, :]), pairs(e_t[:, h, :]),
                                              ALU.subtract).then_inc(l_upd, 1)
                        for lv in range(1, LEVELS):
                            n = (lv - 1) * GH
                            for h in range(GH):
                                dve.wait_ge(w_pe, n + h + 1)
                                b = 4 + 2 * (h % 2)
                                dve.tensor_tensor(dm[:, h, :], dm[:, h, :], psum[:, b, :], ALU.subtract).then_inc(l_upd, 1)
                                dve.tensor_tensor(e_t[:, h, :], e_t[:, h, :], psum[:, b + 1, :],
                                                  ALU.subtract).then_inc(l_upd, 1)
                        dve.memset(S[:, :, :], 0.0).then_inc(c_dve, 1)
                        dve.wait_ge(w_act, 2 * GH)
                        for n in range(NCH):
                            p, r = n // 2, C * (n % 2)
                            dve.wait_ge(c_pe, 2 * n + 1)
                            new = vbt[r:r + C, :, p * P:(p + 1) * P]
                            dve.tensor_tensor(new, new, psum[r:r + C, 4, :].rearrange("p (h k) -> p h k", h=GH),
                                              ALU.subtract).then_inc(c_dve, 1)
                            dve.wait_ge(c_pe, 2 * n + 2)
                            for h in range(GH):
                                ins = dve.scalar_tensor_tensor(out=S[:, h, :], in0=S[:, h, :], scalar=egl[:, h, n:n + 1],
                                                               in1=psum[:, 5, h * P:(h + 1) * P], op0=ALU.mult, op1=ALU.add)
                            ins.then_inc(c_dve, 1)

                z_dve = sem("gated_steps")
                z_sq = sem("gated_squares")
                z_sum = sem("gated_sums")
                z_root = sem("gated_roots")
                z_high = sem("gated_high")
                z_pool = sem("gated_by_z")
                z_low = sem("gated_low")
                inv4 = over("inv_rms", [P, GH, T], F32, "w_high")
                with ExitStack() as scope:
                    block = scope.enter_context(nc.Block())

                    @block.scalar
                    def _(act):
                        for h in range(GH):
                            act.activation(inv4[:, h, :], o[:, h, :], ACT.Square).then_inc(z_sq, 1)
                        for h in range(GH):
                            act.wait_ge(z_sum, h + 1)
                            act.activation(halves(inv4[:, h, :]), pair(h), ACT.Ln, bias=eps_col[:, 0:1],
                                           scale=1.0 / P).then_inc(z_root, 1)
                        for h in range(GH):
                            act.wait_ge(z_root, h + 1)
                            act.activation(inv4[:, h, :], inv4[:, h, :], ACT.Exp, scale=-0.5).then_inc(z_root, 1)
                        for h in range(GH):
                            act.wait_ge(z_dve, h + 1)
                            act.activation(gdn_high[:, h, :], o[:, h, :], ACT.Copy).then_inc(z_high, 1)

                    @block.tensor
                    def _(pe):
                        for h in range(GH):
                            pe.wait_ge(z_sq, h + 1)
                            for u in range(2):
                                mm = pe.matmul(psum[:, 2 * h + u, 0:HT], ones[:, :], inv4[:, h, u * HT:(u + 1) * HT],
                                               start=True, stop=True)
                            mm.then_inc(z_sum, 1)

                    @block.gpsimd
                    def _(pool):
                        pool.wait_ge(z_in, 16)
                        for h in range(GH):
                            pool.tensor_tensor(zt[:, h, :], zt[:, h, :], o[:, h, :], ALU.mult).then_inc(z_pool, 1)

                    @block.vector
                    def _(dve):
                        for h in range(GH):
                            dve.wait_ge(z_root, GH + h + 1)
                            dve.wait_ge(z_pool, h + 1)
                            dve.scalar_tensor_tensor(out=o[:, h, :], in0=zt[:, h, :], scalar=vecs[:, V_GDN:V_GDN + 1],
                                                     in1=inv4[:, h, :], op0=ALU.mult, op1=ALU.mult).then_inc(z_dve, 1)
                        for h in range(GH):
                            dve.wait_ge(z_high, h + 1)
                            dve.tensor_tensor(gdn_low[:, h, :], o[:, h, :], gdn_high[:, h, :].bitcast(F32),
                                              ALU.subtract).then_inc(z_low, 1)

        def merge(fox_o, gdn_o):
            n0 = count["block"]
            nb = n0 + KD
            norm_n = norms[0]
            r0 = KD
            g_in = [sem("gates_loaded0"), sem("gates_loaded1")]
            fox_used = sem("fox_products")
            m_dve = sem("merge_steps")
            m_high = sem("merged_high")
            m_low = sem("merged_low")
            y_out = sem("mixed_copied")
            with ExitStack() as scope:
                gt = sb("gates", [P, 2, 2, T], F32, scope)
                mf = sb("merged", [P, 2, 2, T], F32, scope)
                mg_high = sb("merged_high", [P, KD, T], F32R, scope)
                mg_low = over("merged_low", [P, KD, T], F32R, "proj")
                y = over("mixed", [P, KD, T], F32, "proj", KD * T)
                block = scope.enter_context(nc.Block())

                @block.sync
                def _(sp):
                    for m in range(2, KD):
                        load_block(sp, a["w_merge"], m, n0 + m, m % 2, KD)
                    load_stream(sp, a["w_out"], KD, nb, KD)
                    load_first(sp, a["w_gu2"], nb + KD, KD)

                @block.gpsimd
                def _(pool):
                    for m in range(KD):
                        if m >= 2:
                            pool.wait_ge(m_dve, 3 * (m - 2) + 2)
                        for n in range(2):
                            pool.dma_start(gt[:, m % 2, n, :], a["spill"][4 + 8 * n + m, :, :]).then_inc(g_in[m % 2], 16)

                @block.scalar
                def _(act):
                    split_high(act, n0, 0, KD)
                    split_high(act, n0 + 1, 1, KD)
                    for m in range(KD):
                        split_high(act, n0 + 2 + m, m % 2, KD)
                        act.wait_ge(m_dve, 3 * m + 3)
                        act.activation(mg_high[:, m, :], mf[:, m % 2, 0, :], ACT.Copy).then_inc(m_high, 1)
                    for m in range(KD):
                        if m < KD - 2:
                            split_high(act, nb + 2 + m, m % 2, KD)
                        act.wait_ge(block_used, nb + m + 1)
                        square(act, pair(m % 2), m, norm_n)
                        act.activation(halves(y[:, m, :]), pair(m % 2), ACT.Copy).then_inc(y_out, 1)
                    factor_act(act, norm_n)
                    next_norm_act(act, norm_n + 1, r0, nb + KD)

                @block.vector
                def _(dve):
                    split_low(dve, n0, 0, KD)
                    split_low(dve, n0 + 1, 1, KD)
                    for m in range(KD):
                        split_low(dve, n0 + 2 + m, m % 2, KD)
                        dve.wait_ge(g_in[m % 2], 32 * (m // 2 + 1))
                        dve.wait_ge(fox_used, m + 1)
                        if m >= 2:
                            dve.wait_ge(m_low, m - 1)
                        dve.tensor_tensor(halves(mf[:, m % 2, 0, :]), halves(gt[:, m % 2, 0, :]), pair(2 * (m % 2)),
                                          ALU.mult).then_inc(m_dve, 1)
                        dve.wait_ge(block_used, n0 + m + 1)
                        dve.tensor_tensor(halves(mf[:, m % 2, 1, :]), halves(gt[:, m % 2, 1, :]), pair(2 * (m % 2) + 1),
                                          ALU.mult).then_inc(m_dve, 1)
                        dve.wait_ge(m_dve, 3 * m + 2)
                        dve.tensor_tensor(mf[:, m % 2, 0, :], mf[:, m % 2, 0, :], mf[:, m % 2, 1, :],
                                          ALU.add).then_inc(m_dve, 1)
                        dve.wait_ge(m_high, m + 1)
                        dve.tensor_tensor(mg_low[:, m, :], mf[:, m % 2, 0, :], mg_high[:, m, :].bitcast(F32),
                                          ALU.subtract).then_inc(m_low, 1)
                    for m in range(KD - 2):
                        split_low(dve, nb + 2 + m, m % 2, KD)
                    dve.wait_ge(y_out, KD)
                    residual_dve(dve, y, V_POSTM, 1.0, norm_n, r0)
                    split_low(dve, nb + KD, 0, KD)
                    split_low(dve, nb + KD + 1, 1, KD)

                @block.tensor
                def _(pe):
                    for m in range(KD):
                        if m >= 2:
                            pe.wait_ge(m_dve, 3 * (m - 2) + 2)
                        b = 2 * (m % 2)
                        block_products(pe, n0 + m, m % 2, range(0, 4), b, *fox_o, 0, True, True, fox_used)
                        block_products(pe, n0 + m, m % 2, range(4, 8), b + 1, *gdn_o, 0, True, True)
                    pe.wait_ge(m_dve, 3 * (KD - 2) + 2)
                    for m in range(KD):
                        if m >= 2:
                            pe.wait_ge(y_out, m - 1)
                        block_products(pe, nb + m, m % 2, range(KD), m % 2, mg_high, mg_low, 0, True, True,
                                       by_chunk=(m_low, 0) if m == 0 else None)
                        if m:
                            square_sum(pe, m - 1, norm_n, (m - 1) % 2, start=(m == 1))
                    square_sum(pe, KD - 1, norm_n, 1, stop=True)
                    norm_pe(pe, norm_n + 1)
            count["block"] = nb + KD
            norms[0] += 1

        ffn(0, a["w_gu1"], a["w_dn1"], V_PRE1, V_POST1, False)
        mixer()
        ffn(1, a["w_gu2"], a["w_dn2"], V_PRE2, V_POST2, True)


_INS = ["x_prompt", "x_sample", "cache_k", "cache_v", "cache_logf", "state_gdn", "state_conv", "page_table",
        "ffn1_norm_pre", "ffn1_w_gate", "ffn1_w_up", "ffn1_w_down", "ffn1_norm_post", "mix_norm_pre", "w_in",
        "fox_forget_bias", "gdn_conv_w", "gdn_dt_bias", "gdn_a_log", "gdn_out_norm", "w_branch_fox",
        "w_branch_gdn", "w_out", "mix_norm_post", "ffn2_norm_pre", "ffn2_w_gate", "ffn2_w_up", "ffn2_w_down",
        "ffn2_norm_post"]


def blocks_of(w, nk):
    k, m = w.shape
    w = w.reshape(k // (P * nk), nk, P, m // P, P).transpose(3, 0, 2, 1, 4)
    return np.ascontiguousarray(w.reshape(-1, P, nk * P))


def alternate(*ws):
    return np.ascontiguousarray(np.stack(ws, 1).reshape(-1, *ws[0].shape[1:]))


def chunks(v):
    return np.asarray(v).reshape(-1, P).T


def layout(i):
    f = np.float32
    out = {}
    xs = np.concatenate([i["x_prompt"][0], i["x_sample"][:, 0]], 0)
    out["x"] = xs.T.reshape(KD, P, T).transpose(1, 0, 2)
    for n in (1, 2):
        out[f"w_gu{n}"] = alternate(blocks_of(i[f"ffn{n}_w_gate"][0], KD), blocks_of(i[f"ffn{n}_w_up"][0], KD))
        out[f"w_dn{n}"] = blocks_of(i[f"ffn{n}_w_down"][0], NKD)
    w = i["w_in"][0]
    at = np.cumsum([512, 512, 512, 8, 1536, 4, 4, 512, 1024, 1024])
    qkv, fa, cv, al, be, z, ga, gb = (w[:, 0:at[2]], w[:, at[2]:at[3]], w[:, at[3]:at[4]], w[:, at[4]:at[5]],
                                      w[:, at[5]:at[6]], w[:, at[6]:at[7]], w[:, at[7]:at[8]], w[:, at[8]:at[9]])
    out["w_proj"] = blocks_of(np.concatenate([qkv, cv, z, ga, gb], 1), KD)
    small = np.zeros((D, 96), f)
    small[:, 0:8], small[:, 32:36], small[:, 64:68] = fa, al, be
    out["w_small"] = small.reshape(KD, P, 96).transpose(1, 0, 2)
    branch = np.concatenate([i["w_branch_fox"][0], i["w_branch_gdn"][0]], 0)
    out["w_merge"] = blocks_of(branch, KD)
    out["w_out"] = blocks_of(i["w_out"][0], KD)
    v = np.zeros((P, NVEC), f)
    for c, name in ((V_PRE1, "ffn1_norm_pre"), (V_POST1, "ffn1_norm_post"), (V_PREM, "mix_norm_pre"),
                    (V_POSTM, "mix_norm_post"), (V_PRE2, "ffn2_norm_pre"), (V_POST2, "ffn2_norm_post")):
        v[:, c:c + KD] = chunks(i[name][0])
    v[:, V_GDN] = i["gdn_out_norm"][0]
    v[:, V_CONV:V_CONV + 48] = i["gdn_conv_w"][0].reshape(4, 12, P).transpose(2, 1, 0).reshape(P, 48)
    v[0:8, V_BIAS] = i["fox_forget_bias"][0]
    v[32:36, V_BIAS] = i["gdn_dt_bias"][0]
    v[32:36, V_ALOG] = i["gdn_a_log"][0]
    v[:, V_SIGN] = 1.0
    v[0:8, V_SIGN] = -1.0
    out["vecs"] = v
    out["cache_k"] = i["cache_k"][0][:, ::-1].reshape(PHYS, P, 4, P).transpose(0, 3, 2, 1).reshape(PHYS, P, 512)
    out["cache_v"] = i["cache_v"][0][:, ::-1].reshape(PHYS, P, 512)
    out["cache_logf"] = i["cache_logf"][0][:, ::-1].transpose(0, 2, 1).reshape(PHYS * HEADS, P)
    out["page_table"] = i["page_table"][:, ::-1]
    out["page_order"] = out["page_table"].reshape(2, 4, PAGES).transpose(0, 2, 1).reshape(1, NS * PAGES)
    out["conv_in"] = i["state_conv"][0].transpose(2, 1, 0).reshape(12, P, 3, NS).transpose(1, 0, 2, 3)
    out["state_in"] = i["state_gdn"][0].transpose(2, 1, 0, 3).reshape(P, GH * NS, P)
    out["ident"] = np.eye(P, dtype=f)
    out["ones"] = np.ones((P, P), f)
    r, c = np.arange(P)[:, None], np.arange(P)[None, :]
    sel = np.zeros((P, 8, P), f)
    for h in range(8):
        sel[h, h] = -DH ** 0.5
    for h in range(4):
        sel[32 + h, h] = sel[64 + h, h] = 1.0
    out["sel"] = sel.reshape(P, 1024)
    out["causal"] = np.where(c <= r, 0.0, NEG).astype(f)
    out["chunk_mask"] = np.where((r <= c) & (r // C == c // C), 0.0, NEG).astype(f)
    lev = [((r // (2 * s) == c // (2 * s)) & (r // s % 2 == 0) & (c // s % 2 == 1)).astype(f)
           for s in (1 << n for n in range(LEVELS))]
    out["levels"] = np.stack(lev, 1).reshape(P, LEVELS * P)
    out["chunk_start"] = np.where(np.arange(P)[:, None] < 32, 1.0, np.arange(SEQ) % C != 0).astype(f)
    out["head_mask"] = ((np.arange(P)[:, None] % 32) == (np.arange(512)[None, :] // DH)).astype(f)
    out["group_sel"] = (np.arange(P)[:, None] // 32 == np.arange(4)[None, :]).astype(f)
    out["head_row"] = (np.arange(P)[:, None] % 8).astype(np.int32)
    return {k: np.ascontiguousarray(v) for k, v in out.items()}


_OUTS = [("o_y", (P, KD, T)), ("o_proj", (P, 20, T)), ("o_logf", (HEADS, T)),
         ("o_state", (P, GH, P)), ("o_state_s", (P, GH * NS, P)), ("o_conv_s", (P, 12, 3, NS))]


def kernel(**inputs):
    import concourse.bacc as _bacc
    from concourse.bass_utils import run_bass_kernel_spmd as _run

    arrays = layout({k: np.asarray(v) for k, v in inputs.items()})
    nc = _bacc.Bacc("TRN2", target_bir_lowering=False, num_devices=1)
    aps = {n: nc.dram_tensor("in_" + n, v.shape, mybir.dt.from_np(v.dtype), kind="ExternalInput").ap() for n, v in arrays.items()}
    for n, shape in _OUTS:
        aps[n] = nc.dram_tensor(n, shape, F32, kind="ExternalOutput").ap()
    aps["spill"] = nc.dram_tensor("spill", (20, P, T), F32, kind="Internal").ap()
    program(nc, aps)
    r = _run(nc, [{"in_" + n: v for n, v in arrays.items()}], core_ids=[0]).results[0]
    y = np.ascontiguousarray(r["o_y"].transpose(2, 1, 0).reshape(T, D))
    pr = r["o_proj"].transpose(2, 1, 0).reshape(T, 20 * P)
    k, v, u = pr[:, 0:512], pr[:, 512:1024], pr[:, 1024:]
    lf = r["o_logf"].T
    conv_s = r["o_conv_s"].transpose(3, 2, 1, 0).reshape(NS, 3, 12 * P)
    c = np.ascontiguousarray
    return (c(y[None, :SEQ]), c(y[SEQ:, None]),
            c(k[:SEQ].reshape(1, 1, SEQ, HEADS, DH)), c(v[:SEQ].reshape(1, 1, SEQ, HEADS, DH)), c(lf[:SEQ][None, None]),
            c(r["o_state"].transpose(1, 0, 2)[None, None]), c(u[SEQ - 3:SEQ][None, None]),
            c(k[SEQ:].reshape(1, NS, 1, HEADS, DH)), c(v[SEQ:].reshape(1, NS, 1, HEADS, DH)), c(lf[SEQ:][None, :, None]),
            c(r["o_state_s"].reshape(P, GH, NS, P).transpose(2, 1, 0, 3)[None]), c(conv_s[None]))
```
